# Optimizing a Trainium2 kernel written in Bass

```python
import math
import jax
import jax.numpy as jnp
from jax import lax
import numpy as np

D_MODEL = 1024
BATCH = 1
SEQ = 512
DEPTH = 1

MIX_WIDTH = D_MODEL // 2
DN_HEADS = 4
DN_DIM = MIX_WIDTH // DN_HEADS
DN_CONV = 5
CHUNK = 64
POOL_WINDOWS = (2, 4, 8, 16)
POOL_GROUPS = 4
POOL_DIM = MIX_WIDTH // POOL_GROUPS
ML_HEADS = 4
ML_V_DIM = MIX_WIDTH // ML_HEADS
ML_QK_DIM = ML_V_DIM // 2
N_BRANCH = 3
N_EXPERTS = 32
N_GROUPS = 8
EXPERTS_PER_GROUP = N_EXPERTS // N_GROUPS
TOP_K = 2
D_EXPERT = D_MODEL // 2
MOE_BLOCK = 128
LN_EPS = 1e-5
NORM_EPS = 1e-6

SPLITS = (3 * MIX_WIDTH,
          MIX_WIDTH,
          2 * DN_HEADS,
          2 * DN_HEADS,
          MIX_WIDTH,
          ML_HEADS * ML_QK_DIM,
          ML_HEADS * ML_QK_DIM,
          MIX_WIDTH,
          MIX_WIDTH,
          2 * ML_HEADS,
          2 * ML_HEADS,
          N_BRANCH * D_MODEL)
D_IN_PROJ = sum(SPLITS)

kernel_name = 'hybrid_gdn_pool_mlstm_grouped_moe_encoder'

def layer_norm(x, g, b):
    xf = x.astype(jnp.float32)
    mu = jnp.mean(xf, -1, keepdims=True)
    var = jnp.mean(jnp.square(xf - mu), -1, keepdims=True)
    return ((xf - mu) * lax.rsqrt(var + LN_EPS) * g.astype(jnp.float32) + b.astype(jnp.float32)).astype(x.dtype)

def head_rms_norm(h, w):
    h = h * lax.rsqrt(jnp.mean(h * h, -1, keepdims=True) + NORM_EPS)
    return h.reshape(h.shape[0], h.shape[1], -1) * w

def head_layer_norm(h, w):
    h = h - jnp.mean(h, -1, keepdims=True)
    h = h * lax.rsqrt(jnp.mean(h * h, -1, keepdims=True) + NORM_EPS)
    return h.reshape(h.shape[0], h.shape[1], -1) * w

def l2norm(x):
    return x * lax.rsqrt(jnp.sum(x * x, -1, keepdims=True) + NORM_EPS)

def centred_depthwise_conv(x, w):
    width, ch = w.shape
    pad = width // 2
    return lax.conv_general_dilated(x, w[:, None, :], window_strides=(1,), padding=[(pad, pad)],
                                    dimension_numbers=('NWC', 'WIO', 'NWC'), feature_group_count=ch)

def tri_masks(n):
    ones = jnp.ones((n, n), dtype=bool)
    return jnp.tril(ones), jnp.tril(ones, -1)

def gated_delta_rule(q, k, v, beta, g):
    nb, nh, ns, dk = q.shape
    dv = v.shape[-1]
    nc = ns // CHUNK
    q, k, v = (t.reshape(nb, nh, nc, CHUNK, -1) for t in (q, k, v))
    beta, g = (t.reshape(nb, nh, nc, CHUNK) for t in (beta, g))
    incl, strict = tri_masks(CHUNK)
    gc = jnp.cumsum(g, axis=-1)
    decay = jnp.exp(jnp.where(incl, gc[..., :, None] - gc[..., None, :], -jnp.inf))
    kb = k * beta[..., None]
    m = jnp.where(strict, jnp.einsum('bhnid,bhnjd->bhnij', kb, k) * decay, 0.0)
    a_mat = m + jnp.eye(CHUNK, dtype=m.dtype)
    rhs = jnp.concatenate([v * beta[..., None], kb * jnp.exp(gc)[..., None]], axis=-1)
    sol = lax.linalg.triangular_solve(a_mat, rhs, left_side=True, lower=True, unit_diagonal=True)
    u, w = sol[..., :dv], sol[..., dv:]
    g_last = gc[..., -1]
    k_dec = k * jnp.exp(g_last[..., None] - gc)[..., None]

    def step(state, inp):
        w_n, u_n, kd_n, gl_n = inp
        v_new = u_n - jnp.einsum('bhlk,bhkv->bhlv', w_n, state)
        state_next = state * jnp.exp(gl_n)[..., None, None] + jnp.einsum('bhlk,bhlv->bhkv', kd_n, v_new)
        return state_next, (state, v_new)

    xs = tuple(jnp.moveaxis(t, 2, 0) for t in (w, u, k_dec, g_last))
    s0 = jnp.zeros((nb, nh, dk, dv), jnp.float32)
    _, (states, v_new) = lax.scan(step, s0, xs)
    states = jnp.moveaxis(states, 0, 2)
    v_new = jnp.moveaxis(v_new, 0, 2)
    attn = jnp.einsum('bhnid,bhnjd->bhnij', q, k) * decay
    o = (jnp.einsum('bhnld,bhndv->bhnlv', q * jnp.exp(gc)[..., None], states)
         + jnp.einsum('bhnij,bhnjv->bhniv', attn, v_new))
    return o.reshape(nb, nh, ns, dv)

def mlstm_chunkwise(q, k, v, i_pre, f_pre):
    nb, nh, ns, dqk = q.shape
    dv = v.shape[-1]
    nc = ns // CHUNK
    q, k, v = (t.reshape(nb, nh, nc, CHUNK, -1) for t in (q, k, v))
    i_pre, f_pre = (t.reshape(nb, nh, nc, CHUNK) for t in (i_pre, f_pre))
    incl, _ = tri_masks(CHUNK)
    bc = jnp.cumsum(jax.nn.log_sigmoid(f_pre), axis=-1)
    b_last = bc[..., -1]
    d_log = jnp.where(incl, bc[..., :, None] - bc[..., None, :] + i_pre[..., None, :], -jnp.inf)
    lw = b_last[..., None] - bc + i_pre
    a_max = jnp.max(lw, -1)
    wgt = jnp.exp(lw - a_max[..., None])
    c_chunk = jnp.einsum('bhnl,bhnld,bhnle->bhnde', wgt, k, v)
    n_chunk = jnp.einsum('bhnl,bhnld->bhnd', wgt, k)

    def step(carry, inp):
        c, nv, m = carry
        cc, ncv, am, bl = inp
        m_new = jnp.maximum(bl + m, am)
        sp = jnp.exp(bl + m - m_new)
        sc = jnp.exp(am - m_new)
        c_new = c * sp[..., None, None] + cc * sc[..., None, None]
        n_new = nv * sp[..., None] + ncv * sc[..., None]
        return (c_new, n_new, m_new), (c, nv, m)

    init = (jnp.zeros((nb, nh, dqk, dv), jnp.float32), jnp.zeros((nb, nh, dqk), jnp.float32),
            jnp.zeros((nb, nh), jnp.float32))
    xs = tuple(jnp.moveaxis(t, 2, 0) for t in (c_chunk, n_chunk, a_max, b_last))
    _, (c_prev, n_prev, m_prev) = lax.scan(step, init, xs)
    c_prev, n_prev, m_prev = (jnp.moveaxis(t, 0, 2) for t in (c_prev, n_prev, m_prev))
    inter_log = bc + m_prev[..., None]
    m_out = jnp.maximum(inter_log, jnp.max(d_log, -1))
    s = jnp.einsum('bhnid,bhnjd->bhnij', q, k) * jnp.exp(d_log - m_out[..., None])
    inter = jnp.exp(inter_log - m_out)
    num = (inter[..., None] * jnp.einsum('bhnld,bhnde->bhnle', q, c_prev)
           + jnp.einsum('bhnij,bhnje->bhnie', s, v))
    den = inter * jnp.einsum('bhnld,bhnd->bhnl', q, n_prev) + jnp.sum(s, -1)
    h = num / jnp.maximum(jnp.abs(den), jnp.exp(-m_out))[..., None]
    return h.reshape(nb, nh, ns, dv)

def bidirectional(fn, shared, fwd_gates, bwd_gates):
    flip = lambda t: jnp.flip(t, axis=2)
    y_f = fn(*shared, *fwd_gates)
    y_b = fn(*[flip(t) for t in shared], *[flip(t) for t in bwd_gates])
    return y_f + flip(y_b)

def multiscale_pool(u, w_group, scale):
    nb, ns, _ = u.shape
    cs = jnp.concatenate([jnp.zeros((nb, 1, MIX_WIDTH), u.dtype), jnp.cumsum(u, axis=1)], axis=1)
    pos = jnp.arange(ns)
    outs = []
    for gi, win in enumerate(POOL_WINDOWS):
        lo = jnp.clip(pos - win // 2, 0, ns)
        hi = jnp.clip(pos + win // 2, 0, ns)
        cg = cs[:, :, gi * POOL_DIM:(gi + 1) * POOL_DIM]
        mean = (cg[:, hi] - cg[:, lo]) / (hi - lo).astype(u.dtype)[None, :, None]
        outs.append(mean - u[:, :, gi * POOL_DIM:(gi + 1) * POOL_DIM])
    p = jnp.stack(outs, axis=2)
    y = jnp.einsum('bsgc,gcd->bsgd', p, w_group).reshape(nb, ns, MIX_WIDTH)
    return y * scale

def hybrid_mixer(h, w_in, dn_conv_w, dn_a_log, dn_dt_bias, dn_norm_w, pool_w, pool_scale,
                 ml_gate_b, ml_norm_w, w_branch, w_out):
    nb, ns, _ = h.shape
    f32 = jnp.float32
    idx = [int(c) for c in np.cumsum(SPLITS)[:-1]]
    proj = h @ w_in
    (dn_qkv, dn_z, dn_a, dn_b, pool_u, ml_q, ml_k, ml_v, ml_o, ml_i, ml_f,
     gate_pre) = jnp.split(proj, idx, axis=-1)
    heads = lambda t, nh: t.astype(f32).reshape(nb, ns, nh, -1).transpose(0, 2, 1, 3)
    dir_gates = lambda t: t.astype(f32).reshape(nb, ns, 2, -1).transpose(2, 0, 3, 1)

    qkv = jax.nn.silu(centred_depthwise_conv(dn_qkv.astype(f32), dn_conv_w.astype(f32)))
    dq, dk, dv = jnp.split(qkv, 3, axis=-1)
    dq = l2norm(heads(dq, DN_HEADS)) * DN_DIM ** -0.5
    dk = l2norm(heads(dk, DN_HEADS))
    dv = heads(dv, DN_HEADS)
    beta = jax.nn.sigmoid(dir_gates(dn_b))
    a_log = dn_a_log.astype(f32).reshape(2, 1, DN_HEADS, 1)
    dt_bias = dn_dt_bias.astype(f32).reshape(2, 1, DN_HEADS, 1)
    g = -jnp.exp(a_log) * jax.nn.softplus(dir_gates(dn_a) + dt_bias)
    o_dn = bidirectional(gated_delta_rule, (dq, dk, dv), (beta[0], g[0]), (beta[1], g[1]))
    y_dn = head_rms_norm(o_dn.transpose(0, 2, 1, 3), dn_norm_w.astype(f32)) * jax.nn.silu(dn_z.astype(f32))

    y_pool = multiscale_pool(pool_u.astype(f32), pool_w.astype(f32), pool_scale.astype(f32))

    mq = heads(ml_q, ML_HEADS)
    mk = heads(ml_k, ML_HEADS) * ML_QK_DIM ** -0.5
    mv = heads(ml_v, ML_HEADS)
    gb = ml_gate_b.astype(f32).reshape(2, 2, 1, ML_HEADS, 1)
    ig = dir_gates(ml_i) + gb[0]
    fg = dir_gates(ml_f) + gb[1]
    h_ml = bidirectional(mlstm_chunkwise, (mq, mk, mv), (ig[0], fg[0]), (ig[1], fg[1]))
    y_ml = head_layer_norm(h_ml.transpose(0, 2, 1, 3), ml_norm_w.astype(f32)) * jax.nn.sigmoid(ml_o.astype(f32))

    branches = jnp.stack([y_dn, y_pool, y_ml], axis=2).astype(h.dtype)
    y = jnp.einsum('bsrm,rmd->bsrd', branches, w_branch)
    gate = jax.nn.sigmoid(gate_pre.reshape(nb, ns, N_BRANCH, D_MODEL))
    merged = jnp.sum(gate * y, axis=2)
    return merged @ w_out

def route(h2, router_w, router_b):
    t = h2.shape[0]
    scores = jax.nn.sigmoid(h2.astype(jnp.float32) @ router_w.astype(jnp.float32))
    sel = (scores + router_b.astype(jnp.float32)).reshape(t, N_GROUPS, EXPERTS_PER_GROUP)
    group_score = jnp.sum(lax.top_k(sel, TOP_K)[0], axis=-1)
    grp = jnp.argmax(group_score, axis=-1)
    sel_in = sel[jnp.arange(t), grp]
    _, local = lax.top_k(sel_in, TOP_K)
    expert = grp[:, None] * EXPERTS_PER_GROUP + local
    w = jnp.take_along_axis(scores, expert, axis=1)
    return expert, w / jnp.sum(w, axis=-1, keepdims=True)

def moe_ffn(h, router_w, router_b, w1, w3, w2):
    nb, ns, d = h.shape
    t = nb * ns
    h2 = h.reshape(t, d)
    expert, gate = route(h2, router_w, router_b)
    a = t * TOP_K
    flat_e = expert.reshape(a)
    flat_tok = jnp.repeat(jnp.arange(t, dtype=jnp.int32), TOP_K)
    flat_w = gate.reshape(a)
    order = jnp.argsort(flat_e)
    e_sorted = flat_e[order]
    counts = jnp.bincount(flat_e, length=N_EXPERTS)
    padded = ((counts + MOE_BLOCK - 1) // MOE_BLOCK) * MOE_BLOCK
    start = jnp.cumsum(counts) - counts
    pend = jnp.cumsum(padded)
    pstart = pend - padded
    dest = pstart[e_sorted] + jnp.arange(a) - start[e_sorted]
    n_rows = a + N_EXPERTS * MOE_BLOCK
    n_blocks = n_rows // MOE_BLOCK
    row_tok = jnp.full((n_rows,), t, dtype=jnp.int32).at[dest].set(flat_tok[order])
    row_w = jnp.zeros((n_rows,), jnp.float32).at[dest].set(flat_w[order])
    block_expert = jnp.clip(jnp.searchsorted(pend, jnp.arange(n_blocks) * MOE_BLOCK, side='right'),
                            0, N_EXPERTS - 1)
    hp = jnp.concatenate([h2, jnp.zeros((1, d), h2.dtype)], axis=0)
    xb = hp[row_tok].reshape(n_blocks, MOE_BLOCK, d)

    def expert_block(args):
        xblk, e = args
        act = jax.nn.silu(xblk @ w1[e]) * (xblk @ w3[e])
        return act @ w2[e]

    yb = lax.map(expert_block, (xb, block_expert))
    y = yb.reshape(n_rows, d).astype(jnp.float32) * row_w[:, None]
    out = jnp.zeros((t + 1, d), jnp.float32).at[row_tok].add(y)[:t]
    return out.reshape(nb, ns, d).astype(h.dtype)

def setup_inputs(seed: int = 0) -> dict:
    key = jax.random.key(seed)
    ks = jax.random.split(key, 24)
    f32 = jnp.float32
    nrm = lambda i, shape, scale: jax.random.normal(ks[i], shape, f32) * scale
    out_scale = (8.0 * DEPTH) ** -0.25
    dt = jnp.exp(jax.random.uniform(ks[4], (DEPTH, 2 * DN_HEADS), f32, math.log(1e-3), math.log(1e-1)))
    dn_dt_bias = dt + jnp.log(-jnp.expm1(-dt))
    dn_a_log = jnp.log(jax.random.uniform(ks[5], (DEPTH, 2 * DN_HEADS), f32, 1.0, 16.0))
    f_bias = jnp.tile(jnp.linspace(3.0, 6.0, ML_HEADS, dtype=f32), (DEPTH, 2)) + nrm(6, (DEPTH, 2 * ML_HEADS), 0.1)
    i_bias = nrm(7, (DEPTH, 2 * ML_HEADS), 0.1)
    return {
        'x': nrm(0, (BATCH, SEQ, D_MODEL), 1.0),
        'ln_in_g': 1.0 + nrm(1, (D_MODEL,), 0.02),
        'ln_in_b': nrm(2, (D_MODEL,), 0.02),
        'w_in': nrm(3, (DEPTH, D_MODEL, D_IN_PROJ), D_MODEL ** -0.5),
        'dn_conv_w': nrm(8, (DEPTH, DN_CONV, 3 * MIX_WIDTH), DN_CONV ** -0.5),
        'dn_a_log': dn_a_log,
        'dn_dt_bias': dn_dt_bias,
        'dn_norm_w': 1.0 + nrm(9, (DEPTH, MIX_WIDTH), 0.02),
        'pool_w': nrm(10, (DEPTH, POOL_GROUPS, POOL_DIM, POOL_DIM), POOL_DIM ** -0.5),
        'pool_scale': 1.0 + nrm(11, (DEPTH, MIX_WIDTH), 0.02),
        'ml_gate_b': jnp.concatenate([i_bias, f_bias], axis=-1),
        'ml_norm_w': 1.0 + nrm(12, (DEPTH, MIX_WIDTH), 0.02),
        'w_branch': nrm(13, (DEPTH, N_BRANCH, MIX_WIDTH, D_MODEL), MIX_WIDTH ** -0.5),
        'w_out': nrm(14, (DEPTH, D_MODEL, D_MODEL), out_scale * D_MODEL ** -0.5),
        'ln_mix_g': 1.0 + nrm(15, (DEPTH, D_MODEL), 0.02),
        'ln_mix_b': nrm(16, (DEPTH, D_MODEL), 0.02),
        'router_w': nrm(17, (D_MODEL, N_EXPERTS), D_MODEL ** -0.5),
        'router_b': nrm(18, (N_EXPERTS,), 0.01),
        'moe_w1': nrm(19, (DEPTH, N_EXPERTS, D_MODEL, D_EXPERT), D_MODEL ** -0.5),
        'moe_w3': nrm(20, (DEPTH, N_EXPERTS, D_MODEL, D_EXPERT), D_MODEL ** -0.5),
        'moe_w2': nrm(21, (DEPTH, N_EXPERTS, D_EXPERT, D_MODEL), out_scale * D_EXPERT ** -0.5),
        'ln_ffn_g': 1.0 + nrm(22, (DEPTH, D_MODEL), 0.02),
        'ln_ffn_b': nrm(23, (DEPTH, D_MODEL), 0.02),
    }

def reference(x, ln_in_g, ln_in_b, w_in, dn_conv_w, dn_a_log, dn_dt_bias, dn_norm_w, pool_w, pool_scale,
              ml_gate_b, ml_norm_w, w_branch, w_out, ln_mix_g, ln_mix_b, router_w, router_b,
              moe_w1, moe_w3, moe_w2, ln_ffn_g, ln_ffn_b):
    alpha = (2.0 * DEPTH) ** 0.25
    h = layer_norm(x, ln_in_g, ln_in_b)
    for l in range(DEPTH):
        mix = hybrid_mixer(h, w_in[l], dn_conv_w[l], dn_a_log[l], dn_dt_bias[l], dn_norm_w[l],
                           pool_w[l], pool_scale[l], ml_gate_b[l], ml_norm_w[l], w_branch[l], w_out[l])
        h = layer_norm(alpha * h + mix, ln_mix_g[l], ln_mix_b[l])
        ffn = moe_ffn(h, router_w, router_b, moe_w1[l], moe_w3[l], moe_w2[l])
        h = layer_norm(alpha * h + ffn, ln_ffn_g[l], ln_ffn_b[l])
    return h


_drawn_inputs = setup_inputs


def setup_inputs(seed=0):
    import zlib

    import numpy as np

    out = dict(_drawn_inputs(seed))
    spreads = {}
    factors = {'dn_norm_w': 10.508,
     'pool_scale': 3.681,
     'ml_norm_w': 15.839,
     'ln_ffn_g': 8.012,
     'ln_ffn_b': 8.225}
    for name, (base, spread) in spreads.items():
        noise = np.random.default_rng([zlib.crc32(name.encode()), seed]).standard_normal(out[name].shape)
        drawn = base * np.exp(spread * noise) if base else spread * noise
        out[name] = jnp.asarray(drawn.astype(out[name].dtype))
    for name, factor in factors.items():
        out[name] = (out[name] * factor).astype(out[name].dtype)
    return out
```

```python
import concourse.bass as bass
from concourse import mybir
from concourse.alu_op_type import AluOpType as ALU
from contextlib import ExitStack
import numpy as np

F32 = mybir.dt.float32
F32R = mybir.dt.float32r
I32 = mybir.dt.int32
ACT = mybir.ActivationFunctionType
AX = mybir.AxisListType

P = 128
SEQ, DM = 512, 1024
NT = SEQ // P
KT = DM // P
MW = DM // 2
NH = 4
DV = MW // NH
QK = DV // 2
TAPS = 5
LN_EPS, NORM_EPS = 1e-5, 1e-6
ALPHA = 2.0 ** 0.25
NE, NG = 32, 8
EPG = NE // NG
FE = DM // 2
SLOTS = 64
OVER = (2 * SEQ) // SLOTS
TABLE = SLOTS * (NE + OVER)
FAR = 1 << 20
NEG = -1.0e30

OFF = np.cumsum([0, 3 * MW, MW, 2 * NH, 2 * NH, MW, NH * QK, NH * QK, MW, MW, 2 * NH, 2 * NH, 3 * DM])
C_Q, C_K, C_V, C_Z, C_A, C_U, C_MQ, C_MV, C_MO, C_I, C_G = (
    0, MW, 2 * MW, int(OFF[1]), int(OFF[2]), int(OFF[4]), int(OFF[5]), int(OFF[7]), int(OFF[8]), int(OFF[9]), int(OFF[11]))
LEVELS = [1, 2, 4, 8, 16, 32, 64]
NL = len(LEVELS)


def constants():
    i = np.arange(P)[None, :]
    j = np.arange(P)[:, None]
    upto, after = (j <= i), (j >= i)
    cols = {"ident": np.eye(P), "ones": np.ones((P, P)), "upto": upto, "after": after,
            "neg_fwd": np.where(upto, 0.0, NEG), "neg_bwd": np.where(after, 0.0, NEG),
            "before": j < i}
    for d in range(2):
        for b in LEVELS:
            same = (i // (2 * b)) == (j // (2 * b))
            first_j, first_i = (j // b) % 2 == 0, (i // b) % 2 == 0
            cols[f"level{d}_{b}"] = same & (first_j & ~first_i if d == 0 else first_i & ~first_j)
    edge = np.zeros((P, 4, 16))
    for g, win in enumerate((2, 4, 8, 16)):
        half = win // 2
        for n in range(8):
            edge[:, g, n] = 1.0 / (min(n + half, SEQ) - max(n - half, 0))
            m = SEQ - 8 + n
            edge[:, g, 8 + n] = 1.0 / (min(m + half, SEQ) - max(m - half, 0))
    cols["edge"] = edge.reshape(P, 64)
    sel = np.zeros((P, NH, P))
    for h in range(NH):
        sel[h, h, :] = 1.0
    cols["sel"] = sel.reshape(P, NH * P)
    cols["pair"] = (i[:, 0:SLOTS] == j % SLOTS)
    cols["down"] = np.tile(np.arange(NG, 0, -1.0), (P, 1))
    cols["place"] = np.tile(np.arange(4.0), (P, 1))
    cols["expert"] = np.tile(np.arange(32.0), (P, 1))
    cols["token"] = np.arange(NT)[None, :] * P + j
    return {k: np.asarray(v, np.float32) for k, v in cols.items()}


CONST = constants()
COFF, NCONST = {}, 0
for _key, _table in CONST.items():
    COFF[_key] = (NCONST, _table.shape[1])
    NCONST += _table.shape[1]


class Chain:

    def __init__(self, eng, sem):
        self.eng, self.sem, self.n, self.base = eng, sem, 0, 0

    def add(self, ins):
        self.n += 1
        ins.then_inc(self.sem, 1)
        return ins

    def wait(self):
        self.eng.wait_ge(self.sem, self.base + self.n)

    def link(self, ins):
        self.add(ins)
        self.wait()


def bc(ap, dim, n):
    v = ap.unsqueeze(dim)
    shape = list(v.shape)
    shape[dim] = n
    return v.to_broadcast(shape)


SM_CONV, SM_NORM, SM_W, SM_BIAS, SM_RB, SM_RW = 0, 60, 72, 328, 360, 392
SM_COLS = 392 + KT * NE


def hybrid_encoder(nc, x, ln_in_g, ln_in_b, w_in, pool_w, w_branch, w_out, ln_mix_g, ln_mix_b,
                   moe_w1, moe_w3, moe_w2, ln_ffn_g, ln_ffn_b, const, small, out):
    root = ExitStack()
    stages = [[]]

    def sem(name):
        stages[-1].append(nc.alloc_semaphore(name))
        return stages[-1][-1]

    def zero_last(pool):
        if len(stages) > 1:
            numbers = sorted(s.num for s in stages[-2])
            while numbers:
                n = 1
                while n < len(numbers) and numbers[n] == numbers[0] + n:
                    n += 1
                pool.sem_clear(range(numbers[0], numbers[0] + n))
                numbers = numbers[n:]

    def next_stage():
        if len(stages) > 1:
            for s in stages[-2]:
                nc.release_semaphore(s)
        stages.append([])

    h2_dram = nc.dram_tensor("h2_dram", (SEQ, DM), F32, kind="Internal").ap()
    slots_dram = nc.dram_tensor("slots_dram", (TABLE, 4), I32, kind="Internal").ap()
    y_dram = nc.dram_tensor("y_dram", (4 * SEQ, DM), F32, kind="Internal").ap()
    with root:
        def sb(stack, name, shape, dt=F32):
            return stack.enter_context(nc.sbuf_tensor(name, shape, dt))

        def pb(stack, name, shape=(P, 512), dt=F32):
            return stack.enter_context(nc.psum_tensor(name, list(shape), dt))

        cst = sb(root, "cst", [P, NCONST])
        sml = sb(root, "sml", [P, SM_COLS])
        epsc = sb(root, "epsc", [P, 4])

        def cn(name, rows=P):
            a, n = COFF[name]
            return cst[0:rows, a:a + n]

        ident, ones = cn("ident"), cn("ones")
        h2 = sb(root, "h2", [P, NT, DM])
        rows_all = sb(root, "rows_all", [P, NE + OVER + 1, 4], I32)
        flag = sb(root, "flag", [1, 1 + OVER], I32)
        mixer = ExitStack()
        hT = sb(mixer, "hT", [P, KT, SEQ])
        yT = sb(mixer, "yT", [P, 3, NH, SEQ])
        attention = ExitStack()
        qkT = sb(attention, "qkT", [P, 2, NH, SEQ])
        kTok = sb(attention, "kTok", [P, NT, NH, DV])
        vTok = sb(attention, "vTok", [P, NT, NH, DV])
        beta = sb(attention, "beta", [P, NT, 8])
        cum = sb(attention, "cum", [P, NT, 24])
        gg = sb(attention, "gg", [P, NT, 24])
        mstack = ExitStack()
        mq = sb(mstack, "mq", [P, 4, SEQ])
        mvx = sb(mstack, "mvx", [P, NT, NH, DV + 1])
        mrow = sb(mstack, "mrow", [4, 2, SEQ])
        acol = sb(mstack, "acol", [P, NT, 8])
        emx = sb(mstack, "emx", [P, NT, 8])

        front(nc, sem, sb, pb, cn, locals())
        next_stage()
        mlstm(nc, sem, sb, pb, cn, locals())
        next_stage()
        mstack.close()
        deltanet(nc, sem, sb, pb, cn, locals())
        next_stage()
        attention.close()
        merge(nc, sem, sb, pb, cn, locals())
        next_stage()
        mixer.close()
        experts(nc, sem, sb, pb, cn, locals())
        next_stage()
        final(nc, sem, sb, pb, cn, locals())


def layer_norm_dve(dve, chain, src, stats, mv, rstd, nmr, x_ready, stats_ready, std_ready, scale_ready,
                   norm_ready, gmul_ready, g):
    for t in range(NT):
        x_ready(t)
        for half in range(2):
            chain.add(dve.bn_stats(stats[:, t, half, :], src[:, t, 512 * half:512 * half + 512]))
        chain.wait()
        dve.bn_aggr(mv[:, t, :], stats[:, t, :, :]).then_inc(stats_ready, 1)
    for t in range(NT):
        dve.wait_ge(std_ready, t + 1)
        chain.link(dve.reciprocal(rstd[:, t:t + 1], rstd[:, t:t + 1]))
        dve.wait_ge(stats_ready, t + 1)
        dve.tensor_scalar(nmr[:, t:t + 1], mv[:, t, 0:1], rstd[:, t:t + 1], -1.0, ALU.mult, ALU.mult).then_inc(scale_ready, 1)
    for t in range(NT):
        dve.wait_ge(norm_ready, t + 1)
        dve.tensor_tensor(src[:, t, :], src[:, t, :], g, ALU.mult).then_inc(gmul_ready, 1)


def layer_norm_act(act, src, mv, rstd, nmr, eps, stats_ready, std_ready, scale_ready, norm_ready):
    for t in range(NT):
        act.wait_ge(stats_ready, t + 1)
        act.activation(rstd[:, t:t + 1], mv[:, t, 1:2], ACT.Sqrt, bias=eps).then_inc(std_ready, 1)
    for t in range(NT):
        act.wait_ge(scale_ready, t + 1)
        act.activation(src[:, t, :], src[:, t, :], ACT.Identity, scale=rstd[:, t:t + 1],
                       bias=nmr[:, t:t + 1]).then_inc(norm_ready, 1)


def front(nc, sem, sb, pb, cn, v):
    x, w_in, small, const = v["x"], v["w_in"], v["small"], v["const"]
    cst, sml, epsc, hT, yT, qkT = (v[k] for k in ("cst", "sml", "epsc", "hT", "yT", "qkT"))
    kTok, vTok, beta, cum, gg, mq, mvx, mrow, acol, emx = (
        v[k] for k in ("kTok", "vTok", "beta", "cum", "gg", "mq", "mvx", "mrow", "acol", "emx"))
    ident, ones = v["ident"], v["ones"]
    st = ExitStack()
    with st:
        h = v["h2"]
        ring = sb(st, "ring", [P, 2, KT, 512])
        spare = sb(st, "spare", [P, NT, DM])
        lng, lnb = sb(st, "lng", [P, DM]), sb(st, "lnb", [P, DM])
        stats, mv, rstd, nmr = sb(st, "stats", [P, NT, 2, 6]), sb(st, "mv", [P, NT, 2]), sb(st, "rstd", [P, NT]), sb(st, "nmr", [P, NT])
        raw = sb(st, "raw", [P, 3, SEQ + 4])
        cv = sb(st, "cv", [P, 3, SEQ])
        sp = sb(st, "sp", [P, 3, NT, 16])
        ab = sb(st, "ab", [P, NT, 32])
        pw = sb(st, "pw", [P, NH, DV])
        up = sb(st, "up", [P, 528])
        win = sb(st, "win", [P, 2, 528])
        vT = spare[:, 0:2, :].rearrange("p a (b s) -> p (a b) s", b=2)
        sq = spare[:, 2, :].rearrange("p (a s) -> p a s", a=2)
        nrm = spare[:, 3, :].rearrange("p (a s) -> p a s", a=2)
        tp = [pb(st, f"tp{i}") for i in range(2)]
        pj = [pb(st, f"pj{i}") for i in range(3)]
        gps = pb(st, "gps")
        rps = [pb(st, f"rps{i}") for i in range(2)]

        const_in, small_in, x_in, ln_in = sem("const_in"), sem("small_in"), sem("x_in"), sem("ln_in")
        pw_in = sem("pw_in")
        chunk_in = [sem(f"chunk_in{i}") for i in range(2)]
        chunk_used, eps_set, pads_set = sem("chunk_used"), sem("eps_set"), sem("pads_set")
        stats_ready, std_ready, scale_ready, norm_ready, gmul_ready, h_ready = (
            sem(f"ln1_{n}") for n in ("stats", "std", "scale", "norm", "gmul", "h"))
        turned, turn_copied = sem("h_turned"), sem("h_turn_copied")
        small_proj, small_copied = sem("small_proj"), sem("small_copied")
        proj_done, proj_copied = sem("proj_done"), sem("proj_copied")
        conv_done, silu_done = sem("conv_done"), sem("silu_done")
        gate_abs = sem("gate_abs")
        gate_exp, gate_in, gate_ln, gates_done = sem("gate_exp"), sem("gate_in"), sem("gate_ln"), sem("gates_done")
        cum_done, cum_copied, a_done, a_turned, scan_done, m_turned = (
            sem(n) for n in ("cum_done", "cum_copied", "a_done", "a_turned", "scan_done", "m_turned"))
        em_arg, beta_done = sem("em_arg"), sem("beta_done")
        square_done, sum_done, root_done, qk_normed = sem("square_done"), sem("sum_done"), sem("root_done"), sem("qk_normed")
        tok_turned, tok_copied = sem("tok_turned"), sem("tok_copied")
        up_copied, pooled, pool_mixed, pool_done = sem("up_copied"), sem("pooled"), sem("pool_mixed"), sem("pool_done")
        dve_chain, pool_chain = sem("front_dve_chain"), sem("front_pool_chain")

        starts = [C_Q, C_K, C_V, C_MQ, C_MV, C_Z, C_U, C_MO]
        w_rows = w_in.rearrange("(p k) n -> p k n", k=KT)
        NQKV = 12
        with nc.Block() as block:
            @block.sync
            def _(sp_):
                for t in range(NT):
                    sp_.dma_start(h[:, t, :], x[t * P:(t + 1) * P, :]).then_inc(x_in, 16)
                sp_.dma_start(lng[:, :], v["ln_in_g"].to_broadcast([P, DM])).then_inc(ln_in, 16)
                sp_.dma_start(lnb[:, :], v["ln_in_b"].to_broadcast([P, DM])).then_inc(ln_in, 16)
                sp_.dma_start(cst[:, :], const).then_inc(const_in, 16)
                sp_.dma_start(sml[:, :], small).then_inc(small_in, 16)
                sp_.dma_start(pw[:, :, :], v["pool_w"].rearrange("g c d -> c g d")).then_inc(pw_in, 16)
                for c, at in enumerate(starts):
                    if c >= 2:
                        sp_.wait_ge(chunk_used, c - 1)
                    sp_.dma_start(ring[:, c % 2, :, :], w_rows[:, :, at:at + 512]).then_inc(chunk_in[c % 2], 16)

            @block.tensor
            def _(pe):
                pe.wait_ge(const_in, 16)
                for n in range(2 * NT):
                    t, half = n // 2, n % 2
                    pe.wait_ge(h_ready, t + 1)
                    if n >= 2:
                        pe.wait_ge(turn_copied, n - 1)
                    for k in range(4):
                        last = pe.transpose(tp[n % 2][:, k * P:(k + 1) * P], h[:, t, 4 * half + k::KT], ident)
                    last.then_inc(turned, 1)
                pe.wait_ge(small_in, 16)
                pe.wait_ge(turn_copied, 2 * NT)
                wsm = sml[:, SM_W:SM_W + KT * 32].rearrange("p (k n) -> p k n", k=KT)
                for t in range(NT):
                    for k in range(KT):
                        last = pe.matmul(gps[:, t * 32:(t + 1) * 32], hT[:, k, t * P:(t + 1) * P], wsm[:, k, :],
                                         start=(k == 0), stop=(k == KT - 1))
                last.then_inc(small_proj, 1)
                n = 0

                def chunk(c):
                    nonlocal n
                    pe.wait_ge(chunk_in[c % 2], 16 * (c // 2 + 1))
                    for m in range(4):
                        if n >= 3:
                            pe.wait_ge(proj_copied, n - 2)
                        for k in range(KT):
                            if starts[c] == C_MV:
                                a, b = hT[:, k, m * P:(m + 1) * P], ring[:, c % 2, k, :]
                            else:
                                a, b = ring[:, c % 2, k, m * P:(m + 1) * P], hT[:, k, :]
                            last = pe.matmul(pj[n % 3][:, :], a, b, start=(k == 0), stop=(k == KT - 1))
                        last.then_inc(proj_done, 1)
                        n += 1

                def chunk_and_free(c):
                    chunk(c)
                    if c + 2 < len(starts):
                        pe.wait_ge(proj_done, 4 * (c + 1))
                        pe.sem_inc(chunk_used, 1)

                for c in range(3):
                    chunk_and_free(c)
                pe.wait_ge(gates_done, 2)
                for t in range(NT):
                    o = 128 + 24 * t
                    for d, tri in enumerate((cn("upto"), cn("after"))):
                        m_ = cn("upto") if d == 0 else cn("after")
                        pe.matmul(gps[:, o + 4 * d:o + 4 * d + 4], m_, gg[:, t, 4 * d:4 * d + 4], start=True, stop=True)
                        other = range(t) if d == 0 else range(t + 1, NT)
                        pe.matmul(gps[:, o + 16 + 4 * d:o + 20 + 4 * d], m_, gg[:, t, 8 + 4 * d:12 + 4 * d],
                                  start=True, stop=(len(other) == 0))
                        for u in other:
                            pe.matmul(gps[:, o + 16 + 4 * d:o + 20 + 4 * d], ones, gg[:, u, 8 + 4 * d:12 + 4 * d],
                                      start=False, stop=(u == other[-1]))
                    last = pe.matmul(gps[:, o + 8:o + 16], ones, gg[:, t, 0:8], start=True, stop=True)
                last.then_inc(cum_done, 1)
                chunk_and_free(3)
                pe.wait_ge(a_done, 1)
                for d in range(2):
                    for t in range(NT):
                        last = pe.transpose(rps[d][0:4, t * P:(t + 1) * P], acol[:, t, 4 * d:4 * d + 4], ident)
                last.then_inc(a_turned, 1)
                chunk_and_free(4)
                pe.wait_ge(scan_done, 2)
                for d in range(2):
                    for t in range(NT):
                        last = pe.transpose(gps[:, 256 + 8 * t + 4 * d:260 + 8 * t + 4 * d], mrow[0:4, d, t * P:(t + 1) * P],
                                            ident[0:4, 0:4])
                last.then_inc(m_turned, 1)
                for c in range(5, 8):
                    chunk_and_free(c)
                pe.wait_ge(pw_in, 16)
                for g in range(4):
                    pe.wait_ge(pooled, g + 1)
                    pe.wait_ge(turn_copied, 2 * NT)
                    if g >= 2:
                        pe.wait_ge(pool_done, g - 1)
                    pe.matmul(tp[g % 2][:, :], pw[:, g, :], yT[:, 1, g, :], start=True, stop=True).then_inc(pool_mixed, 1)
                for m in range(8):
                    pe.wait_ge(square_done, m + 1)
                    if m == 0:
                        pe.wait_ge(proj_copied, 32)
                    if m >= 3:
                        pe.wait_ge(root_done, m - 2)
                    pe.matmul(pj[m % 3][:, :], ones, sq[:, m % 2, :], start=True, stop=True).then_inc(sum_done, 1)
                for m in range(8):
                    t = m % 4
                    if m == 0:
                        pe.wait_ge(qk_normed, 8)
                        pe.wait_ge(pool_done, 4)
                    if m >= 2:
                        pe.wait_ge(tok_copied, m - 1)
                    for hd in range(NH):
                        src = qkT[:, 1, hd, :] if m < 4 else vT[:, hd, :]
                        last = pe.transpose(tp[m % 2][:, hd * P:(hd + 1) * P], src[:, t * P:(t + 1) * P], ident)
                    last.then_inc(tok_turned, 1)

            @block.scalar
            def _(act):
                act.wait_ge(eps_set, 1)
                layer_norm_act(act, h, mv, rstd, nmr, epsc[:, 0:1], stats_ready, std_ready, scale_ready, norm_ready)
                for n in range(2 * NT):
                    t, half = n // 2, n % 2
                    act.wait_ge(turned, n + 1)
                    act.activation(hT[:, 4 * half:4 * half + 4, t * P:(t + 1) * P],
                                   tp[n % 2][:, :].rearrange("p (k s) -> p k s", k=4), ACT.Copy).then_inc(turn_copied, 1)
                act.wait_ge(small_proj, 1)
                act.activation(ab[:, :, :], gps[:, 0:128].rearrange("p (t n) -> p t n", t=NT), ACT.Copy).then_inc(small_copied, 1)
                act.wait_ge(small_copied, 1)
                act.activation(beta[:, :, :], ab[:, :, 8:16], ACT.Sigmoid).then_inc(beta_done, 1)
                act.wait_ge(gate_in, 1)
                act.activation(sp[:, 1, :, :], sp[:, 1, :, :], ACT.Abs).then_inc(gate_abs, 1)
                act.wait_ge(gate_abs, 1)
                act.activation(sp[:, 1, :, :], sp[:, 1, :, :], ACT.Exp, scale=-1.0).then_inc(gate_exp, 1)
                act.activation(sml[:, SM_BIAS:SM_BIAS + 8], sml[:, SM_BIAS:SM_BIAS + 8], ACT.Exp).then_inc(gate_exp, 1)
                act.wait_ge(gate_exp, 1)
                act.activation(sp[:, 1, :, :], sp[:, 1, :, :], ACT.Ln, bias=1.0).then_inc(gate_ln, 1)

                def copy_qkv(n):
                    act.wait_ge(proj_done, n + 1)
                    if n >= 3:
                        act.wait_ge(conv_done, n - 2)
                    act.activation(raw[:, n % 3, 2:2 + SEQ], pj[n % 3][:, :], ACT.Copy).then_inc(proj_copied, 1)

                def silu_qkv(n):
                    act.wait_ge(conv_done, n + 1)
                    dst = qkT[:, n // 4, n % 4, :] if n < 8 else vT[:, n % 4, :]
                    act.activation(dst, cv[:, n % 3, :], ACT.Silu).then_inc(silu_done, 1)

                act.wait_ge(pads_set, 1)
                for n in range(NQKV):
                    copy_qkv(n)
                    if n >= 1:
                        silu_qkv(n - 1)
                silu_qkv(NQKV - 1)
                for n in range(12, 16):
                    act.wait_ge(proj_done, n + 1)
                    act.activation(mq[:, n - 12, :], pj[n % 3][:, :], ACT.Copy,
                                   scale=(1.0 if n < 14 else QK ** -0.5)).then_inc(proj_copied, 1)
                for n in range(16, 20):
                    act.wait_ge(proj_done, n + 1)
                    act.activation(mvx[:, n - 16, :, 0:DV], pj[n % 3][:, :].rearrange("p (h e) -> p h e", h=NH),
                                   ACT.Copy).then_inc(proj_copied, 1)
                for n in range(20, 24):
                    act.wait_ge(proj_done, n + 1)
                    act.activation(yT[:, 0, n - 20, :], pj[n % 3][:, :], ACT.Silu).then_inc(proj_copied, 1)
                for n in range(24, 28):
                    act.wait_ge(proj_done, n + 1)
                    if n >= 25:
                        act.wait_ge(pooled, n - 24)
                    act.activation(up[:, 8:8 + SEQ], pj[n % 3][:, :], ACT.Copy).then_inc(proj_copied, 1)
                for n in range(28, 32):
                    act.wait_ge(proj_done, n + 1)
                    act.activation(yT[:, 2, n - 28, :], pj[n % 3][:, :], ACT.Sigmoid).then_inc(proj_copied, 1)
                act.wait_ge(em_arg, 1)
                act.activation(emx[:, :, :], emx[:, :, :], ACT.Exp, scale=-1.0).then_inc(gate_exp, 1)
                for g in range(4):
                    act.wait_ge(pool_mixed, g + 1)
                    act.activation(yT[:, 1, g, :], tp[g % 2][:, :], ACT.Copy,
                                   scale=sml[:, SM_NORM + 4 + g:SM_NORM + 5 + g]).then_inc(pool_done, 1)
                act.wait_ge(silu_done, NQKV)

                def square(m):
                    if m >= 2:
                        act.wait_ge(sum_done, m - 1)
                    act.activation(sq[:, m % 2, :], qkT[:, m // 4, m % 4, :], ACT.Square).then_inc(square_done, 1)

                square(0)
                for m in range(8):
                    if m + 1 < 8:
                        square(m + 1)
                    act.wait_ge(sum_done, m + 1)
                    if m >= 2:
                        act.wait_ge(qk_normed, m - 1)
                    act.activation(nrm[:, m % 2, :], pj[m % 3][:, :], ACT.Sqrt, scale=(float(DV) if m < 4 else 1.0),
                                   bias=epsc[:, 1 if m < 4 else 2:(1 if m < 4 else 2) + 1]).then_inc(root_done, 1)
                for m in range(8):
                    act.wait_ge(tok_turned, m + 1)
                    dst = (kTok if m < 4 else vTok)[:, m % 4, :, :]
                    act.activation(dst, tp[m % 2][:, :].rearrange("p (h e) -> p h e", h=NH), ACT.Copy).then_inc(tok_copied, 1)

            @block.vector
            def _(dve):
                chain = Chain(dve, dve_chain)
                dve.memset(epsc[:, 0:1], LN_EPS)
                dve.memset(epsc[:, 1:2], DV * NORM_EPS)
                dve.memset(epsc[:, 2:3], NORM_EPS).then_inc(eps_set, 1)
                dve.memset(raw[:, :, 0:2], 0.0)
                dve.memset(raw[:, :, SEQ + 2:SEQ + 4], 0.0).then_inc(pads_set, 1)
                dve.memset(mvx[:, :, :, DV:DV + 1], 1.0)

                def x_ready(t):
                    dve.wait_ge(x_in, 16 * (t + 1))
                    if t == 0:
                        dve.wait_ge(ln_in, 32)
                layer_norm_dve(dve, chain, h, stats, mv, rstd, nmr, x_ready, stats_ready, std_ready, scale_ready,
                               norm_ready, gmul_ready, lng[:, :])
                dve.wait_ge(small_copied, 1)
                dve.wait_ge(small_in, 16)
                bias = sml[:, SM_BIAS:SM_BIAS + 32]
                chain.add(dve.tensor_tensor(sp[:, 0, :, 0:8], ab[:, :, 0:8], bc(bias[:, 8:16], 1, NT), ALU.add))
                chain.add(dve.tensor_tensor(sp[:, 0, :, 8:16], ab[:, :, 24:32], bc(bias[:, 24:32], 1, NT), ALU.add))
                chain.add(dve.tensor_tensor(gg[:, :, 16:24], ab[:, :, 16:24], bc(bias[:, 16:24], 1, NT), ALU.add))
                chain.wait()
                dve.tensor_scalar(sp[:, 1, :, :], sp[:, 0, :, :], 1.0, None, ALU.mult).then_inc(gate_in, 1)
                chain.add(dve.tensor_scalar(sp[:, 2, :, 0:8], sp[:, 0, :, 0:8], 0.0, None, ALU.max))
                chain.wait()
                dve.tensor_scalar(sp[:, 2, :, 8:16], sp[:, 0, :, 8:16], 0.0, None, ALU.min).then_inc(gate_in, 1)
                dve.wait_ge(gate_ln, 1)
                dve.wait_ge(gate_in, 2)
                chain.link(dve.tensor_tensor(sp[:, 2, :, 0:8], sp[:, 2, :, 0:8], sp[:, 1, :, 0:8], ALU.add))
                dve.wait_ge(gate_exp, 2)
                chain.link(dve.tensor_tensor(sp[:, 2, :, 0:8], sp[:, 2, :, 0:8], bc(bias[:, 0:8], 1, NT), ALU.mult))
                dve.tensor_scalar(gg[:, :, 0:8], sp[:, 2, :, 0:8], -1.0, None, ALU.mult).then_inc(gates_done, 1)
                dve.tensor_tensor(gg[:, :, 8:16], sp[:, 2, :, 8:16], sp[:, 1, :, 8:16], ALU.subtract).then_inc(gates_done, 1)
                for n in range(NQKV):
                    dve.wait_ge(proj_copied, n + 1)
                    if n >= 3:
                        dve.wait_ge(silu_done, n - 2)
                    taps = sml[:, SM_CONV + TAPS * n:SM_CONV + TAPS * (n + 1)]
                    chain.link(dve.tensor_scalar(cv[:, n % 3, :], raw[:, n % 3, 0:SEQ], taps[:, 0:1], None, ALU.mult))
                    for j in range(1, TAPS):
                        ins = dve.scalar_tensor_tensor(cv[:, n % 3, :], raw[:, n % 3, j:j + SEQ], taps[:, j:j + 1],
                                                       cv[:, n % 3, :], ALU.mult, ALU.add)
                        if j < TAPS - 1:
                            chain.link(ins)
                        else:
                            ins.then_inc(conv_done, 1)
                dve.wait_ge(cum_done, 1)
                dve.tensor_copy(cum[:, :, :], gps[:, 128:224].rearrange("p (t n) -> p t n", t=NT)).then_inc(cum_copied, 1)
                dve.wait_ge(cum_copied, 1)
                dve.tensor_tensor(acol[:, :, :], gg[:, :, 16:24], cum[:, :, 16:24], ALU.subtract).then_inc(a_done, 1)
                zrow = nrm[0:4, 0, :]
                chain.link(dve.memset(zrow, 0.0))
                dve.wait_ge(a_turned, 1)
                dve.tensor_tensor_scan(mrow[0:4, 0, :], rps[0][0:4, :], zrow,
                                       0.0, ALU.max, ALU.max).then_inc(scan_done, 1)
                dve.tensor_tensor_scan(mrow[0:4, 1, ::-1], rps[1][0:4, ::-1], zrow,
                                       0.0, ALU.max, ALU.max).then_inc(scan_done, 1)
                dve.wait_ge(m_turned, 1)
                dve.tensor_tensor(emx[:, :, :], gps[:, 256:288].rearrange("p (t n) -> p t n", t=NT), cum[:, :, 16:24],
                                  ALU.add).then_inc(em_arg, 1)
                for m in range(8):
                    dve.wait_ge(root_done, m + 1)
                    chain.link(dve.reciprocal(nrm[:, m % 2, :], nrm[:, m % 2, :]))
                    dve.tensor_tensor(qkT[:, m // 4, m % 4, :], qkT[:, m // 4, m % 4, :], nrm[:, m % 2, :],
                                      ALU.mult).then_inc(qk_normed, 1)

            @block.gpsimd
            def _(pool):
                v["zero_last"](pool)
                chain = Chain(pool, pool_chain)
                chain.add(pool.memset(up[:, :], 0.0))
                chain.add(pool.memset(win[:, :, :], 0.0))
                for t in range(NT):
                    pool.wait_ge(gmul_ready, t + 1)
                    pool.wait_ge(ln_in, 32)
                    pool.tensor_tensor(h[:, t, :], h[:, t, :], lnb[:, :], ALU.add).then_inc(h_ready, 1)
                chain.wait()
                edge = cn("edge").rearrange("p (g n) -> p g n", g=4)
                pool.wait_ge(const_in, 16)
                for g in range(4):
                    pool.wait_ge(proj_copied, 25 + g)
                    chain.link(pool.tensor_tensor(win[:, 0, 1:528], up[:, 0:527], up[:, 1:528], ALU.add))
                    cur = 0
                    for lvl in range(g):
                        r = 1 << lvl
                        lo, hi = 2 * r, 528 - 2 * r
                        chain.link(pool.tensor_tensor(win[:, 1 - cur, lo:hi], win[:, cur, lo - r:hi - r],
                                                      win[:, cur, lo + r:hi + r], ALU.add))
                        cur = 1 - cur
                    w = win[:, cur, 8:8 + SEQ]
                    chain.add(pool.tensor_tensor(w[:, 0:8], w[:, 0:8], edge[:, g, 0:8], ALU.mult))
                    chain.add(pool.tensor_tensor(w[:, SEQ - 8:SEQ], w[:, SEQ - 8:SEQ], edge[:, g, 8:16], ALU.mult))
                    chain.add(pool.tensor_scalar(w[:, 8:SEQ - 8], w[:, 8:SEQ - 8], 1.0 / (2 << g), None, ALU.mult))
                    chain.wait()
                    pool.tensor_tensor(yT[:, 1, g, :], w, up[:, 8:8 + SEQ], ALU.subtract).then_inc(pooled, 1)
                    pool.wait_ge(pooled, g + 1)


def mlstm(nc, sem, sb, pb, cn, v):
    sml, epsc, yT, mq, mvx, mrow, acol, emx = (v[k] for k in ("sml", "epsc", "yT", "mq", "mvx", "mrow", "acol", "emx"))
    ident = v["ident"]
    st = ExitStack()
    with st:
        scores = sb(st, "scores", [P, 2, NT, SEQ])
        wts = sb(st, "wts", [P, 2, NT, SEQ])
        mdiag = sb(st, "mdiag", [P, 2, NT, P])
        hs = sb(st, "hs", [P, NT, NH, DV])
        tmp = sb(st, "htmp", [P, NT, DV])
        den = sb(st, "den", [P, 2, NT])
        stats, mv, rstd = sb(st, "mstats", [P, NT * NH, 6]), sb(st, "mmv", [P, NT * NH, 2]), sb(st, "mrstd", [P, NT * NH])
        qb = [pb(st, f"qb{i}") for i in range(2)]
        mb = [pb(st, f"mb{i}") for i in range(2)]
        nu = [pb(st, f"nu{i}") for i in range(4)]
        score_done, score_copied, max_spread, diag_ready, exp_done, weighted = (
            sem(n) for n in ("score_done", "score_copied", "max_spread", "diag_ready", "exp_done", "weighted"))
        num_done, den_abs, num_used = sem("num_done"), sem("den_abs"), sem("num_used")
        mvar_ready, mroot_done, mnormed, mturned, yml_done = (
            sem(n) for n in ("mvar_ready", "mroot_done", "mnormed", "mturned", "yml_done"))
        dve_chain = sem("mlstm_dve_chain")

        def span(d, j):
            return (j * P, SEQ) if d == 0 else (0, (j + 1) * P)

        with nc.Block() as block:
            @block.tensor
            def _(pe):
                def score(h):
                    rows = slice(QK * (h % 2), QK * (h % 2) + QK)
                    for j in range(NT):
                        n = 4 * h + j
                        if n >= 2:
                            pe.wait_ge(score_copied, n - 1)
                        pe.matmul(qb[n % 2][:, :], mq[rows, 2 + h // 2, j * P:(j + 1) * P], mq[rows, h // 2, :],
                                  start=True, stop=True).then_inc(score_done, 1)

                def spread(n):
                    h, d = n // 2, n % 2
                    if n >= 2:
                        pe.wait_ge(exp_done, n - 1)
                        pe.wait_ge(diag_ready, n - 1)
                    pe.matmul(mb[n % 2][:, :], cn("sel", 4)[:, h * P:(h + 1) * P], mrow[0:4, d, :],
                              start=True, stop=True).then_inc(max_spread, 1)

                def numerator(n):
                    h, d = n // 2, n % 2
                    pe.wait_ge(weighted, n + 1)
                    if n >= 2:
                        pe.wait_ge(num_used, n - 1)
                    for i in range(NT):
                        js = range(i + 1) if d == 0 else range(i, NT)
                        for j in js:
                            last = pe.matmul(nu[2 * (n % 2) + i // 2][:, (i % 2) * (DV + 1):(i % 2 + 1) * (DV + 1)],
                                             wts[:, n % 2, j, i * P:(i + 1) * P], mvx[:, j, h, :],
                                             start=(j == js[0]), stop=(j == js[-1]))
                    last.then_inc(num_done, 1)

                score(0)
                spread(0)
                spread(1)
                for h in range(NH):
                    if h + 1 < NH:
                        score(h + 1)
                        spread(2 * h + 2)
                    numerator(2 * h)
                    if h + 1 < NH:
                        spread(2 * h + 3)
                    numerator(2 * h + 1)
                for h in range(NH):
                    pe.wait_ge(mnormed, NT * NH)
                    if h >= 2:
                        pe.wait_ge(yml_done, h - 1)
                    for t in range(NT):
                        last = pe.transpose(qb[h % 2][:, t * P:(t + 1) * P], hs[:, t, h, :], ident)
                    last.then_inc(mturned, 1)

            @block.scalar
            def _(act):
                def copy_scores(h):
                    if h >= 2:
                        act.wait_ge(weighted, 2 * (h - 1))
                    for j in range(NT):
                        n = 4 * h + j
                        act.wait_ge(score_done, n + 1)
                        act.activation(scores[:, h % 2, j, :], qb[n % 2][:, :], ACT.Copy).then_inc(score_copied, 1)

                def exps(n):
                    h, d = n // 2, n % 2
                    act.wait_ge(diag_ready, n + 1)
                    if n >= 2:
                        act.wait_ge(num_done, n - 1)
                    for j in range(NT):
                        bias = acol[:, j, 4 * d + h:4 * d + h + 1]
                        last = act.activation(wts[:, n % 2, j, j * P:(j + 1) * P], mdiag[:, n % 2, j, :], ACT.Exp, bias=bias)
                        lo, hi = ((j + 1) * P, SEQ) if d == 0 else (0, j * P)
                        if lo < hi:
                            last = act.activation(wts[:, n % 2, j, lo:hi], mb[n % 2][:, lo:hi], ACT.Exp, bias=bias, scale=-1.0)
                    last.then_inc(exp_done, 1)

                def absolute(n):
                    act.wait_ge(num_done, n + 1)
                    if n >= 2:
                        act.wait_ge(num_used, n - 1)
                    for i2 in range(2):
                        src = nu[2 * (n % 2) + i2][:, 0:2 * (DV + 1)].rearrange("p (i e) -> p i e", i=2)[:, :, DV]
                        last = act.activation(den[:, n % 2, 2 * i2:2 * i2 + 2], src, ACT.Abs)
                    last.then_inc(den_abs, 1)

                copy_scores(0)
                exps(0)
                exps(1)
                for h in range(NH):
                    if h + 1 < NH:
                        copy_scores(h + 1)
                    absolute(2 * h)
                    if h + 1 < NH:
                        exps(2 * h + 2)
                    absolute(2 * h + 1)
                    if h + 1 < NH:
                        exps(2 * h + 3)
                act.wait_ge(mvar_ready, 1)
                act.activation(rstd[:, :], mv[:, :, 1], ACT.Sqrt, bias=epsc[:, 2:3]).then_inc(mroot_done, 1)

            @block.vector
            def _(dve):
                chain = Chain(dve, dve_chain)

                def diag(n):
                    dve.wait_ge(max_spread, n + 1)
                    if n >= 2:
                        dve.wait_ge(exp_done, n - 1)
                    neg = cn("neg_fwd" if n % 2 == 0 else "neg_bwd")
                    dve.scalar_tensor_tensor(mdiag[:, n % 2, :, :], mb[n % 2][:, :].rearrange("p (j i) -> p j i", j=NT), -1.0,
                                             bc(neg, 1, NT), ALU.mult, ALU.add).then_inc(diag_ready, 1)

                def weigh(n):
                    h, d = n // 2, n % 2
                    dve.wait_ge(exp_done, n + 1)
                    dve.wait_ge(score_copied, 4 * (h + 1))
                    for j in range(NT):
                        lo, hi = span(d, j)
                        w = wts[:, n % 2, j, lo:hi]
                        last = dve.tensor_tensor(w, w, scores[:, h % 2, j, lo:hi], ALU.mult)
                    last.then_inc(weighted, 1)

                def divide(n):
                    h, d = n // 2, n % 2
                    dn = den[:, n % 2, :]
                    dve.wait_ge(den_abs, n + 1)
                    chain.link(dve.tensor_tensor(dn, dn, emx[:, :, 4 * d + h], ALU.max))
                    chain.link(dve.reciprocal(dn, dn))
                    for i2 in range(2):
                        src = nu[2 * (n % 2) + i2][:, 0:2 * (DV + 1)].rearrange("p (i e) -> p i e", i=2)[:, :, 0:DV]
                        dst = hs[:, 2 * i2:2 * i2 + 2, h, :] if d == 0 else tmp[:, 2 * i2:2 * i2 + 2, :]
                        last = dve.tensor_tensor(dst, src, bc(dn[:, 2 * i2:2 * i2 + 2], 2, DV), ALU.mult)
                    last.then_inc(num_used, 1)
                    if d == 1:
                        dve.wait_ge(num_used, n + 1)
                        chain.link(dve.tensor_tensor(hs[:, :, h, :], hs[:, :, h, :], tmp[:, :, :], ALU.add))

                diag(0)
                diag(1)
                weigh(0)
                for n in range(2 * NH):
                    if n + 2 < 2 * NH:
                        diag(n + 2)
                    if n + 1 < 2 * NH:
                        weigh(n + 1)
                    divide(n)
                for g in range(NT * NH):
                    chain.add(dve.bn_stats(stats[:, g, :], hs[:, g // NH, g % NH, :]))
                chain.wait()
                for g in range(NT * NH):
                    last = dve.bn_aggr(mv[:, g, :], stats[:, g, :])
                last.then_inc(mvar_ready, 1)
                dve.wait_ge(mroot_done, 1)
                chain.link(dve.reciprocal(rstd[:, :], rstd[:, :]))
                for g in range(NT * NH):
                    o = hs[:, g // NH, g % NH, :]
                    dve.tensor_scalar(o, o, mv[:, g, 0:1], rstd[:, g:g + 1], ALU.subtract, ALU.mult).then_inc(mnormed, 1)
                for h in range(NH):
                    dve.wait_ge(mturned, h + 1)
                    dve.scalar_tensor_tensor(yT[:, 2, h, :], qb[h % 2][:, :], sml[:, SM_NORM + 8 + h:SM_NORM + 9 + h],
                                             yT[:, 2, h, :], ALU.mult, ALU.mult).then_inc(yml_done, 1)

            @block.gpsimd
            def _(pool):
                v["zero_last"](pool)


def deltanet(nc, sem, sb, pb, cn, v):
    sml, epsc, yT, qkT, kTok, vTok, beta, cum, gg = (
        v[k] for k in ("sml", "epsc", "yT", "qkT", "kTok", "vTok", "beta", "cum", "gg"))
    ident, ones = v["ident"], v["ones"]
    st = ExitStack()
    NB = 2 * NT
    BATCH = [(m % 2, m // 2 if m % 2 == 0 else NT - 1 - m // 2) for m in range(NB)]
    with st:
        def four(name, n):
            return sb(st, name, [P, n, NH, P])

        dec, mt, tt, tn, at, qe = four("dec", 2), four("mt", 4), four("tt", 4), four("tn", 4), four("at", 4), four("qe", 4)
        ot, y1s = four("ot", 2), four("y1s", 2)
        rhs, vn, vnd = four("rhs", 2), four("vn", 2), four("vnd", 2)
        state = four("state", 2)
        oT = sb(st, "oT", [P, NH, SEQ])
        eg = sb(st, "eg", [P, NT, 3, 8])
        pr = [pb(st, f"pr{i}") for i in range(2)]
        lv = [[pb(st, f"lv{i}{j}") for j in range(2)] for i in range(2)]
        sc = [pb(st, f"sc{i}") for i in range(2)]
        (gr_done, kk_done, qk_done, turn_done, dif_ready, dec_ready, egr_ready, qe_ready, kk_used, mt_ready, tt_ready,
         at_ready, tn_copied) = (sem("dn_" + n) for n in (
             "gr_done", "kk_done", "qk_done", "turn_done", "dif_ready", "dec_ready", "egr_ready", "qe_ready", "kk_used",
             "mt_ready", "tt_ready", "at_ready", "tn_copied"))
        ot_ready, y1_done, y1_copied, p2_done, t_updated = (
            sem("dn_" + n) for n in ("ot_ready", "y1_done", "y1_copied", "p2_done", "t_updated"))
        ks_done, r_ready, tr_done, vn_ready, ds_done, o_done, s_updated, o_taken = (
            sem("dn_" + n) for n in ("ks_done", "r_ready", "tr_done", "vn_ready", "ds_done", "o_done", "s_updated", "o_taken"))
        eg_arg, eg_ready, s_zero = sem("dn_eg_arg"), sem("dn_eg_ready"), sem("dn_s_zero")
        osq_done, osum_done, oroot_done, y_done = (sem("dn_" + n) for n in ("osq", "osum", "oroot", "y"))
        dve_chain, pool_chain = sem("dn_dve_chain"), sem("dn_pool_chain")

        order = []
        for m in range(2):
            order += [("gram", m), ("attn", m), ("turn", m)]
        for p in range(NT):
            a, b = 2 * p, 2 * p + 1
            for l in range(1, NL):
                order += [("y1", a, l), ("y1", b, l)]
                if p >= 1 and l <= 3:
                    order += [(("read", "solve", "write")[l - 1], m) for m in (a - 2, b - 2)]
                if p + 1 < NT:
                    order += {3: [("gram", a + 2)], 4: [("attn", a + 2), ("turn", a + 2)],
                              5: [("gram", b + 2)], 6: [("attn", b + 2), ("turn", b + 2)]}.get(l, [])
                order += [("p2", a, l), ("p2", b, l)]
        for step in ("read", "solve", "write"):
            order += [(step, NB - 2), (step, NB - 1)]

        def at_level(m, l):
            return (m // 2) * 2 * (NL - 1) + 2 * (l - 1) + m % 2

        def tile(t):
            return slice(t * P, (t + 1) * P)

        def heads(ap):
            return ap[:, :].rearrange("p (h e) -> p h e", h=NH)

        with nc.Block() as block:
            @block.tensor
            def _(pe):
                pe.wait_ge(s_zero, 2)
                for op in order:
                    kind, m = op[0], op[1]
                    d, t = BATCH[m]
                    tri = cn("upto" if d == 0 else "after")
                    if kind == "gram":
                        if m >= 1:
                            pe.wait_ge(at_ready, m)
                            pe.wait_ge(tn_copied, m)
                        for h in range(NH):
                            last = pe.matmul(pr[0][:, tile(h)], gg[:, t, 4 * d + h:4 * d + h + 1].to_broadcast([P, P]), tri,
                                             start=True, stop=True)
                        last.then_inc(gr_done, 1)
                        for h in range(NH):
                            last = pe.matmul(pr[1][:, tile(h)], qkT[:, 1, h, tile(t)], qkT[:, 1, h, tile(t)],
                                             start=True, stop=True)
                        last.then_inc(kk_done, 1)
                    elif kind == "attn":
                        pe.wait_ge(dif_ready, m + 1)
                        pe.wait_ge(egr_ready, m + 1)
                        for h in range(NH):
                            last = pe.matmul(pr[0][:, tile(h)], qkT[:, 1, h, tile(t)], qkT[:, 0, h, tile(t)],
                                             start=True, stop=True)
                        last.then_inc(qk_done, 1)
                    elif kind == "turn":
                        pe.wait_ge(kk_used, m + 1)
                        pe.wait_ge(tt_ready, m + 1)
                        for h in range(NH):
                            last = pe.transpose(pr[1][:, tile(h)], tt[:, m % 4, h, :], ident)
                        last.then_inc(turn_done, 1)
                    elif kind == "y1":
                        l = op[2]
                        i = at_level(m, l)
                        pe.wait_ge(ot_ready, i + 1)
                        pe.wait_ge(tn_copied, m + 1)
                        if i >= 2:
                            pe.wait_ge(t_updated, i - 1)
                        for h in range(NH):
                            last = pe.matmul(lv[m % 2][0][:, tile(h)], ot[:, i % 2, h, :], tn[:, m % 4, h, :],
                                             start=True, stop=True)
                        last.then_inc(y1_done, 1)
                    elif kind == "p2":
                        l = op[2]
                        pe.wait_ge(y1_copied, at_level(m, l) + 1)
                        for h in range(NH):
                            if l < NL - 1:
                                pe.matmul(lv[m % 2][0][:, tile(h)], tt[:, m % 4, h, :], y1s[:, m % 2, h, :],
                                          start=True, stop=True)
                            last = pe.matmul(lv[m % 2][1][:, tile(h)], y1s[:, m % 2, h, :], tt[:, m % 4, h, :],
                                             start=True, stop=True)
                        last.then_inc(p2_done, 1)
                    elif kind == "read":
                        if m >= 2:
                            pe.wait_ge(s_updated, m - 1)
                        if m >= 1:
                            pe.wait_ge(r_ready, m)
                            if m % 2 == 0:
                                pe.wait_ge(s_updated, m)
                        for h in range(NH):
                            last = pe.matmul(sc[m % 2][:, tile(h)], qkT[:, 1, h, tile(t)], state[:, d, h, :],
                                             start=True, stop=True)
                        last.then_inc(ks_done, 1)
                    elif kind == "solve":
                        pe.wait_ge(r_ready, m + 1)
                        pe.wait_ge(t_updated, at_level(m, NL - 1) + 1)
                        for h in range(NH):
                            last = pe.matmul(sc[m % 2][:, tile(h)], tt[:, m % 4, h, :], rhs[:, d, h, :], start=True, stop=True)
                        last.then_inc(tr_done, 1)
                    elif kind == "write":
                        pe.wait_ge(vn_ready, m + 1)
                        pe.wait_ge(at_ready, m + 1)
                        pe.wait_ge(qe_ready, m + 1)
                        for h in range(NH):
                            pe.matmul(sc[m % 2][:, tile(h)], vn[:, d, h, :], at[:, m % 4, h, :], start=True, stop=False)
                            last = pe.matmul(sc[m % 2][:, tile(h)], state[:, d, h, :], qe[:, m % 4, h, :], start=False, stop=True)
                        last.then_inc(o_done, 1)
                        pe.wait_ge(o_taken, m + 1)
                        for h in range(NH):
                            last = pe.matmul(sc[m % 2][:, tile(h)], kTok[:, t, h, :], vnd[:, d, h, :], start=True, stop=True)
                        last.then_inc(ds_done, 1)
                for h in range(NH):
                    pe.wait_ge(osq_done, h + 1)
                    if h >= 2:
                        pe.wait_ge(oroot_done, h - 1)
                    pe.matmul(pr[h % 2][:, :], ones, rhs[:, h % 2, :, :].rearrange("p h e -> p (h e)"),
                              start=True, stop=True).then_inc(osum_done, 1)

            @block.scalar
            def _(act):
                act.wait_ge(eg_arg, 1)
                act.activation(eg[:, :, :, :], eg[:, :, :, :], ACT.Exp).then_inc(eg_ready, 1)
                for op in order:
                    kind, m = op[0], op[1]
                    d, t = BATCH[m]
                    if kind == "gram":
                        act.wait_ge(gr_done, m + 1)
                        if m >= 4:
                            act.wait_ge(o_done, m - 3)
                        act.activation(qe[:, m % 4, :, :], heads(pr[0]), ACT.Exp).then_inc(egr_ready, 1)
                        act.wait_ge(dif_ready, m + 1)
                        act.activation(dec[:, m % 2, :, :], dec[:, m % 2, :, :], ACT.Exp).then_inc(dec_ready, 1)
                    elif kind == "turn":
                        act.wait_ge(turn_done, m + 1)
                        act.activation(tn[:, m % 4, :, :], heads(pr[1]), ACT.Copy).then_inc(tn_copied, 1)
                    elif kind == "y1":
                        act.wait_ge(y1_done, at_level(m, op[2]) + 1)
                        act.activation(y1s[:, m % 2, :, :], heads(lv[m % 2][0]), ACT.Copy).then_inc(y1_copied, 1)
                    elif kind == "write" and m < NB // 2:
                        act.wait_ge(o_done, m + 1)
                        act.activation(oT[:, :, tile(t)], heads(sc[m % 2]), ACT.Copy).then_inc(o_taken, 1)
                for h in range(NH):
                    act.wait_ge(o_taken, NB)
                    if h >= 2:
                        act.wait_ge(osum_done, h - 1)
                    act.activation(rhs[:, h % 2, :, :].rearrange("p h e -> p (h e)"), oT[:, h, :], ACT.Square).then_inc(osq_done, 1)
                    act.wait_ge(osum_done, h + 1)
                    if h >= 2:
                        act.wait_ge(y_done, h - 1)
                    act.activation(vn[:, h % 2, :, :].rearrange("p h e -> p (h e)"), pr[h % 2][:, :], ACT.Sqrt,
                                   scale=1.0 / DV, bias=epsc[:, 2:3]).then_inc(oroot_done, 1)

            @block.vector
            def _(dve):
                chain = Chain(dve, dve_chain)
                for d in range(2):
                    dve.memset(state[:, d, :, :], 0.0).then_inc(s_zero, 1)
                chain.add(dve.tensor_copy(eg[:, :, 0, :], cum[:, :, 0:8]))
                chain.add(dve.tensor_tensor(eg[:, :, 1, :], cum[:, :, 8:16], cum[:, :, 0:8], ALU.subtract))
                chain.wait()
                dve.tensor_copy(eg[:, :, 2, :], cum[:, :, 8:16]).then_inc(eg_arg, 1)
                for op in order:
                    kind, m = op[0], op[1]
                    d, t = BATCH[m]
                    col = slice(4 * d, 4 * d + 4)
                    if kind == "gram":
                        dve.wait_ge(egr_ready, m + 1)
                        if m >= 2:
                            dve.wait_ge(at_ready, m - 1)
                        dd = dec[:, m % 2, :, :]
                        chain.link(dve.tensor_tensor(dd, heads(pr[0]), bc(cum[:, t, col], 2, P), ALU.subtract))
                        dve.tensor_tensor(dd, dd, bc(cn("neg_fwd" if d == 0 else "neg_bwd"), 1, NH), ALU.add).then_inc(dif_ready, 1)
                        dve.wait_ge(kk_done, m + 1)
                        dve.wait_ge(dec_ready, m + 1)
                        if m >= 4:
                            dve.wait_ge(ot_ready, at_level(m - 4, NL - 1) + 1)
                            dve.wait_ge(tr_done, m - 3)
                        dve.tensor_tensor(mt[:, m % 4, :, :], heads(pr[1]), dd, ALU.mult).then_inc(kk_used, 1)
                        dve.wait_ge(kk_used, m + 1)
                        dve.tensor_tensor(mt[:, m % 4, :, :], mt[:, m % 4, :, :], bc(beta[:, t, col], 2, P), ALU.mult).then_inc(mt_ready, 1)
                        dve.wait_ge(mt_ready, m + 1)
                        chain.link(dve.scalar_tensor_tensor(tt[:, m % 4, :, :], mt[:, m % 4, :, :], -1.0,
                                                            bc(cn(f"level{d}_1"), 1, NH), ALU.mult, ALU.mult))
                        dve.tensor_tensor(tt[:, m % 4, :, :], tt[:, m % 4, :, :], bc(ident, 1, NH), ALU.add).then_inc(tt_ready, 1)
                    elif kind == "attn":
                        dve.wait_ge(qk_done, m + 1)
                        if m >= 4:
                            dve.wait_ge(o_done, m - 3)
                        dve.tensor_tensor(at[:, m % 4, :, :], heads(pr[0]), dec[:, m % 2, :, :], ALU.mult).then_inc(at_ready, 1)
                    elif kind == "p2":
                        l = op[2]
                        dve.wait_ge(p2_done, at_level(m, l) + 1)
                        if l < NL - 1:
                            chain.add(dve.tensor_tensor(tn[:, m % 4, :, :], tn[:, m % 4, :, :], heads(lv[m % 2][0]), ALU.subtract))
                            chain.wait()
                        dve.tensor_tensor(tt[:, m % 4, :, :], tt[:, m % 4, :, :], heads(lv[m % 2][1]), ALU.subtract).then_inc(t_updated, 1)
                    elif kind == "read":
                        dve.wait_ge(ks_done, m + 1)
                        dve.wait_ge(eg_ready, 1)
                        r = rhs[:, d, :, :]
                        chain.link(dve.tensor_tensor(r, heads(sc[m % 2]), bc(eg[:, t, 0, col], 2, DV), ALU.mult))
                        dve.tensor_tensor(r, vTok[:, t, :, :], r, ALU.subtract).then_inc(r_ready, 1)
                    elif kind == "solve":
                        dve.wait_ge(tr_done, m + 1)
                        chain.link(dve.tensor_tensor(vn[:, d, :, :], heads(sc[m % 2]), bc(beta[:, t, col], 2, DV), ALU.mult))
                        if m >= 2:
                            dve.wait_ge(ds_done, m - 1)
                        dve.tensor_tensor(vnd[:, d, :, :], vn[:, d, :, :], bc(eg[:, t, 1, col], 2, DV), ALU.mult).then_inc(vn_ready, 1)
                    elif kind == "write":
                        dve.wait_ge(o_done, m + 1)
                        if m >= NB // 2:
                            dve.tensor_tensor(oT[:, :, tile(t)], oT[:, :, tile(t)], heads(sc[m % 2]), ALU.add).then_inc(o_taken, 1)
                        s = state[:, d, :, :]
                        chain.link(dve.tensor_tensor(s, s, bc(eg[:, t, 2, col], 2, DV), ALU.mult))
                        dve.wait_ge(ds_done, m + 1)
                        dve.tensor_tensor(s, s, heads(sc[m % 2]), ALU.add).then_inc(s_updated, 1)
                for h in range(NH):
                    dve.wait_ge(oroot_done, h + 1)
                    r = vn[:, h % 2, :, :].rearrange("p h e -> p (h e)")
                    chain.link(dve.reciprocal(r, r))
                    chain.link(dve.tensor_tensor(r, r, yT[:, 0, h, :], ALU.mult))
                    dve.scalar_tensor_tensor(yT[:, 0, h, :], oT[:, h, :], sml[:, SM_NORM + h:SM_NORM + h + 1], r,
                                             ALU.mult, ALU.mult).then_inc(y_done, 1)

            @block.gpsimd
            def _(pool):
                v["zero_last"](pool)
                for op in order:
                    kind, m = op[0], op[1]
                    d, t = BATCH[m]
                    if kind == "gram":
                        pool.wait_ge(egr_ready, m + 1)
                        pool.tensor_tensor(qe[:, m % 4, :, :], qe[:, m % 4, :, :], qkT[:, 0, :, tile(t)], ALU.mult).then_inc(qe_ready, 1)
                    elif kind == "y1":
                        l = op[2]
                        i = at_level(m, l)
                        pool.wait_ge(mt_ready, m + 1)
                        if i >= 2:
                            pool.wait_ge(y1_done, i - 1)
                        pool.tensor_tensor(ot[:, i % 2, :, :], mt[:, m % 4, :, :], bc(cn(f"level{d}_{LEVELS[l]}"), 1, NH),
                                           ALU.mult).then_inc(ot_ready, 1)


def merge(nc, sem, sb, pb, cn, v):
    w_in, w_branch, w_out = v["w_in"], v["w_branch"], v["w_out"]
    sml, epsc, hT, yT, h2, rows_all, flag = (v[k] for k in ("sml", "epsc", "hT", "yT", "h2", "rows_all", "flag"))
    ident, ones = v["ident"], v["ones"]
    st = ExitStack()
    with st:
        gw = sb(st, "gw", [P, 3, KT, 512])
        bw = sb(st, "bw", [P, 3, NH, 512])
        wo = gw
        merged = sb(st, "merged", [P, KT, SEQ])
        sig = sb(st, "sig", [P, 2, SEQ])
        part = sb(st, "part", [P, 2, SEQ])
        lng, lnb = sb(st, "lng2", [P, DM]), sb(st, "lnb2", [P, DM])
        stats, mv, rstd, nmr = sb(st, "stats2", [P, NT, 2, 6]), sb(st, "mv2", [P, NT, 2]), sb(st, "rstd2", [P, NT]), sb(st, "nmr2", [P, NT])
        r4 = lambda name: sb(st, name, [P, NT, NE])
        sco, sel, rank, gt, pos, dest, alt, prod = (r4(n) for n in ("sco", "sel", "rank", "gt", "pos", "dest", "alt", "prod"))
        onek = sb(st, "onek", [P, 2, NT, NE])
        mask = r4("mask")
        hi, lo = sb(st, "hi", [P, NT * NG, 2]), sb(st, "lo", [P, NT * NG, 2])
        g3 = sb(st, "g3", [P, 4, NT * NG])
        gm = sb(st, "gm", [P, 2, NT])
        sk = sb(st, "sk", [P, 4, NT])
        dk = sb(st, "dk", [P, 2, NT])
        dki = sb(st, "dki", [P, 2, NT], I32)
        pay = sb(st, "pay", [P, NT, 2, 4], I32)
        ce = sb(st, "ce", [P, 5, NE])
        eo = sb(st, "eo", [1, OVER, NE])
        eov = sb(st, "eov", [1, 1 + OVER])
        far = sb(st, "far", [P, TABLE * 4 // P], I32)
        gp = [pb(st, f"gp{i}") for i in range(3)]
        yp = [pb(st, f"yp{i}") for i in range(3)]
        lp, cp = pb(st, "lp"), pb(st, "cp")
        gw_in = [sem(f"gw_in{i}") for i in range(3)]
        wo_in, ln_in, far_out, h2_out, tab_in = sem("wo_in"), sem("ln2_in"), sem("far_out"), sem("h2_out"), sem("tab_in")
        far_set, gate_done, branch_done, sig_done, part_done, merged_sum = (
            sem("mg_" + n) for n in ("far_set", "gate_done", "branch_done", "sig_done", "part_done", "merged_sum"))
        out_done, res_done = sem("mg_out_done"), sem("mg_res_done")
        stats_ready, std_ready, scale_ready, norm_ready, gmul_ready, h2_ready = (
            sem(f"ln2_{n}") for n in ("stats", "std", "scale", "norm", "gmul", "h"))
        turned, turn_copied, logit_done, score_done = sem("mg_turned"), sem("mg_turn_copied"), sem("mg_logits"), sem("mg_scores")
        mask_done, pos_done, pay_done, scattered, rows_done = sem("mg_mask"), sem("mg_pos"), sem("mg_pay"), sem("mg_scattered"), sem("mg_rows_done")
        dve_chain = sem("mg_dve_chain")
        w_rows = w_in.rearrange("(p k) n -> p k n", k=KT)
        NU = 6
        with nc.Block() as block:
            @block.sync
            def _(sp):
                for u in range(NU):
                    half, r = u // 3, u % 3
                    if u >= 3:
                        sp.wait_ge(branch_done, 4 * (u - 2))
                    at = C_G + r * DM + half * 512
                    sp.dma_start(gw[:, u % 3, :, :], w_rows[:, :, at:at + 512]).then_inc(gw_in[u % 3], 16)
                    sp.dma_start(bw[:, u % 3, :, :], w_branch[r].rearrange("(k p) n -> p k n", p=P)[:, :, half * 512:half * 512 + 512])\
                        .then_inc(gw_in[u % 3], 16)
                    if u == 2:
                        sp.dma_start(lng[:, :], v["ln_mix_g"].to_broadcast([P, DM])).then_inc(ln_in, 16)
                        sp.dma_start(lnb[:, :], v["ln_mix_b"].to_broadcast([P, DM])).then_inc(ln_in, 16)
                        sp.wait_ge(far_set, 1)
                        sp.dma_start(v["slots_dram"].rearrange("(p a) b -> p (a b)", p=P), far[:, :]).then_inc(far_out, 16)
                for half in range(2):
                    sp.wait_ge(branch_done, 4 * (half + 4))
                    sp.dma_start(wo[:, half, :, :], w_out.rearrange("(k p) n -> p k n", p=P)[:, :, half * 512:half * 512 + 512]).then_inc(wo_in, 16)
                for t in range(NT):
                    sp.wait_ge(h2_ready, t + 1)
                    sp.dma_start(v["h2_dram"][t * P:(t + 1) * P, :], h2[:, t, :]).then_inc(h2_out, 16)
                sp.wait_ge(scattered, 16 * 2 * NT)
                sd = v["slots_dram"]
                for half in range(2):
                    rows = slice(half * SLOTS, (half + 1) * SLOTS)
                    sp.dma_start(rows_all[rows, 0:NE, :], sd[0:SLOTS * NE, :].rearrange("(s e) w -> s e w", e=NE)).then_inc(tab_in, 16)
                    sp.dma_start(rows_all[rows, NE:NE + OVER, :], sd[SLOTS * NE:, :].rearrange("(s e) w -> s e w", e=OVER)).then_inc(tab_in, 16)
                sp.wait_ge(h2_out, 16 * NT)

            @block.tensor
            def _(pe):
                for u in range(NU):
                    half, r = u // 3, u % 3
                    pe.wait_ge(gw_in[u % 3], 32 * (u // 3 + 1))
                    for m in range(4):
                        n = 4 * u + m
                        if n >= 3:
                            pe.wait_ge(sig_done, n - 2)
                            pe.wait_ge(part_done, n - 2)
                        for k in range(KT):
                            last = pe.matmul(gp[n % 3][:, :], gw[:, u % 3, k, m * P:(m + 1) * P], hT[:, k, :],
                                             start=(k == 0), stop=(k == KT - 1))
                        last.then_inc(gate_done, 1)
                        for k in range(NH):
                            last = pe.matmul(yp[n % 3][:, :], bw[:, u % 3, k, m * P:(m + 1) * P], yT[:, r, k, :],
                                             start=(k == 0), stop=(k == NH - 1))
                        last.then_inc(branch_done, 1)
                pe.wait_ge(wo_in, 32)
                pe.wait_ge(merged_sum, 24)
                for n in range(2 * NT):
                    t, half = n // 2, n % 2
                    if n < 3:
                        pe.wait_ge(part_done, 24)
                    else:
                        pe.wait_ge(res_done, n - 2)
                    for k in range(KT):
                        last = pe.matmul(yp[n % 3][:, :], merged[:, k, t * P:(t + 1) * P], wo[:, half, k, :],
                                         start=(k == 0), stop=(k == KT - 1))
                    last.then_inc(out_done, 1)
                for n in range(2 * NT):
                    t, half = n // 2, n % 2
                    pe.wait_ge(h2_ready, t + 1)
                    if n >= 2:
                        pe.wait_ge(turn_copied, n - 1)
                    for k in range(4):
                        last = pe.transpose(gp[n % 2][:, k * P:(k + 1) * P], h2[:, t, 4 * half + k::KT], ident)
                    last.then_inc(turned, 1)
                wr = sml[:, SM_RW:SM_RW + KT * NE].rearrange("p (k n) -> p k n", k=KT)
                pe.wait_ge(turn_copied, 2 * NT)
                for t in range(NT):
                    for k in range(KT):
                        last = pe.matmul(lp[:, t * NE:(t + 1) * NE], hT[:, k, t * P:(t + 1) * P], wr[:, k, :],
                                         start=(k == 0), stop=(k == KT - 1))
                last.then_inc(logit_done, 1)
                pe.wait_ge(mask_done, 1)
                for t in range(NT):
                    pe.matmul(cp[:, t * NE:(t + 1) * NE], cn("before"), mask[:, t, :], start=True, stop=(t == 0))
                    for u in range(t):
                        pe.matmul(cp[:, t * NE:(t + 1) * NE], ones, mask[:, u, :], start=False, stop=(u == t - 1))
                for t in range(NT):
                    last = pe.matmul(cp[:, NT * NE:(NT + 1) * NE], ones, mask[:, t, :], start=(t == 0), stop=(t == NT - 1))
                last.then_inc(pos_done, 1)

            @block.scalar
            def _(act):
                for n in range(4 * NU):
                    act.wait_ge(gate_done, n + 1)
                    if n >= 2:
                        act.wait_ge(part_done, n - 1)
                    act.activation(sig[:, n % 2, :], gp[n % 3][:, :], ACT.Sigmoid).then_inc(sig_done, 1)
                layer_norm_act(act, h2, mv, rstd, nmr, epsc[:, 0:1], stats_ready, std_ready, scale_ready, norm_ready)
                for n in range(2 * NT):
                    t, half = n // 2, n % 2
                    act.wait_ge(turned, n + 1)
                    act.activation(hT[:, 4 * half:4 * half + 4, t * P:(t + 1) * P],
                                   gp[n % 2][:, :].rearrange("p (k s) -> p k s", k=4), ACT.Copy).then_inc(turn_copied, 1)
                act.wait_ge(logit_done, 1)
                act.activation(sco[:, :, :], lp[:, 0:NT * NE].rearrange("p (t e) -> p t e", t=NT), ACT.Sigmoid).then_inc(score_done, 1)

            @block.vector
            def _(dve):
                chain = Chain(dve, dve_chain)
                dve.memset(far[:, :], FAR).then_inc(far_set, 1)
                for n in range(4 * NU):
                    u, m = n // 4, n % 4
                    half, r = u // 3, u % 3
                    dve.wait_ge(sig_done, n + 1)
                    dve.wait_ge(branch_done, n + 1)
                    dst = merged[:, 4 * half + m, :]
                    if r == 0:
                        dve.tensor_tensor(dst, sig[:, n % 2, :], yp[n % 3][:, :], ALU.mult).then_inc(part_done, 1)
                        dve.sem_inc(merged_sum, 1)
                    else:
                        dve.tensor_tensor(part[:, n % 2, :], sig[:, n % 2, :], yp[n % 3][:, :], ALU.mult).then_inc(part_done, 1)
                        dve.wait_ge(part_done, n + 1)
                        dve.tensor_tensor(dst, dst, part[:, n % 2, :], ALU.add).then_inc(merged_sum, 1)
                for n in range(2 * NT):
                    t, half = n // 2, n % 2
                    dve.wait_ge(out_done, n + 1)
                    r = h2[:, t, half * 512:half * 512 + 512]
                    dve.scalar_tensor_tensor(r, r, ALPHA, yp[n % 3][:, :], ALU.mult, ALU.add).then_inc(res_done, 1)

                def x_ready(t):
                    dve.wait_ge(res_done, 2 * t + 2)
                    if t == 0:
                        dve.wait_ge(ln_in, 32)
                layer_norm_dve(dve, chain, h2, stats, mv, rstd, nmr, x_ready, stats_ready, std_ready, scale_ready,
                               norm_ready, gmul_ready, lng[:, :])
                rb = sml[:, SM_RB:SM_RB + NE]
                flat = lambda ap: ap.rearrange("p t (g e) -> p (t g) e", e=EPG)
                dve.wait_ge(score_done, 1)
                chain.link(dve.tensor_tensor(sel[:, :, :], sco[:, :, :], bc(rb, 1, NT), ALU.add))
                sv = flat(sel[:, :, :])
                chain.add(dve.tensor_tensor(hi[:, :, :], sv[:, :, 0::2], sv[:, :, 1::2], ALU.max))
                chain.link(dve.tensor_tensor(lo[:, :, :], sv[:, :, 0::2], sv[:, :, 1::2], ALU.min))
                chain.add(dve.tensor_tensor(g3[:, 0, :], hi[:, :, 0], hi[:, :, 1], ALU.max))
                chain.add(dve.tensor_tensor(g3[:, 1, :], hi[:, :, 0], hi[:, :, 1], ALU.min))
                chain.link(dve.tensor_tensor(g3[:, 2, :], lo[:, :, 0], lo[:, :, 1], ALU.max))
                chain.link(dve.tensor_tensor(g3[:, 1, :], g3[:, 1, :], g3[:, 2, :], ALU.max))
                chain.link(dve.tensor_tensor(g3[:, 0, :], g3[:, 0, :], g3[:, 1, :], ALU.add))
                gs = g3[:, 0, :].rearrange("p (t g) -> p t g", t=NT)
                eq = g3[:, 1, :].rearrange("p (t g) -> p t g", t=NT)
                chain.link(dve.tensor_reduce(gm[:, 0, :], gs, AX.X, ALU.max))
                chain.link(dve.tensor_tensor(eq, gs, bc(gm[:, 0, :], 2, NG), ALU.is_equal))
                chain.link(dve.tensor_tensor(eq, eq, bc(cn("down"), 1, NT), ALU.mult))
                chain.link(dve.tensor_reduce(gm[:, 1, :], eq, AX.X, ALU.max))
                chain.link(dve.tensor_tensor(eq, eq, bc(gm[:, 1, :], 2, NG), ALU.is_equal))
                rk = flat(rank[:, :, :])
                gv = flat(gt[:, :, :])
                chain.link(dve.tensor_copy(rk, bc(cn("place"), 1, NT * NG)))
                for s in range(1, EPG):
                    chain.link(dve.tensor_tensor(gv[:, :, 0:EPG - s], sv[:, :, s:], sv[:, :, 0:EPG - s], ALU.is_gt))
                    chain.link(dve.tensor_tensor(rk[:, :, 0:EPG - s], rk[:, :, 0:EPG - s], gv[:, :, 0:EPG - s], ALU.add))
                    chain.link(dve.tensor_tensor(rk[:, :, s:], rk[:, :, s:], gv[:, :, 0:EPG - s], ALU.subtract))
                for k in range(2):
                    chain.add(dve.scalar_tensor_tensor(flat(onek[:, k, :, :]), rk, float(k), bc(g3[:, 1, :], 2, EPG),
                                                       ALU.is_equal, ALU.mult))
                chain.wait()
                dve.tensor_tensor(mask[:, :, :], onek[:, 0, :, :], onek[:, 1, :, :], ALU.add).then_inc(mask_done, 1)
                for k in range(2):
                    chain.link(dve.tensor_tensor(prod[:, :, :], onek[:, k, :, :], sco[:, :, :], ALU.mult))
                    chain.link(dve.tensor_reduce(sk[:, k, :], prod[:, :, :], AX.X, ALU.add))
                chain.link(dve.tensor_tensor(sk[:, 2, :], sk[:, 0, :], sk[:, 1, :], ALU.add))
                chain.link(dve.reciprocal(sk[:, 3, :], sk[:, 2, :]))
                for k in range(2):
                    chain.add(dve.tensor_copy(pay[:, :, k, 0], cn("token")))
                    chain.add(dve.tensor_scalar(pay[:, :, k, 1], cn("token"), float(2 * k * SEQ), None, ALU.add))
                    chain.add(dve.tensor_scalar(pay[:, :, k, 3], cn("token"), float((2 * k + 1) * SEQ), None, ALU.add))
                    chain.add(dve.tensor_tensor(pay[:, :, k, 2].bitcast(F32), sk[:, k, :], sk[:, 3, :], ALU.mult))
                dve.wait_ge(pos_done, 1)
                chain.add(dve.tensor_copy(pos[:, :, :], cp[:, 0:NT * NE].rearrange("p (t e) -> p t e", t=NT)))
                chain.add(dve.tensor_copy(ce[:, 0, :], cp[:, NT * NE:(NT + 1) * NE]))
                chain.add(dve.memset(ce[:, 1, :], 0.0))
                chain.add(dve.memset(ce[:, 4, :], 1.0))
                chain.link(dve.memset(gt[:, :, :], 0.0))
                for b in range(1, SEQ // SLOTS):
                    chain.add(dve.scalar_tensor_tensor(ce[:, 1, :], ce[:, 0, :], float(b * SLOTS), ce[:, 1, :], ALU.is_gt, ALU.add))
                    chain.link(dve.scalar_tensor_tensor(gt[:, :, :], pos[:, :, :], float(b * SLOTS), gt[:, :, :], ALU.is_ge, ALU.add))
                chain.link(dve.tensor_tensor_scan(ce[:, 2, :], ce[:, 4, :], ce[:, 1, :], 0.0, ALU.mult, ALU.add))
                chain.link(dve.tensor_tensor(ce[:, 3, :], ce[:, 2, :], ce[:, 1, :], ALU.subtract))
                chain.add(dve.tensor_tensor(eo[:, :, :], bc(ce[0:1, 2, :], 1, OVER), bc(cn("expert", 1)[:, 0:OVER], 2, NE), ALU.is_le))
                chain.link(dve.scalar_tensor_tensor(pos[:, :, :], gt[:, :, :], -float(SLOTS), pos[:, :, :], ALU.mult, ALU.add))
                chain.link(dve.tensor_reduce(eov[:, 1:1 + OVER], eo[:, :, :], AX.X, ALU.add))
                chain.link(dve.tensor_scalar(eov[:, 1:1 + OVER], eov[:, 1:1 + OVER], float(NE - 1), None, ALU.min))
                chain.link(dve.tensor_copy(eov[:, 0:1], ce[0:1, 2, NE - 1:NE]))
                chain.add(dve.tensor_copy(flag[:, :], eov[:, :]))
                chain.link(dve.scalar_tensor_tensor(dest[:, :, :], pos[:, :, :], float(NE), bc(cn("expert"), 1, NT), ALU.mult, ALU.add))
                chain.link(dve.scalar_tensor_tensor(alt[:, :, :], pos[:, :, :], float(OVER), gt[:, :, :], ALU.mult, ALU.add))
                chain.link(dve.tensor_tensor(alt[:, :, :], alt[:, :, :], bc(ce[:, 3, :], 1, NT), ALU.add))
                chain.link(dve.scalar_tensor_tensor(alt[:, :, :], alt[:, :, :], float(SLOTS * NE - 1), dest[:, :, :], ALU.add, ALU.subtract))
                chain.link(dve.scalar_tensor_tensor(alt[:, :, :], gt[:, :, :], 1.0, alt[:, :, :], ALU.min, ALU.mult))
                chain.link(dve.tensor_tensor(dest[:, :, :], dest[:, :, :], alt[:, :, :], ALU.add))
                for k in range(2):
                    chain.link(dve.tensor_tensor(prod[:, :, :], onek[:, k, :, :], dest[:, :, :], ALU.mult))
                    chain.link(dve.tensor_reduce(dk[:, k, :], prod[:, :, :], AX.X, ALU.add))
                dve.tensor_copy(dki[:, :, :], dk[:, :, :]).then_inc(pay_done, 1)
                dve.memset(rows_all[:, NE + OVER, :], FAR)
                dve.wait_ge(tab_in, 64)
                dve.tensor_copy(rows_all[SLOTS:, 0:NE + OVER, 1], rows_all[SLOTS:, 0:NE + OVER, 3]).then_inc(rows_done, 1)

            @block.gpsimd
            def _(pool):
                v["zero_last"](pool)
                for t in range(NT):
                    pool.wait_ge(gmul_ready, t + 1)
                    pool.wait_ge(ln_in, 32)
                    pool.tensor_tensor(h2[:, t, :], h2[:, t, :], lnb[:, :], ALU.add).then_inc(h2_ready, 1)
                pool.wait_ge(pay_done, 1)
                pool.wait_ge(far_out, 16)
                for t in range(NT):
                    for k in range(2):
                        pool.indirect_dma_start(v["slots_dram"], bass.IndirectOffsetOnAxis(ap=dki[:, k, t:t + 1], axis=0),
                                                pay[:, t, k, :], None, bounds_check=TABLE - 1, oob_is_err=False).then_inc(scattered, 16)
                pool.wait_ge(scattered, 16 * 2 * NT)


def experts(nc, sem, sb, pb, cn, v):
    rows_all, flag = v["rows_all"], v["flag"]
    w1, w3, w2 = (v[k] for k in ("moe_w1", "moe_w3", "moe_w2"))
    ident = v["ident"]
    w_dram = [w1.rearrange("e (p k) n -> e p (k n)", p=P), w3.rearrange("e (p k) n -> e p (k n)", p=P),
              w2.rearrange("e (p k) n -> e p (k n)", p=P)]
    WC = KT * FE
    HALF = WC // 2
    FT = FE // P
    UNITS = 6
    NRAW, NSPLIT = 6, 4
    st = ExitStack()
    with st:
        raw = sb(st, "wraw", [P, NRAW, HALF])
        whi, wlo = sb(st, "whi", [P, NSPLIT, HALF], F32R), sb(st, "wlo", [P, NSPLIT, HALF], F32R)
        xg = sb(st, "xg", [SLOTS, 2, DM])
        tok = sb(st, "tok", [SLOTS, 2, 1], I32)
        idx = sb(st, "idx", [P, 2, 1], I32)
        gate = sb(st, "gate", [P, 2, 1])
        xs = sb(st, "xs", [P, 2, KT, 2, SLOTS], F32R)
        hc = sb(st, "hc", [P, 2, FE])
        sl = sb(st, "sl", [P, FT * SLOTS])
        prd = sb(st, "prd", [P, FT * SLOTS])
        ac = sb(st, "ac", [P, FT, 2, SLOTS], F32R)
        ys = sb(st, "ys", [P, 2, DM])
        tx, gb = pb(st, "tx"), pb(st, "gb")
        hb = [pb(st, f"hb{i}") for i in range(4)]
        yb = [pb(st, f"yb{i}") for i in range(2)]

        class Signals:

            def __init__(self, tag):
                self.w_in = [sem(f"{tag}_w_in{i}") for i in range(6)]
                self.gathered = [sem(f"{tag}_gathered{i}") for i in range(2)]
                self.hi_done = sem(f"{tag}_hi_done")
                self.lo_done = sem(f"{tag}_lo_done")
                self.part_used = sem(f"{tag}_part_used")
                self.gate_ready = sem(f"{tag}_gate_ready")
                self.row_ready = sem(f"{tag}_row_ready")
                self.index_ready = sem(f"{tag}_index_ready")
                self.x_turned = sem(f"{tag}_x_turned")
                self.xhi_done = sem(f"{tag}_xhi_done")
                self.xlo_done = sem(f"{tag}_xlo_done")
                self.h_copied = sem(f"{tag}_h_copied")
                self.paired = sem(f"{tag}_paired")
                self.silu_done = sem(f"{tag}_silu_done")
                self.act_done = sem(f"{tag}_act_done")
                self.ahi_done = sem(f"{tag}_ahi_done")
                self.alo_done = sem(f"{tag}_alo_done")
                self.y_ready = sem(f"{tag}_y_ready")
                self.scattered = sem(f"{tag}_scattered")
                self.stored = sem(f"{tag}_stored")
                self.steps_begun = sem(f"{tag}_steps_begun")
                self.turns_begun = sem(f"{tag}_turns_begun")

        def wait(eng, s, value):
            if not (isinstance(value, int) and value <= 0):
                eng.wait_ge(s, value)

        def blocks(eng, count, step):
            for e in range(2):
                step(e, e, 0)
            with eng.Fori(1, count // 2) as it:
                for j in range(2):
                    step(it * 2 + j, j, it)

        W1, W2, W3 = (0, 1), (2, 3), (4, 5)

        def sync_program(sp, S, count, expert):
            def load(e, u, which, ex, half):
                wait(sp, S.lo_done, e * UNITS + (u + 1 - NRAW))
                sp.dma_start(raw[:, u, :], w_dram[which][bass.ds(ex, 1), :, half * HALF:(half + 1) * HALF].rearrange("o p n -> (o p) n"))\
                    .then_inc(S.w_in[u], 16)

            def step(e, j, it):
                ex = expert(sp, e)
                before = ex if isinstance(e, int) and e == 0 else expert(sp, e - 1)
                for half in range(2):
                    load(e, W1[half], 0, ex, half)
                for half in range(2):
                    load(e, W2[half], 2, before, half)
                for half in range(2):
                    load(e, W3[half], 1, ex, half)
            blocks(sp, count, step)
            last = expert(sp, count - 1)
            for half in range(2):
                load(count, half, 2, last, half)

        def pool_program(pool, S, count, first):
            def fetch(e, j):
                wait(pool, S.x_turned, e - 1)
                pool.tensor_copy(tok[:, j, :], rows_all[0:SLOTS, bass.ds(e + first, 1), 0:1].rearrange("p o w -> p (o w)")).then_inc(S.index_ready, 1)
                wait(pool, S.index_ready, e + 1)
                pool.sem_inc(S.steps_begun, 1)
                pool.indirect_dma_start(xg[:, j, :], None, v["h2_dram"], bass.IndirectOffsetOnAxis(ap=tok[:, j, :], axis=0),
                                        bounds_check=SEQ - 1, oob_is_err=False).then_inc(S.gathered[j], 16)

            def store(e, j):
                pool.tensor_copy(gate[:, j, :], rows_all[:, bass.ds(e + first, 1), 2:3].bitcast(F32).rearrange("p o w -> p (o w)"))\
                    .then_inc(S.gate_ready, 1)
                pool.tensor_copy(idx[:, j, :], rows_all[:, bass.ds(e + first, 1), 1:2].rearrange("p o w -> p (o w)")).then_inc(S.row_ready, 1)
                wait(pool, S.row_ready, e + 1)
                pool.wait_ge(S.y_ready, e * 2 + 2)
                pool.sem_inc(S.steps_begun, 1)
                pool.indirect_dma_start(v["y_dram"], bass.IndirectOffsetOnAxis(ap=idx[:, j, :], axis=0),
                                        ys[:, j, :], None, bounds_check=4 * SEQ - 1, oob_is_err=False).then_inc(S.scattered, 16)
                pool.wait_ge(S.scattered, e * 16 + 16)
                pool.sem_inc(S.stored, 1)

            def step(e, j, it):
                fetch(e + 1, 1 - j)
                if not (isinstance(e, int) and e == 0):
                    store(e - 1, 1 - j)
            fetch(0, 0)
            blocks(pool, count, step)
            store(count - 1, 1)
            pool.wait_ge(S.gathered[0], 16 * (count // 2 + 1))

        def tensor_program(pe, S, count):
            def turn(e, j, round_):
                wait(pe, S.xlo_done, e)
                pe.wait_ge(S.gathered[j], round_ * 16 + 16)
                pe.sem_inc(S.turns_begun, 1)
                for k in range(KT):
                    last = pe.transpose(tx[:, k * SLOTS:(k + 1) * SLOTS], xg[:, j, k::KT], ident[0:SLOTS, 0:SLOTS])
                last.then_inc(S.x_turned, 1)

            def first_products(e, j, u, w, half):
                part = (UNITS * j + u) % NSPLIT
                bank = hb[2 * j + w]
                pe.wait_ge(S.lo_done, e * UNITS + (u + 1))
                for kk in range(4):
                    lhs = xs[:, j, 4 * half + kk, :, :].rearrange("p a s -> p (a s)")
                    cols = slice(kk * FE, (kk + 1) * FE)
                    pe.matmul(bank[:, :], lhs, whi[:, part, cols], start=(half == 0 and kk == 0), stop=False)
                    last = pe.matmul(bank[:, :], lhs, wlo[:, part, cols], start=False, stop=(half == 1 and kk == 3))
                last.then_inc(S.part_used, 1)

            def add_pairs(e):
                for w in range(2):
                    pe.wait_ge(S.h_copied, e * 2 + (w + 1))
                    for f in range(FT):
                        last = pe.matmul(gb[:, (w * FT + f) * SLOTS:(w * FT + f + 1) * SLOTS], hc[:, w, f::FT], cn("pair"),
                                         start=True, stop=True)
                last.then_inc(S.paired, 1)

            def second_products(e, body, bj, u, half):
                part = (UNITS * bj + u) % NSPLIT
                pe.wait_ge(S.alo_done, e + 1)
                wait(pe, S.y_ready, e * 2)
                pe.wait_ge(S.lo_done, body * UNITS + (u + 1))
                for kk in range(2):
                    k = 2 * half + kk
                    lhs = ac[:, k, :, :].rearrange("p a s -> p (a s)")
                    for c in range(2):
                        cols = slice(kk * DM + c * 512, kk * DM + c * 512 + 512)
                        pe.matmul(yb[c][:, :], lhs, whi[:, part, cols], start=(k == 0), stop=False)
                        last = pe.matmul(yb[c][:, :], lhs, wlo[:, part, cols], start=False, stop=(k == FT - 1))
                last.then_inc(S.part_used, 1)

            def step(e, j, it):
                head = isinstance(e, int) and e == 0
                pe.wait_ge(S.xlo_done, e + 1)
                first_products(e, j, W1[0], 0, 0)
                if not head:
                    add_pairs(e - 1)
                first_products(e, j, W1[1], 0, 1)
                for half in range(2):
                    if head:
                        pe.wait_ge(S.lo_done, W2[half] + 1)
                        pe.wait_ge(S.part_used, W2[half])
                        pe.sem_inc(S.part_used, 1)
                    else:
                        second_products(e - 1, e, j, W2[half], half)
                first_products(e, j, W3[0], 1, 0)
                turn(e + 1, 1 - j, it + j)
                first_products(e, j, W3[1], 1, 1)
            turn(0, 0, 0)
            blocks(pe, count, step)
            add_pairs(count - 1)
            for half in range(2):
                second_products(count - 1, count, 0, half, half)

        def scalar_program(act, S, count):
            def high(e, j, u):
                act.wait_ge(S.w_in[u], e * 16 + 16)
                wait(act, S.part_used, e * UNITS + (u + 1 - NSPLIT))
                act.activation(whi[:, (UNITS * j + u) % NSPLIT, :], raw[:, u, :], ACT.Copy).then_inc(S.hi_done, 1)

            def x_high(e, j):
                act.wait_ge(S.x_turned, e + 1)
                wait(act, S.part_used, e * UNITS - UNITS)
                act.activation(xs[:, j, :, 0, :], tx[:, :].rearrange("p (k s) -> p k s", k=KT), ACT.Copy).then_inc(S.xhi_done, 1)

            def copy_h(e, j, w):
                act.wait_ge(S.part_used, e * UNITS + ((W1, W3)[w][1] + 1))
                act.activation(hc[:, w, :], hb[2 * j + w][:, :], ACT.Copy).then_inc(S.h_copied, 1)

            def gated(e):
                act.wait_ge(S.paired, e + 1)
                act.activation(sl[:, :], gb[:, 0:FT * SLOTS], ACT.Silu).then_inc(S.silu_done, 1)

            def act_high(e):
                act.wait_ge(S.act_done, e + 1)
                wait(act, S.part_used, e * UNITS + (W2[1] + 1))
                act.activation(ac[:, :, 0, :], prd[:, :].rearrange("p (f s) -> p f s", f=FT), ACT.Copy).then_inc(S.ahi_done, 1)

            def weigh_y(e, j, used):
                act.wait_ge(S.part_used, used)
                wait(act, S.stored, e - 1)
                act.wait_ge(S.gate_ready, e + 1)
                for half in range(2):
                    act.activation(ys[:, j, half * 512:half * 512 + 512], yb[half][:, :], ACT.Copy, scale=gate[:, j, 0:1])\
                        .then_inc(S.y_ready, 1)

            def step(e, j, it):
                head = isinstance(e, int) and e == 0
                for u in range(3):
                    high(e, j, u)
                if not head:
                    copy_h(e - 1, 1 - j, 1)
                high(e, j, 3)
                if not head:
                    gated(e - 1)
                    act_high(e - 1)
                high(e, j, 4)
                copy_h(e, j, 0)
                high(e, j, 5)
                if not head:
                    weigh_y(e - 1, 1 - j, e * UNITS + (W2[1] + 1))
                x_high(e + 1, 1 - j)
            x_high(0, 0)
            blocks(act, count, step)
            high(count, 0, 0)
            high(count, 0, 1)
            copy_h(count - 1, 1, 1)
            gated(count - 1)
            act_high(count - 1)
            weigh_y(count - 1, 1, count * UNITS + 2)

        def vector_program(dve, S, count):
            def low(e, j, u):
                part = (UNITS * j + u) % NSPLIT
                dve.wait_ge(S.hi_done, e * UNITS + (u + 1))
                dve.tensor_tensor(wlo[:, part, :], raw[:, u, :], whi[:, part, :].bitcast(F32), ALU.subtract).then_inc(S.lo_done, 1)

            def x_low(e, j):
                dve.wait_ge(S.xhi_done, e + 1)
                dve.tensor_tensor(xs[:, j, :, 1, :], tx[:, :].rearrange("p (k s) -> p k s", k=KT),
                                  xs[:, j, :, 0, :].bitcast(F32), ALU.subtract).then_inc(S.xlo_done, 1)

            def product(e):
                dve.wait_ge(S.silu_done, e + 1)
                dve.tensor_tensor(prd[:, :], sl[:, :], gb[:, FT * SLOTS:2 * FT * SLOTS], ALU.mult).then_inc(S.act_done, 1)
                dve.wait_ge(S.ahi_done, e + 1)
                dve.tensor_tensor(ac[:, :, 1, :], prd[:, :].rearrange("p (f s) -> p f s", f=FT),
                                  ac[:, :, 0, :].bitcast(F32), ALU.subtract).then_inc(S.alo_done, 1)

            def step(e, j, it):
                for u in range(4):
                    low(e, j, u)
                if not (isinstance(e, int) and e == 0):
                    product(e - 1)
                low(e, j, 4)
                low(e, j, 5)
                x_low(e + 1, 1 - j)
            x_low(0, 0)
            blocks(dve, count, step)
            low(count, 0, 0)
            low(count, 0, 1)
            product(count - 1)

        zeroed = sem("moe_zeroed")
        first_blocks, more_blocks = Signals("moe"), Signals("over")
        with nc.Block() as block:
            S = first_blocks

            @block.sync
            def _(sp):
                sync_program(sp, S, NE, lambda eng, e: e)

            @block.gpsimd
            def _(pool):
                v["zero_last"](pool)
                pool.memset(xg[:, :, :], 0.0).then_inc(zeroed, 1)
                pool.wait_ge(zeroed, 1)
                pool_program(pool, S, NE, 0)

            @block.tensor
            def _(pe):
                tensor_program(pe, S, NE)

            @block.scalar
            def _(act):
                scalar_program(act, S, NE)

            @block.vector
            def _(dve):
                vector_program(dve, S, NE)

        def any_more(eng):
            return eng.value_load(flag[0:1, 0:1], min_val=0, max_val=OVER) > 0

        with nc.Block() as block:
            S2 = more_blocks

            @block.sync
            def _(sp):
                with sp.If(any_more(sp)):
                    sync_program(sp, S2, OVER, lambda eng, e: eng.value_load(flag[0:1, bass.ds(e + 1, 1)], min_val=0, max_val=NE - 1))

            @block.gpsimd
            def _(pool):
                with pool.If(any_more(pool)):
                    pool_program(pool, S2, OVER, NE)

            @block.tensor
            def _(pe):
                with pe.If(any_more(pe)):
                    tensor_program(pe, S2, OVER)

            @block.scalar
            def _(act):
                with act.If(any_more(act)):
                    scalar_program(act, S2, OVER)

            @block.vector
            def _(dve):
                with dve.If(any_more(dve)):
                    vector_program(dve, S2, OVER)


def final(nc, sem, sb, pb, cn, v):
    h2, epsc = v["h2"], v["epsc"]
    st = ExitStack()
    with st:
        yr = sb(st, "yr", [P, NT, 4, DM])
        lng, lnb = sb(st, "lng3", [P, DM]), sb(st, "lnb3", [P, DM])
        stats, mv, rstd, nmr = sb(st, "stats3", [P, NT, 2, 6]), sb(st, "mv3", [P, NT, 2]), sb(st, "rstd3", [P, NT]), sb(st, "nmr3", [P, NT])
        y_in = [sem(f"y_in{t}") for t in range(NT)]
        ln_in, summed, out_done = sem("ln3_in"), sem("fin_summed"), sem("out_done")
        stats_ready, std_ready, scale_ready, norm_ready, gmul_ready, o_ready = (
            sem(f"ln3_{n}") for n in ("stats", "std", "scale", "norm", "gmul", "o"))
        dve_chain = sem("fin_dve_chain")
        with nc.Block() as block:
            @block.sync
            def _(sp):
                for t in range(NT):
                    sp.dma_start(yr[:, t, :, :], v["y_dram"].rearrange("(q s) d -> s q d", q=4)[t * P:(t + 1) * P, :, :]).then_inc(y_in[t], 16)
                    if t == 0:
                        sp.dma_start(lng[:, :], v["ln_ffn_g"].to_broadcast([P, DM])).then_inc(ln_in, 16)
                        sp.dma_start(lnb[:, :], v["ln_ffn_b"].to_broadcast([P, DM])).then_inc(ln_in, 16)
                for t in range(NT):
                    sp.wait_ge(o_ready, t + 1)
                    sp.dma_start(v["out"][t * P:(t + 1) * P, :], h2[:, t, :]).then_inc(out_done, 16)
                sp.wait_ge(out_done, 16 * NT)

            @block.scalar
            def _(act):
                layer_norm_act(act, h2, mv, rstd, nmr, epsc[:, 0:1], stats_ready, std_ready, scale_ready, norm_ready)

            @block.vector
            def _(dve):
                chain = Chain(dve, dve_chain)

                def x_ready(t):
                    if t == 0:
                        dve.wait_ge(ln_in, 32)
                    dve.wait_ge(y_in[t], 16)
                    r = h2[:, t, :]
                    chain.link(dve.scalar_tensor_tensor(r, r, ALPHA, yr[:, t, 0, :], ALU.mult, ALU.add))
                    for q in range(1, 4):
                        chain.link(dve.tensor_tensor(r, r, yr[:, t, q, :], ALU.add))
                layer_norm_dve(dve, chain, h2, stats, mv, rstd, nmr, x_ready, stats_ready, std_ready, scale_ready,
                               norm_ready, gmul_ready, lng[:, :])

            @block.gpsimd
            def _(pool):
                v["zero_last"](pool)
                for t in range(NT):
                    pool.wait_ge(gmul_ready, t + 1)
                    pool.tensor_tensor(h2[:, t, :], h2[:, t, :], lnb[:, :], ALU.add).then_inc(o_ready, 1)


def kernel(**inputs):
    import numpy as _np
    import concourse.bacc as _bacc
    from concourse import mybir as _mybir
    from concourse.bass_utils import run_bass_kernel_spmd as _run

    a = {k: _np.asarray(v) for k, v in inputs.items()}
    rows = lambda t: _np.broadcast_to(_np.reshape(t, (1, -1)), (P, t.size))
    by_part = lambda t: _np.reshape(t, (P, -1))
    column = lambda t: _np.reshape(t, (-1, P)).T
    w_in = a["w_in"][0]
    gate_cols = _np.concatenate([w_in[:, C_A:C_A + 16], w_in[:, C_I:C_I + 16]], axis=1)
    small = _np.concatenate([
        _np.reshape(_np.transpose(_np.reshape(a["dn_conv_w"][0], (TAPS, 12, P)), (2, 1, 0)), (P, 60)),
        column(a["dn_norm_w"][0]), column(a["pool_scale"][0]), column(a["ml_norm_w"][0]),
        by_part(gate_cols), rows(a["dn_a_log"][0]), rows(a["dn_dt_bias"][0]), rows(a["ml_gate_b"][0]),
        rows(a["router_b"]), by_part(a["router_w"])], axis=1)
    arrays = {
        "x": a["x"][0], "ln_in_g": a["ln_in_g"][None], "ln_in_b": a["ln_in_b"][None], "w_in": w_in,
        "pool_w": a["pool_w"][0], "w_branch": a["w_branch"][0], "w_out": a["w_out"][0],
        "ln_mix_g": a["ln_mix_g"], "ln_mix_b": a["ln_mix_b"], "moe_w1": a["moe_w1"][0], "moe_w3": a["moe_w3"][0],
        "moe_w2": a["moe_w2"][0], "ln_ffn_g": a["ln_ffn_g"], "ln_ffn_b": a["ln_ffn_b"],
        "const": _np.concatenate(list(CONST.values()), axis=1), "small": small,
    }
    nc = _bacc.Bacc("TRN2", target_bir_lowering=False, num_devices=1)
    feed, args = {}, []
    for name, t in arrays.items():
        if name.startswith("ln_") and t.ndim == 1:
            t = t[None]
        t = _np.ascontiguousarray(t)
        feed[f"in_{name}"] = t
        args.append(nc.dram_tensor(f"in_{name}", t.shape, _mybir.dt.from_np(t.dtype), kind="ExternalInput").ap())
    args.append(nc.dram_tensor("result", (SEQ, DM), _mybir.dt.float32, kind="ExternalOutput").ap())
    hybrid_encoder(nc, *args)
    r = _run(nc, [feed], core_ids=[0])
    return _np.reshape(r.results[0]["result"], (1, SEQ, DM))
```

```python
import concourse.bass as bass
from concourse import mybir
from concourse.alu_op_type import AluOpType as ALU
from contextlib import ExitStack
import numpy as np

F32 = mybir.dt.float32
F32R = mybir.dt.float32r
I32 = mybir.dt.int32
ACT = mybir.ActivationFunctionType
AX = mybir.AxisListType

P = 128
SEQ, DM = 512, 1024
NT = SEQ // P
KT = DM // P
MW = DM // 2
NH = 4
DV = MW // NH
QK = DV // 2
TAPS = 5
LN_EPS, NORM_EPS = 1e-5, 1e-6
ALPHA = 2.0 ** 0.25
NE, NG = 32, 8
EPG = NE // NG
FE = DM // 2
SLOTS = 64
WC = KT * FE
HALF = WC // 2
NRAW, NSPLIT = 6, 4
OVER = (2 * SEQ) // SLOTS
TABLE = SLOTS * (NE + OVER)
FAR = 1 << 20
NEG = -1.0e30

OFF = np.cumsum([0, 3 * MW, MW, 2 * NH, 2 * NH, MW, NH * QK, NH * QK, MW, MW, 2 * NH, 2 * NH, 3 * DM])
C_Q, C_K, C_V, C_Z, C_A, C_U, C_MQ, C_MV, C_MO, C_I, C_G = (
    0, MW, 2 * MW, int(OFF[1]), int(OFF[2]), int(OFF[4]), int(OFF[5]), int(OFF[7]), int(OFF[8]), int(OFF[9]), int(OFF[11]))
LEVELS = [1, 2, 4, 8, 16, 32, 64]
NL = len(LEVELS)


def constants():
    i = np.arange(P)[None, :]
    j = np.arange(P)[:, None]
    upto, after = (j <= i), (j >= i)
    cols = {"ident": np.eye(P), "ones": np.ones((P, P)), "upto": upto, "after": after,
            "neg_fwd": np.where(upto, 0.0, NEG), "neg_bwd": np.where(after, 0.0, NEG),
            "before": j < i}
    for d in range(2):
        for b in LEVELS:
            same = (i // (2 * b)) == (j // (2 * b))
            first_j, first_i = (j // b) % 2 == 0, (i // b) % 2 == 0
            cols[f"level{d}_{b}"] = same & (first_j & ~first_i if d == 0 else first_i & ~first_j)
    edge = np.zeros((P, 4, 16))
    for g, win in enumerate((2, 4, 8, 16)):
        half = win // 2
        for n in range(8):
            edge[:, g, n] = 1.0 / (min(n + half, SEQ) - max(n - half, 0))
            m = SEQ - 8 + n
            edge[:, g, 8 + n] = 1.0 / (min(m + half, SEQ) - max(m - half, 0))
    cols["edge"] = edge.reshape(P, 64)
    sel = np.zeros((P, NH, P))
    for h in range(NH):
        sel[h, h, :] = 1.0
    cols["sel"] = sel.reshape(P, NH * P)
    cols["pair"] = (i[:, 0:SLOTS] == j % SLOTS)
    cols["down"] = np.tile(np.arange(NG, 0, -1.0), (P, 1))
    cols["place"] = np.tile(np.arange(4.0), (P, 1))
    cols["expert"] = np.tile(np.arange(32.0), (P, 1))
    cols["token"] = np.arange(NT)[None, :] * P + j
    return {k: np.asarray(v, np.float32) for k, v in cols.items()}


CONST = constants()
COFF, NCONST = {}, 0
for _key, _table in CONST.items():
    COFF[_key] = (NCONST, _table.shape[1])
    NCONST += _table.shape[1]


class Chain:

    def __init__(self, eng, sem):
        self.eng, self.sem, self.n, self.base = eng, sem, 0, 0

    def add(self, ins):
        self.n += 1
        ins.then_inc(self.sem, 1)
        return ins

    def wait(self):
        self.eng.wait_ge(self.sem, self.base + self.n)

    def link(self, ins):
        self.add(ins)
        self.wait()


def bc(ap, dim, n):
    v = ap.unsqueeze(dim)
    shape = list(v.shape)
    shape[dim] = n
    return v.to_broadcast(shape)


SM_CONV, SM_NORM, SM_W, SM_BIAS, SM_RB, SM_RW = 0, 60, 72, 328, 360, 392
SM_COLS = 392 + KT * NE


def hybrid_encoder(nc, x, ln_in_g, ln_in_b, w_in, pool_w, w_branch, w_out, ln_mix_g, ln_mix_b,
                   moe_w1, moe_w3, moe_w2, ln_ffn_g, ln_ffn_b, const, small, out):
    root = ExitStack()
    stages = [[]]

    def sem(name):
        stages[-1].append(nc.alloc_semaphore(name))
        return stages[-1][-1]

    def zero_last(pool):
        if len(stages) > 1:
            numbers = sorted(s.num for s in stages[-2])
            while numbers:
                n = 1
                while n < len(numbers) and numbers[n] == numbers[0] + n:
                    n += 1
                pool.sem_clear(range(numbers[0], numbers[0] + n))
                numbers = numbers[n:]

    def next_stage():
        if len(stages) > 1:
            for s in stages[-2]:
                nc.release_semaphore(s)
        stages.append([])

    h2_dram = nc.dram_tensor("h2_dram", (SEQ, DM), F32, kind="Internal").ap()
    h_dram = nc.dram_tensor("h_dram", (SEQ, DM), F32, kind="Internal").ap()
    kept_dram = nc.dram_tensor("kept_dram", (2, KT, P, SEQ), F32, kind="Internal").ap()
    slots_dram = nc.dram_tensor("slots_dram", (TABLE, 4), I32, kind="Internal").ap()
    y_dram = nc.dram_tensor("y_dram", (2 * SEQ, DM), F32, kind="Internal").ap()
    with root:
        def sb(stack, name, shape, dt=F32):
            return stack.enter_context(nc.sbuf_tensor(name, shape, dt))

        def pb(stack, name, shape=(P, 512), dt=F32):
            return stack.enter_context(nc.psum_tensor(name, list(shape), dt))

        cst = sb(root, "cst", [P, NCONST])
        sml = sb(root, "sml", [P, SM_COLS])
        epsc = sb(root, "epsc", [P, 4])

        def cn(name, rows=P):
            a, n = COFF[name]
            return cst[0:rows, a:a + n]

        ident, ones = cn("ident"), cn("ones")
        h2 = sb(root, "h2", [P, NT, DM])
        rows_all = sb(root, "rows_all", [P, NE + OVER + 1, 4], I32)
        flag = sb(root, "flag", [1, 1 + OVER], I32)
        wraw = sb(root, "wraw", [P, NRAW, HALF])
        mixer = ExitStack()
        hT = sb(mixer, "hT", [P, KT, SEQ])
        yT = sb(mixer, "yT", [P, 3, NH, SEQ])
        attention = ExitStack()
        qkT = sb(attention, "qkT", [P, 2, NH, SEQ])
        kTok = sb(attention, "kTok", [P, NT, NH, DV])
        vTok = sb(attention, "vTok", [P, NT, NH, DV])
        beta = sb(attention, "beta", [P, NT, 8])
        cum = sb(attention, "cum", [P, NT, 24])
        gg = sb(attention, "gg", [P, NT, 24])
        mstack = ExitStack()
        mq = sb(mstack, "mq", [P, 4, SEQ])
        mvx = sb(mstack, "mvx", [P, NT, NH, DV + 1])
        mrow = sb(mstack, "mrow", [4, 2, SEQ])
        acol = sb(mstack, "acol", [P, NT, 8])
        emx = sb(mstack, "emx", [P, NT, 8])

        rooms = h2[:, :, :].rearrange("p a b -> p (a b)")
        gw = [rooms[:, KT * P * i:KT * P * (i + 1)].rearrange("p (k n) -> p k n", k=KT) for i in range(3)]
        bw = [rooms[:, 3 * KT * P + NH * P * i:3 * KT * P + NH * P * (i + 1)].rearrange("p (k n) -> p k n", k=NH) for i in range(2)]
        w_rows = w_in.rearrange("(p k) n -> p k n", k=KT)

        front(nc, sem, sb, pb, cn, locals())
        next_stage()
        mlstm(nc, sem, sb, pb, cn, locals())
        next_stage()
        mstack.close()
        deltanet(nc, sem, sb, pb, cn, locals())
        next_stage()
        attention.close()
        merge(nc, sem, sb, pb, cn, locals())
        next_stage()
        mixer.close()
        experts(nc, sem, sb, pb, cn, locals())
        next_stage()
        final(nc, sem, sb, pb, cn, locals())


def layer_norm_dve(dve, chain, src, stats, mv, rstd, nmr, x_ready, stats_ready, std_ready, scale_ready,
                   norm_ready, gmul_ready, g, ln_in, lag):
    for step in range(NT + lag):
        t = step
        if t < NT:
            x_ready(t)
            for half in range(2):
                chain.add(dve.bn_stats(stats[:, t, half, :], src[:, t, 512 * half:512 * half + 512]))
            chain.wait()
            dve.bn_aggr(mv[:, t, :], stats[:, t, :, :]).then_inc(stats_ready, 1)
            dve.wait_ge(std_ready, t + 1)
            chain.link(dve.reciprocal(rstd[:, t:t + 1], rstd[:, t:t + 1]))
            dve.wait_ge(stats_ready, t + 1)
            dve.tensor_scalar(nmr[:, t:t + 1], mv[:, t, 0:1], rstd[:, t:t + 1], -1.0, ALU.mult, ALU.mult).then_inc(scale_ready, 1)
        t = step - lag
        if t >= 0:
            if t == 0:
                dve.wait_ge(ln_in, 32)
            dve.wait_ge(norm_ready, t + 1)
            dve.tensor_tensor(src[:, t, :], src[:, t, :], g, ALU.mult).then_inc(gmul_ready, 1)


def layer_norm_act(act, src, mv, rstd, nmr, eps, stats_ready, std_ready, scale_ready, norm_ready, between=None):
    for t in range(NT):
        if between is not None:
            between(t)
        act.wait_ge(stats_ready, t + 1)
        act.activation(rstd[:, t:t + 1], mv[:, t, 1:2], ACT.Sqrt, bias=eps).then_inc(std_ready, 1)
        act.wait_ge(scale_ready, t + 1)
        act.activation(src[:, t, :], src[:, t, :], ACT.Identity, scale=rstd[:, t:t + 1],
                       bias=nmr[:, t:t + 1]).then_inc(norm_ready, 1)


def front(nc, sem, sb, pb, cn, v):
    x, w_in, small, const = v["x"], v["w_in"], v["small"], v["const"]
    cst, sml, epsc, hT, yT, qkT = (v[k] for k in ("cst", "sml", "epsc", "hT", "yT", "qkT"))
    kTok, vTok, beta, cum, gg, mq, mvx, mrow, acol, emx = (
        v[k] for k in ("kTok", "vTok", "beta", "cum", "gg", "mq", "mvx", "mrow", "acol", "emx"))
    ident, ones = v["ident"], v["ones"]
    st = ExitStack()
    with st:
        h = v["h2"]
        ring = v["wraw"][:, 0:4, :].rearrange("p (r a) (b n) -> p r (a b) n", r=2, n=512)
        spare = v["wraw"][:, 4:6, :].rearrange("p a (b n) -> p (a b) n", n=DM)
        lng, lnb = sb(st, "lng", [P, DM]), sb(st, "lnb", [P, DM])
        stats, mv, rstd, nmr = sb(st, "stats", [P, NT, 2, 6]), sb(st, "mv", [P, NT, 2]), sb(st, "rstd", [P, NT]), sb(st, "nmr", [P, NT])
        raw = sb(st, "raw", [P, 3, SEQ + 4])
        cv = sb(st, "cv", [P, 3, SEQ])
        sp = sb(st, "sp", [P, 3, NT, 16])
        ab = sb(st, "ab", [P, NT, 32])
        others = sb(st, "others", [P, NT, 8])
        pw = sb(st, "pw", [P, NH, DV])
        up = sb(st, "up", [P, 528])
        win = sb(st, "win", [P, 2, 528])
        vT = spare[:, 0:2, :].rearrange("p a (b s) -> p (a b) s", b=2)
        sq = spare[:, 2, :].rearrange("p (a s) -> p a s", a=2)
        nrm = spare[:, 3, :].rearrange("p (a s) -> p a s", a=2)
        tp = [pb(st, f"tp{i}") for i in range(2)]
        pj = [pb(st, f"pj{i}") for i in range(3)]
        gps = pb(st, "gps")
        rps = [pb(st, f"rps{i}") for i in range(2)]

        ident_in, const_in, small_in, ln_in = sem("ident_in"), sem("const_in"), sem("small_in"), sem("ln_in")
        x_in = [sem(f"x_in{t}") for t in range(NT)]
        rows_proj, rows_copied = sem("gate_rows_proj"), sem("gate_rows_copied")
        pw_in, h_out = sem("pw_in"), sem("h_out")
        chunk_in = [sem(f"chunk_in{i}") for i in range(2)]
        chunk_used, eps_set, pads_set = sem("chunk_used"), sem("eps_set"), sem("pads_set")
        stats_ready, std_ready, scale_ready, norm_ready, gmul_ready, h_ready = (
            sem(f"ln1_{n}") for n in ("stats", "std", "scale", "norm", "gmul", "h"))
        turned, turn_copied = sem("h_turned"), sem("h_turn_copied")
        small_proj, small_copied = sem("small_proj"), sem("small_copied")
        proj_done, proj_copied = sem("proj_done"), sem("proj_copied")
        conv_done, silu_done = sem("conv_done"), sem("silu_done")
        gate_abs = sem("gate_abs")
        gate_exp, gate_in, gate_ln, gates_done = sem("gate_exp"), sem("gate_in"), sem("gate_ln"), sem("gates_done")
        cum_done, cum_copied, a_done, a_turned, scan_done, m_turned = (
            sem(n) for n in ("cum_done", "cum_copied", "a_done", "a_turned", "scan_done", "m_turned"))
        em_arg, beta_done = sem("em_arg"), sem("beta_done")
        square_done, sum_done, root_done, qk_normed = sem("square_done"), sem("sum_done"), sem("root_done"), sem("qk_normed")
        tok_turned, tok_copied = sem("tok_turned"), sem("tok_copied")
        up_copied, pooled, pool_mixed, pool_done = sem("up_copied"), sem("pooled"), sem("pool_mixed"), sem("pool_done")
        dve_chain, pool_chain = sem("front_dve_chain"), sem("front_pool_chain")

        starts = [C_Q, C_K, C_V, C_MQ, C_MV, C_U, C_Z, C_MO]
        w_rows = w_in.rearrange("(p k) n -> p k n", k=KT)
        NQKV = 12
        with nc.Block() as block:
            @block.sync
            def _(sp_):
                for t in range(NT):
                    sp_.dma_start(h[:, t, :], x[t * P:(t + 1) * P, :]).then_inc(x_in[t], 16)
                    if t == 0:
                        sp_.dma_start(lng[:, :], v["ln_in_g"].to_broadcast([P, DM])).then_inc(ln_in, 16)
                        sp_.dma_start(lnb[:, :], v["ln_in_b"].to_broadcast([P, DM])).then_inc(ln_in, 16)
                        sp_.dma_start(cst[:, 0:P], const[:, 0:P]).then_inc(ident_in, 16)
                for c, at in enumerate(starts):
                    if c == 1:
                        sp_.dma_start(sml[:, :], small).then_inc(small_in, 16)
                        sp_.dma_start(cst[:, P:], const[:, P:]).then_inc(const_in, 16)
                        sp_.dma_start(pw[:, :, :], v["pool_w"].rearrange("g c d -> c g d")).then_inc(pw_in, 16)
                    if c >= 2:
                        sp_.wait_ge(chunk_used, c - 1)
                    sp_.dma_start(ring[:, c % 2, :, :], w_rows[:, :, at:at + 512]).then_inc(chunk_in[c % 2], 16)
                    if c == 1:
                        for t in range(NT):
                            sp_.wait_ge(h_ready, t + 1)
                            sp_.dma_start(v["h_dram"][t * P:(t + 1) * P, :], h[:, t, :]).then_inc(h_out, 16)
                sp_.wait_ge(h_out, 16 * NT)

            @block.tensor
            def _(pe):
                pe.wait_ge(ident_in, 16)
                for n in range(2 * NT):
                    t, half = n // 2, n % 2
                    pe.wait_ge(h_ready, t + 1)
                    if n >= 2:
                        pe.wait_ge(turn_copied, n - 1)
                    for k in range(4):
                        last = pe.transpose(tp[n % 2][:, k * P:(k + 1) * P], h[:, t, 4 * half + k::KT], ident)
                    last.then_inc(turned, 1)
                pe.wait_ge(turn_copied, 2 * NT)
                n = 0

                def chunk(c, between=None):
                    nonlocal n
                    pe.wait_ge(chunk_in[c % 2], 16 * (c // 2 + 1))
                    for m in range(4):
                        if n >= 3:
                            pe.wait_ge(proj_copied, n - 2)
                        for k in range(KT):
                            if starts[c] == C_MV:
                                a, b = hT[:, k, m * P:(m + 1) * P], ring[:, c % 2, k, :]
                            else:
                                a, b = ring[:, c % 2, k, m * P:(m + 1) * P], hT[:, k, :]
                            last = pe.matmul(pj[n % 3][:, :], a, b, start=(k == 0), stop=(k == KT - 1))
                        last.then_inc(proj_done, 1)
                        n += 1
                        if between is not None:
                            between(m)

                def chunk_and_free(c, between=None):
                    chunk(c, between)
                    if c + 2 < len(starts):
                        pe.wait_ge(proj_done, 4 * (c + 1))
                        pe.sem_inc(chunk_used, 1)

                chunk_and_free(0)
                pe.wait_ge(small_in, 16)
                wsm = sml[:, SM_W:SM_W + KT * 32].rearrange("p (k n) -> p k n", k=KT)
                for k in range(KT):
                    last = pe.matmul(rps[0][0:32, :], wsm[:, k, :], hT[:, k, :], start=(k == 0), stop=(k == KT - 1))
                last.then_inc(rows_proj, 1)

                def gate_rows(m):
                    if m == 1:
                        pe.wait_ge(rows_copied, 1)
                        for t in range(NT):
                            last = pe.transpose(gps[:, t * 32:(t + 1) * 32], nrm[0:32, 0, t * P:(t + 1) * P], ident[0:32, 0:32])
                        last.then_inc(small_proj, 1)

                chunk_and_free(1, gate_rows)
                chunk_and_free(2)
                pe.wait_ge(const_in, 16)
                pe.wait_ge(gates_done, 4)
                sums = gps[:, 128:224].rearrange("p (t n) -> p t n", t=NT)
                for d, tri in enumerate((cn("upto"), cn("after"))):
                    a, b = slice(4 * d, 4 * d + 4), slice(8 + 4 * d, 12 + 4 * d)
                    pe.matmul(sums[:, :, a], tri, gg[:, :, a], start=True, stop=True)
                    pe.matmul(sums[:, :, 16 + 4 * d:20 + 4 * d], tri, gg[:, :, b], start=True, stop=False)
                    pe.matmul(sums[:, :, 16 + 4 * d:20 + 4 * d], ones, others[:, :, a], start=False, stop=True)
                last = pe.matmul(sums[:, :, 8:16], ones, gg[:, :, 0:8], start=True, stop=True)
                last.then_inc(cum_done, 1)
                chunk_and_free(3)
                pe.wait_ge(a_done, 1)
                for d in range(2):
                    for t in range(NT):
                        last = pe.transpose(rps[d][0:4, t * P:(t + 1) * P], acol[:, t, 4 * d:4 * d + 4], ident)
                last.then_inc(a_turned, 1)
                def head_sum(m):
                    pe.wait_ge(square_done, m + 1)
                    if m >= 2:
                        pe.wait_ge(root_done, m - 1)
                    pe.matmul(tp[m % 2][:, :], ones, sq[:, m % 2, :], start=True, stop=True).then_inc(sum_done, 1)

                def token_rows(m):
                    t = m % 4
                    if m < 4:
                        pe.wait_ge(qk_normed, 8)
                    if m >= 2:
                        pe.wait_ge(tok_copied, m - 1)
                    for hd in range(NH):
                        src = qkT[:, 1, hd, :] if m < 4 else vT[:, hd, :]
                        last = pe.transpose(tp[m % 2][:, hd * P:(hd + 1) * P], src[:, t * P:(t + 1) * P], ident)
                    last.then_inc(tok_turned, 1)

                def pool_mix(g):
                    pe.wait_ge(pooled, g + 1)
                    if g >= 2:
                        pe.wait_ge(pool_done, g - 1)
                    pe.matmul(rps[g % 2][:, :], pw[:, g, :], yT[:, 1, g, :], start=True, stop=True).then_inc(pool_mixed, 1)

                chunk_and_free(4, head_sum)
                pe.wait_ge(scan_done, 2)
                for d in range(2):
                    for t in range(NT):
                        last = pe.transpose(gps[:, 256 + 8 * t + 4 * d:260 + 8 * t + 4 * d], mrow[0:4, d, t * P:(t + 1) * P],
                                            ident[0:4, 0:4])
                last.then_inc(m_turned, 1)
                chunk_and_free(5, lambda m: head_sum(4 + m))
                chunk_and_free(6, lambda m: token_rows(m))
                pe.wait_ge(pw_in, 16)

                def last_hook(m):
                    token_rows(4 + m)
                    pool_mix(m)

                chunk_and_free(7, last_hook)

            @block.scalar
            def _(act):
                act.wait_ge(eps_set, 1)
                def copy_turned(t):
                    for half in range(2):
                        act.wait_ge(turned, 2 * t + half + 1)
                        act.activation(hT[:, 4 * half:4 * half + 4, t * P:(t + 1) * P],
                                       tp[half][:, :].rearrange("p (k s) -> p k s", k=4), ACT.Copy).then_inc(turn_copied, 1)

                def before(t):
                    if t >= 2:
                        copy_turned(t - 2)

                layer_norm_act(act, h, mv, rstd, nmr, epsc[:, 0:1], stats_ready, std_ready, scale_ready, norm_ready, before)
                for t in range(NT - 2, NT):
                    copy_turned(t)
                def token_gates():
                    act.wait_ge(small_proj, 1)
                    act.activation(ab[:, :, :], gps[:, 0:128].rearrange("p (t n) -> p t n", t=NT), ACT.Copy).then_inc(small_copied, 1)
                    act.wait_ge(small_copied, 1)
                    act.activation(beta[:, :, :], ab[:, :, 8:16], ACT.Sigmoid).then_inc(beta_done, 1)
                    act.wait_ge(gate_in, 1)
                    act.activation(sp[:, 1, :, :], sp[:, 1, :, :], ACT.Abs).then_inc(gate_abs, 1)
                    act.wait_ge(gate_abs, 1)
                    act.activation(sp[:, 1, :, :], sp[:, 1, :, :], ACT.Exp, scale=-1.0).then_inc(gate_exp, 1)
                    act.activation(sml[:, SM_BIAS:SM_BIAS + 8], sml[:, SM_BIAS:SM_BIAS + 8], ACT.Exp).then_inc(gate_exp, 1)
                    act.wait_ge(gate_exp, 1)
                    act.activation(sp[:, 1, :, :], sp[:, 1, :, :], ACT.Ln, bias=1.0).then_inc(gate_ln, 1)

                def gates(n):
                    if n == 4:
                        act.wait_ge(rows_proj, 1)
                        act.activation(nrm[0:32, 0, :], rps[0][0:32, :], ACT.Copy).then_inc(rows_copied, 1)
                    if n != 6:
                        return
                    token_gates()

                def copy_qkv(n):
                    act.wait_ge(proj_done, n + 1)
                    if n >= 3:
                        act.wait_ge(conv_done, n - 2)
                    act.activation(raw[:, n % 3, 2:2 + SEQ], pj[n % 3][:, :], ACT.Copy).then_inc(proj_copied, 1)

                def silu_qkv(n):
                    act.wait_ge(conv_done, n + 1)
                    dst = qkT[:, n // 4, n % 4, :] if n < 8 else vT[:, n % 4, :]
                    act.activation(dst, cv[:, n % 3, :], ACT.Silu).then_inc(silu_done, 1)

                act.wait_ge(pads_set, 1)
                for n in range(NQKV):
                    copy_qkv(n)
                    if n >= 1:
                        silu_qkv(n - 1)
                    gates(n)
                silu_qkv(NQKV - 1)
                for n in range(12, 16):
                    act.wait_ge(proj_done, n + 1)
                    act.activation(mq[:, n - 12, :], pj[n % 3][:, :], ACT.Copy,
                                   scale=(1.0 if n < 14 else QK ** -0.5)).then_inc(proj_copied, 1)
                def square(m):
                    act.wait_ge(silu_done, m + 1)
                    if m >= 2:
                        act.wait_ge(sum_done, m - 1)
                    act.activation(sq[:, m % 2, :], qkT[:, m // 4, m % 4, :], ACT.Square).then_inc(square_done, 1)

                def root(m):
                    act.wait_ge(sum_done, m + 1)
                    if m >= 2:
                        act.wait_ge(qk_normed, m - 1)
                    act.activation(nrm[:, m % 2, :], tp[m % 2][:, :], ACT.Sqrt, scale=(float(DV) if m < 4 else 1.0),
                                   bias=epsc[:, 1 if m < 4 else 2:(1 if m < 4 else 2) + 1]).then_inc(root_done, 1)

                def token_copy(m):
                    act.wait_ge(tok_turned, m + 1)
                    dst = (kTok if m < 4 else vTok)[:, m % 4, :, :]
                    act.activation(dst, tp[m % 2][:, :].rearrange("p (h e) -> p h e", h=NH), ACT.Copy).then_inc(tok_copied, 1)

                square(0)
                for n in range(16, 20):
                    act.wait_ge(proj_done, n + 1)
                    act.activation(mvx[:, n - 16, :, 0:DV], pj[n % 3][:, :].rearrange("p (h e) -> p h e", h=NH),
                                   ACT.Copy).then_inc(proj_copied, 1)
                    square(n - 15)
                    root(n - 16)
                for n in range(20, 24):
                    act.wait_ge(proj_done, n + 1)
                    if n >= 21:
                        act.wait_ge(pooled, n - 20)
                    act.activation(up[:, 8:8 + SEQ], pj[n % 3][:, :], ACT.Copy).then_inc(proj_copied, 1)
                    if n < 23:
                        square(n - 15)
                    root(n - 16)
                for n in range(24, 28):
                    act.wait_ge(proj_done, n + 1)
                    act.activation(yT[:, 0, n - 24, :], pj[n % 3][:, :], ACT.Silu).then_inc(proj_copied, 1)
                    token_copy(n - 24)
                act.wait_ge(em_arg, 1)
                act.activation(emx[:, :, :], emx[:, :, :], ACT.Exp, scale=-1.0).then_inc(gate_exp, 1)
                for n in range(28, 32):
                    act.wait_ge(proj_done, n + 1)
                    act.activation(yT[:, 2, n - 28, :], pj[n % 3][:, :], ACT.Sigmoid).then_inc(proj_copied, 1)
                    token_copy(n - 24)
                    g = n - 28
                    act.wait_ge(pool_mixed, g + 1)
                    act.activation(yT[:, 1, g, :], rps[g % 2][:, :], ACT.Copy,
                                   scale=sml[:, SM_NORM + 4 + g:SM_NORM + 5 + g]).then_inc(pool_done, 1)

            @block.vector
            def _(dve):
                chain = Chain(dve, dve_chain)
                dve.memset(epsc[:, 0:1], LN_EPS)
                dve.memset(epsc[:, 1:2], DV * NORM_EPS)
                dve.memset(epsc[:, 2:3], NORM_EPS).then_inc(eps_set, 1)
                dve.memset(raw[:, :, 0:2], 0.0)
                dve.memset(raw[:, :, SEQ + 2:SEQ + 4], 0.0).then_inc(pads_set, 1)
                dve.memset(mvx[:, :, :, DV:DV + 1], 1.0)

                def x_ready(t):
                    dve.wait_ge(x_in[t], 16)
                layer_norm_dve(dve, chain, h, stats, mv, rstd, nmr, x_ready, stats_ready, std_ready, scale_ready,
                               norm_ready, gmul_ready, lng[:, :], ln_in, 1)
                def gates():
                    dve.wait_ge(small_copied, 1)
                    dve.wait_ge(small_in, 16)
                    bias = sml[:, SM_BIAS:SM_BIAS + 32]
                    chain.add(dve.tensor_tensor(sp[:, 0, :, 0:8], ab[:, :, 0:8], bc(bias[:, 8:16], 1, NT), ALU.add))
                    chain.add(dve.tensor_tensor(sp[:, 0, :, 8:16], ab[:, :, 24:32], bc(bias[:, 24:32], 1, NT), ALU.add))
                    chain.add(dve.tensor_tensor(gg[:, :, 16:24], ab[:, :, 16:24], bc(bias[:, 16:24], 1, NT), ALU.add))
                    chain.wait()
                    dve.tensor_scalar(sp[:, 1, :, :], sp[:, 0, :, :], 1.0, None, ALU.mult).then_inc(gate_in, 1)
                    chain.add(dve.tensor_scalar(sp[:, 2, :, 0:8], sp[:, 0, :, 0:8], 0.0, None, ALU.max))
                    chain.wait()
                    dve.tensor_scalar(sp[:, 2, :, 8:16], sp[:, 0, :, 8:16], 0.0, None, ALU.min).then_inc(gate_in, 1)
                    dve.wait_ge(gate_ln, 1)
                    dve.wait_ge(gate_in, 2)
                    chain.link(dve.tensor_tensor(sp[:, 2, :, 0:8], sp[:, 2, :, 0:8], sp[:, 1, :, 0:8], ALU.add))
                    dve.wait_ge(gate_exp, 2)
                    chain.link(dve.tensor_tensor(sp[:, 2, :, 0:8], sp[:, 2, :, 0:8], bc(bias[:, 0:8], 1, NT), ALU.mult))
                    dve.tensor_scalar(gg[:, :, 0:8], sp[:, 2, :, 0:8], -1.0, None, ALU.mult).then_inc(gates_done, 1)
                    dve.tensor_tensor(gg[:, :, 8:16], sp[:, 2, :, 8:16], sp[:, 1, :, 8:16], ALU.subtract).then_inc(gates_done, 1)
                    dve.wait_ge(gates_done, 2)
                    dve.memset(others[:, 0, 0:4], 0.0)
                    chain.link(dve.memset(others[:, NT - 1, 4:8], 0.0))
                    for t in range(1, NT):
                        u = NT - 1 - t
                        first = dve.tensor_tensor(others[:, t, 0:4], others[:, t - 1, 0:4], gg[:, t - 1, 8:12], ALU.add)
                        second = dve.tensor_tensor(others[:, u, 4:8], others[:, u + 1, 4:8], gg[:, u + 1, 12:16], ALU.add)
                        if t < NT - 1:
                            chain.add(first)
                            chain.link(second)
                        else:
                            first.then_inc(gates_done, 1)
                            second.then_inc(gates_done, 1)

                dve.wait_ge(small_in, 16)
                for n in range(NQKV):
                    dve.wait_ge(proj_copied, n + 1)
                    if n >= 3:
                        dve.wait_ge(silu_done, n - 2)
                    taps = sml[:, SM_CONV + TAPS * n:SM_CONV + TAPS * (n + 1)]
                    chain.link(dve.tensor_scalar(cv[:, n % 3, :], raw[:, n % 3, 0:SEQ], taps[:, 0:1], None, ALU.mult))
                    for j in range(1, TAPS):
                        ins = dve.scalar_tensor_tensor(cv[:, n % 3, :], raw[:, n % 3, j:j + SEQ], taps[:, j:j + 1],
                                                       cv[:, n % 3, :], ALU.mult, ALU.add)
                        if j < TAPS - 1:
                            chain.link(ins)
                        else:
                            ins.then_inc(conv_done, 1)
                    if n == 6:
                        gates()
                dve.wait_ge(cum_done, 1)
                dve.tensor_copy(cum[:, :, :], gps[:, 128:224].rearrange("p (t n) -> p t n", t=NT)).then_inc(cum_copied, 1)
                dve.wait_ge(cum_copied, 1)
                dve.tensor_tensor(acol[:, :, :], gg[:, :, 16:24], cum[:, :, 16:24], ALU.subtract).then_inc(a_done, 1)
                zrow = lng[0:4, 0:SEQ]
                chain.link(dve.memset(zrow, 0.0))
                dve.wait_ge(a_turned, 1)
                dve.tensor_tensor_scan(mrow[0:4, 0, :], rps[0][0:4, :], zrow,
                                       0.0, ALU.max, ALU.max).then_inc(scan_done, 1)
                dve.tensor_tensor_scan(mrow[0:4, 1, ::-1], rps[1][0:4, ::-1], zrow,
                                       0.0, ALU.max, ALU.max).then_inc(scan_done, 1)
                for m in range(8):
                    if m == 4:
                        dve.wait_ge(m_turned, 1)
                        dve.tensor_tensor(emx[:, :, :], gps[:, 256:288].rearrange("p (t n) -> p t n", t=NT), cum[:, :, 16:24],
                                          ALU.add).then_inc(em_arg, 1)
                    dve.wait_ge(root_done, m + 1)
                    chain.link(dve.reciprocal(nrm[:, m % 2, :], nrm[:, m % 2, :]))
                    dve.tensor_tensor(qkT[:, m // 4, m % 4, :], qkT[:, m // 4, m % 4, :], nrm[:, m % 2, :],
                                      ALU.mult).then_inc(qk_normed, 1)

            @block.gpsimd
            def _(pool):
                v["zero_last"](pool)
                chain = Chain(pool, pool_chain)
                chain.add(pool.memset(up[:, :], 0.0))
                chain.add(pool.memset(win[:, :, :], 0.0))
                for t in range(NT):
                    pool.wait_ge(gmul_ready, t + 1)
                    pool.wait_ge(ln_in, 32)
                    pool.tensor_tensor(h[:, t, :], h[:, t, :], lnb[:, :], ALU.add).then_inc(h_ready, 1)
                chain.wait()
                edge = cn("edge").rearrange("p (g n) -> p g n", g=4)
                pool.wait_ge(const_in, 16)
                for g in range(4):
                    pool.wait_ge(proj_copied, 21 + g)
                    chain.link(pool.tensor_tensor(win[:, 0, 1:528], up[:, 0:527], up[:, 1:528], ALU.add))
                    cur = 0
                    for lvl in range(g):
                        r = 1 << lvl
                        lo, hi = 2 * r, 528 - 2 * r
                        chain.link(pool.tensor_tensor(win[:, 1 - cur, lo:hi], win[:, cur, lo - r:hi - r],
                                                      win[:, cur, lo + r:hi + r], ALU.add))
                        cur = 1 - cur
                    w = win[:, cur, 8:8 + SEQ]
                    chain.add(pool.tensor_tensor(w[:, 0:8], w[:, 0:8], edge[:, g, 0:8], ALU.mult))
                    chain.add(pool.tensor_tensor(w[:, SEQ - 8:SEQ], w[:, SEQ - 8:SEQ], edge[:, g, 8:16], ALU.mult))
                    chain.add(pool.tensor_scalar(w[:, 8:SEQ - 8], w[:, 8:SEQ - 8], 1.0 / (2 << g), None, ALU.mult))
                    chain.wait()
                    pool.tensor_tensor(yT[:, 1, g, :], w, up[:, 8:8 + SEQ], ALU.subtract).then_inc(pooled, 1)
                    pool.wait_ge(pooled, g + 1)


def mlstm(nc, sem, sb, pb, cn, v):
    sml, epsc, yT, mq, mvx, mrow, acol, emx = (v[k] for k in ("sml", "epsc", "yT", "mq", "mvx", "mrow", "acol", "emx"))
    ident = v["ident"]
    st = ExitStack()
    with st:
        scores = v["wraw"][:, 0:2, :].rearrange("p r (j s) -> p r j s", j=NT)
        wts = v["wraw"][:, 2:4, :].rearrange("p r (j s) -> p r j s", j=NT)
        mdiag = sb(st, "mdiag", [P, 2, NT, P])
        hs = sb(st, "hs", [P, NT, NH, DV])
        tmp = sb(st, "htmp", [P, NT, DV])
        den = sb(st, "den", [P, 2, NT])
        stats, mv, rstd = sb(st, "mstats", [P, NT * NH, 6]), sb(st, "mmv", [P, NT * NH, 2]), sb(st, "mrstd", [P, NT * NH])
        qb = [pb(st, f"qb{i}") for i in range(2)]
        mb = [pb(st, f"mb{i}") for i in range(2)]
        nu = [pb(st, f"nu{i}") for i in range(4)]
        score_done, score_copied, max_spread, diag_ready, exp_done, weighted = (
            sem(n) for n in ("score_done", "score_copied", "max_spread", "diag_ready", "exp_done", "weighted"))
        num_done, den_abs, num_used = sem("num_done"), sem("den_abs"), sem("num_used")
        mvar_ready, mroot_done, mnormed, mturned, yml_done = (
            sem(n) for n in ("mvar_ready", "mroot_done", "mnormed", "mturned", "yml_done"))
        dve_chain, rooms_filled = sem("mlstm_dve_chain"), sem("rooms_filled")

        def span(d, j):
            return (j * P, SEQ) if d == 0 else (0, (j + 1) * P)

        with nc.Block() as block:
            @block.sync
            def _(sp):
                for i, r in enumerate((1, 2, 0)):
                    at = C_G + r * DM
                    sp.dma_start(v["gw"][i], v["w_rows"][:, :, at:at + P]).then_inc(rooms_filled, 16)
                    if i < 2:
                        sp.dma_start(v["bw"][i], v["w_branch"][r].rearrange("(k p) n -> p k n", p=P)[:, :, 0:P])\
                            .then_inc(rooms_filled, 16)
                sp.wait_ge(rooms_filled, 16 * 5)

            @block.tensor
            def _(pe):
                def score(h):
                    rows = slice(QK * (h % 2), QK * (h % 2) + QK)
                    for j in range(NT):
                        n = 4 * h + j
                        if n >= 2:
                            pe.wait_ge(score_copied, n - 1)
                        pe.matmul(qb[n % 2][:, :], mq[rows, 2 + h // 2, j * P:(j + 1) * P], mq[rows, h // 2, :],
                                  start=True, stop=True).then_inc(score_done, 1)

                def spread(n):
                    h, d = n // 2, n % 2
                    if n >= 2:
                        pe.wait_ge(exp_done, n - 1)
                        pe.wait_ge(diag_ready, n - 1)
                    pe.matmul(mb[n % 2][:, :], cn("sel", 4)[:, h * P:(h + 1) * P], mrow[0:4, d, :],
                              start=True, stop=True).then_inc(max_spread, 1)

                def numerator(n):
                    h, d = n // 2, n % 2
                    pe.wait_ge(weighted, n + 1)
                    if n >= 2:
                        pe.wait_ge(num_used, n - 1)
                    for i in range(NT):
                        js = range(i + 1) if d == 0 else range(i, NT)
                        for j in js:
                            last = pe.matmul(nu[2 * (n % 2) + i // 2][:, (i % 2) * (DV + 1):(i % 2 + 1) * (DV + 1)],
                                             wts[:, n % 2, j, i * P:(i + 1) * P], mvx[:, j, h, :],
                                             start=(j == js[0]), stop=(j == js[-1]))
                    last.then_inc(num_done, 1)

                score(0)
                spread(0)
                spread(1)
                for h in range(NH):
                    if h + 1 < NH:
                        score(h + 1)
                        spread(2 * h + 2)
                    numerator(2 * h)
                    if h + 1 < NH:
                        spread(2 * h + 3)
                    numerator(2 * h + 1)
                for h in range(NH):
                    pe.wait_ge(mnormed, NT * (h + 1))
                    if h >= 2:
                        pe.wait_ge(yml_done, h - 1)
                    for t in range(NT):
                        last = pe.transpose(qb[h % 2][:, t * P:(t + 1) * P], hs[:, t, h, :], ident)
                    last.then_inc(mturned, 1)

            @block.scalar
            def _(act):
                def copy_scores(h):
                    if h >= 2:
                        act.wait_ge(weighted, 2 * (h - 1))
                    for j in range(NT):
                        n = 4 * h + j
                        act.wait_ge(score_done, n + 1)
                        act.activation(scores[:, h % 2, j, :], qb[n % 2][:, :], ACT.Copy).then_inc(score_copied, 1)

                def exps(n):
                    h, d = n // 2, n % 2
                    act.wait_ge(diag_ready, n + 1)
                    if n >= 2:
                        act.wait_ge(num_done, n - 1)
                    for j in range(NT):
                        bias = acol[:, j, 4 * d + h:4 * d + h + 1]
                        last = act.activation(wts[:, n % 2, j, j * P:(j + 1) * P], mdiag[:, n % 2, j, :], ACT.Exp, bias=bias)
                        lo, hi = ((j + 1) * P, SEQ) if d == 0 else (0, j * P)
                        if lo < hi:
                            last = act.activation(wts[:, n % 2, j, lo:hi], mb[n % 2][:, lo:hi], ACT.Exp, bias=bias, scale=-1.0)
                    last.then_inc(exp_done, 1)

                def absolute(n):
                    act.wait_ge(num_done, n + 1)
                    if n >= 2:
                        act.wait_ge(num_used, n - 1)
                    for i2 in range(2):
                        src = nu[2 * (n % 2) + i2][:, 0:2 * (DV + 1)].rearrange("p (i e) -> p i e", i=2)[:, :, DV]
                        last = act.activation(den[:, n % 2, 2 * i2:2 * i2 + 2], src, ACT.Abs)
                    last.then_inc(den_abs, 1)

                copy_scores(0)
                exps(0)
                exps(1)
                for h in range(NH):
                    if h + 1 < NH:
                        copy_scores(h + 1)
                    absolute(2 * h)
                    if h + 1 < NH:
                        exps(2 * h + 2)
                    absolute(2 * h + 1)
                    if h + 1 < NH:
                        exps(2 * h + 3)
                act.wait_ge(mvar_ready, NH)
                act.activation(rstd[:, :], mv[:, :, 1], ACT.Sqrt, bias=epsc[:, 2:3]).then_inc(mroot_done, 1)

            @block.vector
            def _(dve):
                chain = Chain(dve, dve_chain)

                def diag(n):
                    dve.wait_ge(max_spread, n + 1)
                    if n >= 2:
                        dve.wait_ge(exp_done, n - 1)
                    neg = cn("neg_fwd" if n % 2 == 0 else "neg_bwd")
                    dve.scalar_tensor_tensor(mdiag[:, n % 2, :, :], mb[n % 2][:, :].rearrange("p (j i) -> p j i", j=NT), -1.0,
                                             bc(neg, 1, NT), ALU.mult, ALU.add).then_inc(diag_ready, 1)

                def weigh(n):
                    h, d = n // 2, n % 2
                    dve.wait_ge(exp_done, n + 1)
                    dve.wait_ge(score_copied, 4 * (h + 1))
                    for j in range(NT):
                        lo, hi = span(d, j)
                        w = wts[:, n % 2, j, lo:hi]
                        last = dve.tensor_tensor(w, w, scores[:, h % 2, j, lo:hi], ALU.mult)
                    last.then_inc(weighted, 1)

                def divide(n):
                    h, d = n // 2, n % 2
                    dn = den[:, n % 2, :]
                    dve.wait_ge(den_abs, n + 1)
                    chain.link(dve.tensor_tensor(dn, dn, emx[:, :, 4 * d + h], ALU.max))
                    chain.link(dve.reciprocal(dn, dn))
                    for i2 in range(2):
                        src = nu[2 * (n % 2) + i2][:, 0:2 * (DV + 1)].rearrange("p (i e) -> p i e", i=2)[:, :, 0:DV]
                        dst = hs[:, 2 * i2:2 * i2 + 2, h, :] if d == 0 else tmp[:, 2 * i2:2 * i2 + 2, :]
                        last = dve.tensor_tensor(dst, src, bc(dn[:, 2 * i2:2 * i2 + 2], 2, DV), ALU.mult)
                    last.then_inc(num_used, 1)
                    if d == 1:
                        dve.wait_ge(num_used, n + 1)
                        chain.link(dve.tensor_tensor(hs[:, :, h, :], hs[:, :, h, :], tmp[:, :, :], ALU.add))
                        for t in range(NT):
                            chain.add(dve.bn_stats(stats[:, h * NT + t, :], hs[:, t, h, :]))
                        chain.wait()
                        for t in range(NT):
                            last = dve.bn_aggr(mv[:, h * NT + t, :], stats[:, h * NT + t, :])
                        last.then_inc(mvar_ready, 1)

                diag(0)
                diag(1)
                weigh(0)
                for n in range(2 * NH):
                    if n + 2 < 2 * NH:
                        diag(n + 2)
                    if n + 1 < 2 * NH:
                        weigh(n + 1)
                    divide(n)
                dve.wait_ge(mroot_done, 1)
                chain.link(dve.reciprocal(rstd[:, :], rstd[:, :]))

                def norm(h):
                    for t in range(NT):
                        g = h * NT + t
                        o = hs[:, t, h, :]
                        dve.tensor_scalar(o, o, mv[:, g, 0:1], rstd[:, g:g + 1], ALU.subtract, ALU.mult).then_inc(mnormed, 1)

                def place(h):
                    dve.wait_ge(mturned, h + 1)
                    dve.scalar_tensor_tensor(yT[:, 2, h, :], qb[h % 2][:, :], sml[:, SM_NORM + 8 + h:SM_NORM + 9 + h],
                                             yT[:, 2, h, :], ALU.mult, ALU.mult).then_inc(yml_done, 1)

                norm(0)
                norm(1)
                for h in range(NH):
                    place(h)
                    if h + 2 < NH:
                        norm(h + 2)

            @block.gpsimd
            def _(pool):
                v["zero_last"](pool)


def deltanet(nc, sem, sb, pb, cn, v):
    sml, epsc, yT, qkT, kTok, vTok, beta, cum, gg = (
        v[k] for k in ("sml", "epsc", "yT", "qkT", "kTok", "vTok", "beta", "cum", "gg"))
    ident, ones = v["ident"], v["ones"]
    st = ExitStack()
    NB = 2 * NT
    BATCH = [(m % 2, m // 2 if m % 2 == 0 else NT - 1 - m // 2) for m in range(NB)]
    with st:
        def four(name, n):
            return sb(st, name, [P, n, NH, P])

        dec = four("dec", 2)
        mt, tt, tn, at, qe = (v["wraw"][:, i, :].rearrange("p (m h e) -> p m h e", m=4, h=NH) for i in range(5))
        ot, rhs = (v["wraw"][:, 5, 1024 * i:1024 * i + 1024].rearrange("p (m h e) -> p m h e", m=2, h=NH) for i in range(2))
        y1s = sb(st, "y1s", [P, 2, 2, NH, P])
        stage = sb(st, "stage", [P, 2, 2, SEQ])
        sig = sb(st, "sigd", [P, 2, SEQ])
        part = sb(st, "partd", [P, SEQ])
        gw, bw = v["gw"], v["bw"]
        w_rows, w_branch = v["w_rows"], v["w_branch"]
        hT = v["hT"]
        vn, vnd = four("vn", 2), four("vnd", 2)
        state = four("state", 2)
        oT = sb(st, "oT", [P, NH, SEQ])
        osq, oroot = sb(st, "osq", [P, NH, P]), sb(st, "oroot", [P, NH, P])
        eg = sb(st, "eg", [P, NT, 3, 8])
        pr = [pb(st, f"pr{i}") for i in range(2)]
        lv = [pb(st, f"lv{i}") for i in range(2)]
        gate_ps, branch_ps = pb(st, "gate_ps"), pb(st, "branch_ps")
        sc = [pb(st, f"sc{i}") for i in range(2)]
        (gr_done, kk_done, qk_done, turn_done, dif_ready, dec_ready, egr_ready, qe_ready, kk_used, mt_ready, tt_ready,
         at_ready, tn_copied) = (sem("dn_" + n) for n in (
             "gr_done", "kk_done", "qk_done", "turn_done", "dif_ready", "dec_ready", "egr_ready", "qe_ready", "kk_used",
             "mt_ready", "tt_ready", "at_ready", "tn_copied"))
        ot_ready, y1_done, y1_copied, p2_done, t_updated, again_done, again_copied = (
            sem("dn_" + n) for n in ("ot_ready", "y1_done", "y1_copied", "p2_done", "t_updated", "again_done", "again_copied"))
        ks_done, r_ready, tr_done, vn_ready, ds_done, o_done, s_updated, o_taken = (
            sem("dn_" + n) for n in ("ks_done", "r_ready", "tr_done", "vn_ready", "ds_done", "o_done", "s_updated", "o_taken"))
        eg_arg, eg_ready, s_zero = sem("dn_eg_arg"), sem("dn_eg_ready"), sem("dn_s_zero")
        osq_done, osum_done, oroot_done, y_done = (sem("dn_" + n) for n in ("osq", "osum", "oroot", "y"))
        dve_chain, y1_cleared = sem("dn_dve_chain"), sem("dn_y1_cleared")
        gw_in, bw_in = [sem(f"dn_gw_in{i}") for i in range(3)], [sem(f"dn_bw_in{i}") for i in range(2)]
        gate_done, branch_done, sig_done, gated, kept_done, next_bw = (
            sem("dn_" + n) for n in ("gate_done", "branch_done", "sig_done", "gated", "kept_done", "next_bw"))
        kept_out = [[sem(f"dn_kept_out{i}{j}") for j in range(2)] for i in range(2)]

        order = []
        for m in range(2):
            order += [("gram", m), ("attn", m), ("turn", m)]
        for p in range(NT):
            a, b = 2 * p, 2 * p + 1
            for l in range(1, NL):
                order += [("y1", a, l), ("y1", b, l)]
                if p >= 1 and l <= 3:
                    order += [(("read", "solve", "write")[l - 1], m) for m in (a - 2, b - 2)]
                if l == 4:
                    order += [("norm", m) for m in (a - 2, b - 2) if m >= NB // 2]
                if p + 1 < NT:
                    order += {3: [("gram", a + 2)], 4: [("attn", a + 2), ("turn", a + 2)],
                              5: [("gram", b + 2)], 6: [("attn", b + 2), ("turn", b + 2)]}.get(l, [])
                order += [("p2", a, l), ("p2", b, l)]
                if l < NL - 1:
                    order += [("again", a, l), ("again", b, l)]
        for step in ("read", "solve", "write"):
            order += [(step, NB - 2), (step, NB - 1)]
        order += [("norm", NB - 2), ("norm", NB - 1)]
        BURST = 4
        fill = []
        for c in range(KT):
            for i, (what, r, n) in enumerate((("gate", 1, KT), ("branch", 1, NH), ("gate", 2, KT), ("branch", 2, NH), ("gate", 0, KT))):
                fill += [("fill", what, c, r, k) for k in range(n)]
        weight = {"gram": 2.0, "attn": 1.0, "turn": 2.0, "y1": 2.0, "p2": 2.0, "again": 1.0, "read": 2.0, "solve": 2.0, "write": 2.5, "norm": 3.0}
        whole = sum(weight[op[0]] for op in order)
        mixed, given, seen = [], 0, 0.0
        for op in order:
            mixed.append(op)
            seen += weight[op[0]]
            upto = BURST * int(len(fill) * seen / whole / BURST + 0.5)
            mixed += fill[given:upto]
            given = upto
        order = mixed

        def at_level(m, l):
            return (m // 2) * 2 * (NL - 1) + 2 * (l - 1) + m % 2

        def at_again(m, l):
            return (m // 2) * 2 * (NL - 2) + 2 * (l - 1) + m % 2

        def tile(t):
            return slice(t * P, (t + 1) * P)

        def heads(ap):
            return ap[:, :].rearrange("p (h e) -> p h e", h=NH)

        def halves(ap, l, side):
            return ap.rearrange("p h (n s b) -> p h n s b", s=2, b=LEVELS[l])[:, :, :, side, :]

        def packed(bank, part, l):
            return bank[:, 256 * part:256 * part + 256].rearrange("p (h n b) -> p h n b", h=NH, b=LEVELS[l])

        def fill_gate(c, r):
            return 3 * c + (1, 2, 0).index(r)

        def fill_branch(c, r):
            return 2 * c + r - 1

        with nc.Block() as block:
            @block.sync
            def _(sp):
                def load_gate(g):
                    c, r = g // 3, (1, 2, 0)[g % 3]
                    at = C_G + r * DM + c * P
                    if g >= 3:
                        sp.wait_ge(gate_done, g - 2)
                        sp.dma_start(gw[g % 3], w_rows[:, :, at:at + P]).then_inc(gw_in[g % 3], 16)

                def load_branch(b):
                    c, r = b // 2, b % 2 + 1
                    if b >= 2:
                        sp.wait_ge(branch_done, b - 1)
                        sp.dma_start(bw[b % 2], w_branch[r].rearrange("(k p) n -> p k n", p=P)[:, :, c * P:c * P + P])\
                            .then_inc(bw_in[b % 2], 16)

                def keep(sp, c):
                    sp.wait_ge(kept_done, c + 1)
                    sp.dma_start(v["kept_dram"][1, c], stage[:, 1, c % 2, :]).then_inc(kept_out[1][c % 2], 16)
                    sp.wait_ge(sig_done, 3 * (c + 1))
                    sp.dma_start(v["kept_dram"][0, c], stage[:, 0, c % 2, :]).then_inc(kept_out[0][c % 2], 16)

                for c in range(KT):
                    for i in range(3):
                        load_gate(3 * c + i)
                        if i < 2:
                            load_branch(2 * c + i)
                    if c >= 1:
                        keep(sp, c - 1)
                keep(sp, KT - 1)
                sp.wait_ge(gate_done, 3 * KT)
                sp.wait_ge(branch_done, 2 * KT)
                sp.dma_start(v["h2"][:, :, :], w_branch[0].rearrange("(k p) n -> p k n", p=P)).then_inc(next_bw, 16)
                for c in range(KT - 2, KT):
                    for i in range(2):
                        sp.wait_ge(kept_out[i][c % 2], 16 * (c // 2 + 1))
                sp.wait_ge(next_bw, 16)

            @block.tensor
            def _(pe):
                pe.wait_ge(s_zero, 2)
                for op in order:
                    if op[0] == "fill":
                        what, c, r, k = op[1:]
                        if what == "gate":
                            g = fill_gate(c, r)
                            if k == 0:
                                if g >= 3:
                                    pe.wait_ge(gw_in[g % 3], 16 * (g // 3))
                                if g >= 1:
                                    pe.wait_ge(sig_done, g)
                            last = pe.matmul(gate_ps[:, :], gw[g % 3][:, k, :], hT[:, k, :], start=(k == 0), stop=(k == KT - 1))
                            if k == KT - 1:
                                last.then_inc(gate_done, 1)
                        else:
                            b = fill_branch(c, r)
                            if k == 0:
                                if b >= 2:
                                    pe.wait_ge(bw_in[b % 2], 16 * (b // 2))
                                if b >= 1:
                                    pe.wait_ge(gated, b)
                            last = pe.matmul(branch_ps[:, :], bw[b % 2][:, k, :], yT[:, r, k, :], start=(k == 0), stop=(k == NH - 1))
                            if k == NH - 1:
                                last.then_inc(branch_done, 1)
                        continue
                    kind, m = op[0], op[1]
                    d, t = BATCH[m]
                    tri = cn("upto" if d == 0 else "after")
                    if kind == "gram":
                        if m >= 1:
                            pe.wait_ge(at_ready, m)
                            pe.wait_ge(tn_copied, m)
                        for h in range(NH):
                            last = pe.matmul(pr[0][:, tile(h)], gg[:, t, 4 * d + h:4 * d + h + 1].to_broadcast([P, P]), tri,
                                             start=True, stop=True)
                        last.then_inc(gr_done, 1)
                        for h in range(NH):
                            last = pe.matmul(pr[1][:, tile(h)], qkT[:, 1, h, tile(t)], qkT[:, 1, h, tile(t)],
                                             start=True, stop=True)
                        last.then_inc(kk_done, 1)
                    elif kind == "attn":
                        pe.wait_ge(dif_ready, m + 1)
                        pe.wait_ge(egr_ready, m + 1)
                        for h in range(NH):
                            last = pe.matmul(pr[0][:, tile(h)], qkT[:, 1, h, tile(t)], qkT[:, 0, h, tile(t)],
                                             start=True, stop=True)
                        last.then_inc(qk_done, 1)
                    elif kind == "turn":
                        pe.wait_ge(kk_used, m + 1)
                        pe.wait_ge(tt_ready, m + 1)
                        for h in range(NH):
                            last = pe.transpose(pr[1][:, tile(h)], tt[:, m % 4, h, :], ident)
                        last.then_inc(turn_done, 1)
                    elif kind == "y1":
                        l = op[2]
                        i = at_level(m, l)
                        pe.wait_ge(ot_ready, i + 1)
                        pe.wait_ge(tn_copied, m + 1)
                        if i >= 2:
                            pe.wait_ge(t_updated, i - 1)
                        if l > 1:
                            pe.wait_ge(again_copied, at_again(m, l - 1) + 1)
                        for h in range(NH):
                            last = pe.matmul(packed(lv[d], 0, l)[:, h], ot[:, i % 2, h, :],
                                             halves(tn[:, m % 4, :, :], l, d)[:, h], start=True, stop=True)
                        last.then_inc(y1_done, 1)
                    elif kind == "p2":
                        l = op[2]
                        pe.wait_ge(y1_copied, at_level(m, l) + 1)
                        pe.wait_ge(y1_cleared, at_level(m, l) + 1)
                        for h in range(NH):
                            last = pe.matmul(packed(lv[d], 1, l)[:, h], y1s[:, d, l % 2, h, :],
                                             halves(tt[:, m % 4, :, :], l, 1 - d)[:, h], start=True, stop=True)
                        last.then_inc(p2_done, 1)
                    elif kind == "again":
                        l = op[2]
                        pe.wait_ge(t_updated, at_level(m, l) + 1)
                        for h in range(NH):
                            last = pe.transpose(lv[d][:, tile(h)], tt[:, m % 4, h, :], ident)
                        last.then_inc(again_done, 1)
                    elif kind == "norm":
                        n = m - NB // 2
                        pe.wait_ge(osq_done, n + 1)
                        pe.wait_ge(o_taken, m + 1)
                        if m < NB - 2:
                            pe.wait_ge(s_updated, m + 1)
                        pe.matmul(sc[m % 2][:, :], ones, osq[:, :, :].rearrange("p h e -> p (h e)"),
                                  start=True, stop=True).then_inc(osum_done, 1)
                    elif kind == "read":
                        if m >= 2:
                            pe.wait_ge(s_updated, m - 1)
                        if m >= 1:
                            pe.wait_ge(r_ready, m)
                            if m % 2 == 0:
                                pe.wait_ge(s_updated, m)
                        if m >= NB // 2 + 2:
                            pe.wait_ge(oroot_done, m - NB // 2 - 1)
                        for h in range(NH):
                            last = pe.matmul(sc[m % 2][:, tile(h)], qkT[:, 1, h, tile(t)], state[:, d, h, :],
                                             start=True, stop=True)
                        last.then_inc(ks_done, 1)
                    elif kind == "solve":
                        pe.wait_ge(r_ready, m + 1)
                        pe.wait_ge(t_updated, at_level(m, NL - 1) + 1)
                        for h in range(NH):
                            last = pe.matmul(sc[m % 2][:, tile(h)], tt[:, m % 4, h, :], rhs[:, d, h, :], start=True, stop=True)
                        last.then_inc(tr_done, 1)
                    elif kind == "write":
                        pe.wait_ge(vn_ready, m + 1)
                        pe.wait_ge(at_ready, m + 1)
                        pe.wait_ge(qe_ready, m + 1)
                        for h in range(NH):
                            pe.matmul(sc[m % 2][:, tile(h)], vn[:, d, h, :], at[:, m % 4, h, :], start=True, stop=False)
                            last = pe.matmul(sc[m % 2][:, tile(h)], state[:, d, h, :], qe[:, m % 4, h, :], start=False, stop=True)
                        last.then_inc(o_done, 1)
                        if m < NB - 2:
                            pe.wait_ge(o_taken, m + 1)
                            for h in range(NH):
                                last = pe.matmul(sc[m % 2][:, tile(h)], kTok[:, t, h, :], vnd[:, d, h, :], start=True, stop=True)
                            last.then_inc(ds_done, 1)

            @block.scalar
            def _(act):
                act.wait_ge(eg_arg, 1)
                act.activation(eg[:, :, :, :], eg[:, :, :, :], ACT.Exp).then_inc(eg_ready, 1)
                for op in order:
                    if op[0] == "fill":
                        what, c, r, k = op[1:]
                        if what == "gate" and k == KT - 1:
                            g = fill_gate(c, r)
                            act.wait_ge(gate_done, g + 1)
                            if r == 0:
                                dst = stage[:, 0, c % 2, :]
                                if c >= 2:
                                    act.wait_ge(kept_out[0][c % 2], 16 * (c // 2))
                            else:
                                dst = sig[:, r - 1, :]
                                if c >= 1:
                                    act.wait_ge(gated, fill_branch(c, r) - 1)
                            act.activation(dst, gate_ps[:, :], ACT.Sigmoid).then_inc(sig_done, 1)
                        continue
                    kind, m = op[0], op[1]
                    d, t = BATCH[m]
                    if kind == "gram":
                        act.wait_ge(gr_done, m + 1)
                        if m >= 4:
                            act.wait_ge(o_done, m - 3)
                        act.activation(qe[:, m % 4, :, :], heads(pr[0]), ACT.Exp).then_inc(egr_ready, 1)
                        act.wait_ge(dif_ready, m + 1)
                        act.activation(dec[:, m % 2, :, :], dec[:, m % 2, :, :], ACT.Exp).then_inc(dec_ready, 1)
                    elif kind == "turn":
                        act.wait_ge(turn_done, m + 1)
                        act.activation(tn[:, m % 4, :, :], heads(pr[1]), ACT.Copy).then_inc(tn_copied, 1)
                    elif kind == "again":
                        l = op[2]
                        act.wait_ge(again_done, at_again(m, l) + 1)
                        act.activation(halves(tn[:, m % 4, :, :], l, d), halves(heads(lv[d]), l, d), ACT.Copy).then_inc(again_copied, 1)
                    elif kind == "y1":
                        act.wait_ge(y1_done, at_level(m, op[2]) + 1)
                        act.wait_ge(y1_cleared, at_level(m, op[2]) + 1)
                        act.activation(halves(y1s[:, d, op[2] % 2, :, :], op[2], d), packed(lv[d], 0, op[2]),
                                       ACT.Copy).then_inc(y1_copied, 1)
                    elif kind == "write" and m < NB // 2:
                        act.wait_ge(o_done, m + 1)
                        act.activation(oT[:, :, tile(t)], heads(sc[m % 2]), ACT.Copy).then_inc(o_taken, 1)
                    elif kind == "norm":
                        n = m - NB // 2
                        act.wait_ge(o_taken, m + 1)
                        if n >= 1:
                            act.wait_ge(osum_done, n)
                        act.activation(osq[:, :, :], oT[:, :, tile(t)], ACT.Square).then_inc(osq_done, 1)
                        act.wait_ge(osum_done, n + 1)
                        if n >= 1:
                            act.wait_ge(y_done, n)
                        act.activation(oroot[:, :, :], heads(sc[m % 2]), ACT.Sqrt,
                                       scale=1.0 / DV, bias=epsc[:, 2:3]).then_inc(oroot_done, 1)

            @block.vector
            def _(dve):
                chain = Chain(dve, dve_chain)
                for d in range(2):
                    dve.memset(state[:, d, :, :], 0.0).then_inc(s_zero, 1)
                chain.add(dve.tensor_copy(eg[:, :, 0, :], cum[:, :, 0:8]))
                chain.add(dve.tensor_tensor(eg[:, :, 1, :], cum[:, :, 8:16], cum[:, :, 0:8], ALU.subtract))
                chain.wait()
                dve.tensor_copy(eg[:, :, 2, :], cum[:, :, 8:16]).then_inc(eg_arg, 1)
                for op in order:
                    if op[0] == "fill":
                        what, c, r, k = op[1:]
                        if what == "branch" and k == NH - 1:
                            b = fill_branch(c, r)
                            dve.wait_ge(branch_done, b + 1)
                            dve.wait_ge(sig_done, fill_gate(c, r) + 1)
                            dst = stage[:, 1, c % 2, :]
                            if r == 1:
                                if c >= 2:
                                    dve.wait_ge(kept_out[1][c % 2], 16 * (c // 2))
                                dve.tensor_tensor(dst, sig[:, 0, :], branch_ps[:, :], ALU.mult).then_inc(gated, 1)
                            else:
                                dve.tensor_tensor(part[:, :], sig[:, 1, :], branch_ps[:, :], ALU.mult).then_inc(gated, 1)
                                dve.wait_ge(gated, b + 1)
                                dve.tensor_tensor(dst, dst, part[:, :], ALU.add).then_inc(kept_done, 1)
                                dve.wait_ge(kept_done, c + 1)
                        continue
                    kind, m = op[0], op[1]
                    d, t = BATCH[m]
                    col = slice(4 * d, 4 * d + 4)
                    if kind == "gram":
                        dve.wait_ge(egr_ready, m + 1)
                        if m >= 2:
                            dve.wait_ge(at_ready, m - 1)
                        dd = dec[:, m % 2, :, :]
                        chain.link(dve.tensor_tensor(dd, heads(pr[0]), bc(cum[:, t, col], 2, P), ALU.subtract))
                        dve.tensor_tensor(dd, dd, bc(cn("neg_fwd" if d == 0 else "neg_bwd"), 1, NH), ALU.add).then_inc(dif_ready, 1)
                        dve.wait_ge(kk_done, m + 1)
                        dve.wait_ge(dec_ready, m + 1)
                        if m >= 4:
                            dve.wait_ge(ot_ready, at_level(m - 4, NL - 1) + 1)
                            dve.wait_ge(tr_done, m - 3)
                        dve.tensor_tensor(mt[:, m % 4, :, :], heads(pr[1]), dd, ALU.mult).then_inc(kk_used, 1)
                        dve.wait_ge(kk_used, m + 1)
                        dve.tensor_tensor(mt[:, m % 4, :, :], mt[:, m % 4, :, :], bc(beta[:, t, col], 2, P), ALU.mult).then_inc(mt_ready, 1)
                        dve.wait_ge(mt_ready, m + 1)
                        chain.link(dve.scalar_tensor_tensor(tt[:, m % 4, :, :], mt[:, m % 4, :, :], -1.0,
                                                            bc(cn(f"level{d}_1"), 1, NH), ALU.mult, ALU.mult))
                        dve.tensor_tensor(tt[:, m % 4, :, :], tt[:, m % 4, :, :], bc(ident, 1, NH), ALU.add).then_inc(tt_ready, 1)
                    elif kind == "attn":
                        dve.wait_ge(qk_done, m + 1)
                        if m >= 4:
                            dve.wait_ge(o_done, m - 3)
                        dve.tensor_tensor(at[:, m % 4, :, :], heads(pr[0]), dec[:, m % 2, :, :], ALU.mult).then_inc(at_ready, 1)
                    elif kind == "p2":
                        l = op[2]
                        dve.wait_ge(p2_done, at_level(m, l) + 1)
                        old = halves(tt[:, m % 4, :, :], l, 1 - d)
                        dve.tensor_tensor(old, old, packed(lv[d], 1, l), ALU.subtract).then_inc(t_updated, 1)
                    elif kind == "read":
                        dve.wait_ge(ks_done, m + 1)
                        dve.wait_ge(eg_ready, 1)
                        r = rhs[:, d, :, :]
                        chain.link(dve.tensor_tensor(r, heads(sc[m % 2]), bc(eg[:, t, 0, col], 2, DV), ALU.mult))
                        dve.tensor_tensor(r, vTok[:, t, :, :], r, ALU.subtract).then_inc(r_ready, 1)
                    elif kind == "solve":
                        dve.wait_ge(tr_done, m + 1)
                        chain.link(dve.tensor_tensor(vn[:, d, :, :], heads(sc[m % 2]), bc(beta[:, t, col], 2, DV), ALU.mult))
                        if m >= 2:
                            dve.wait_ge(ds_done, m - 1)
                        dve.tensor_tensor(vnd[:, d, :, :], vn[:, d, :, :], bc(eg[:, t, 1, col], 2, DV), ALU.mult).then_inc(vn_ready, 1)
                    elif kind == "write":
                        dve.wait_ge(o_done, m + 1)
                        if m >= NB // 2:
                            dve.tensor_tensor(oT[:, :, tile(t)], oT[:, :, tile(t)], heads(sc[m % 2]), ALU.add).then_inc(o_taken, 1)
                        if m < NB - 2:
                            s = state[:, d, :, :]
                            chain.link(dve.tensor_tensor(s, s, bc(eg[:, t, 2, col], 2, DV), ALU.mult))
                            dve.wait_ge(ds_done, m + 1)
                            dve.tensor_tensor(s, s, heads(sc[m % 2]), ALU.add).then_inc(s_updated, 1)
                    elif kind == "norm":
                        r, o = oroot[:, :, :], oT[:, :, tile(t)]
                        dve.wait_ge(o_taken, m + 1)
                        dve.wait_ge(oroot_done, m - NB // 2 + 1)
                        chain.link(dve.reciprocal(r, r))
                        chain.link(dve.tensor_tensor(r, r, o, ALU.mult))
                        chain.link(dve.tensor_tensor(r, r, bc(sml[:, SM_NORM:SM_NORM + NH], 2, P), ALU.mult))
                        dve.tensor_tensor(yT[:, 0, :, tile(t)], yT[:, 0, :, tile(t)], r, ALU.mult).then_inc(y_done, 1)

            @block.gpsimd
            def _(pool):
                v["zero_last"](pool)
                for op in order:
                    if op[0] == "fill":
                        continue
                    kind, m = op[0], op[1]
                    d, t = BATCH[m]
                    if kind == "gram":
                        pool.wait_ge(egr_ready, m + 1)
                        pool.tensor_tensor(qe[:, m % 4, :, :], qe[:, m % 4, :, :], qkT[:, 0, :, tile(t)], ALU.mult).then_inc(qe_ready, 1)
                    elif kind == "y1":
                        l = op[2]
                        i = at_level(m, l)
                        if i >= 4:
                            pool.wait_ge(p2_done, i - 3)
                        pool.memset(y1s[:, d, l % 2, :, :], 0.0).then_inc(y1_cleared, 1)
                        pool.wait_ge(mt_ready, m + 1)
                        if i >= 2:
                            pool.wait_ge(y1_done, i - 1)
                        pool.tensor_tensor(ot[:, i % 2, :, :], mt[:, m % 4, :, :], bc(cn(f"level{d}_{LEVELS[l]}"), 1, NH),
                                           ALU.mult).then_inc(ot_ready, 1)


def merge(nc, sem, sb, pb, cn, v):
    w_in, w_branch, w_out = v["w_in"], v["w_branch"], v["w_out"]
    sml, epsc, hT, yT, h2, rows_all, flag = (v[k] for k in ("sml", "epsc", "hT", "yT", "h2", "rows_all", "flag"))
    ident, ones = v["ident"], v["ones"]
    st = ExitStack()
    with st:
        wo = v["wraw"][:, 0:4, :].rearrange("p (r a) (b n) -> p r (a b) n", r=2, n=512)
        bw = h2[:, :, :]
        merged = v["wraw"][:, 4:6, :].rearrange("p a (b n) -> p (a b) n", n=SEQ)
        sig = sb(st, "sig", [P, KT, SEQ])
        lng, lnb = sb(st, "lng2", [P, DM]), sb(st, "lnb2", [P, DM])
        stats, mv, rstd, nmr = sb(st, "stats2", [P, NT, 2, 6]), sb(st, "mv2", [P, NT, 2]), sb(st, "rstd2", [P, NT]), sb(st, "nmr2", [P, NT])
        r4 = lambda name: sb(st, name, [P, NT, NE])
        sco, sel, rank, gt, pos, dest, alt, prod = (r4(n) for n in ("sco", "sel", "rank", "gt", "pos", "dest", "alt", "prod"))
        onek = sb(st, "onek", [P, 2, NT, NE])
        mask = r4("mask")
        earlier = sb(st, "earlier", [P, NT + 1, NE])
        hi, lo = sb(st, "hi", [P, NT * NG, 2]), sb(st, "lo", [P, NT * NG, 2])
        g3 = sb(st, "g3", [P, 4, NT * NG])
        gm = sb(st, "gm", [P, 2, NT])
        sk = sb(st, "sk", [P, 4, NT])
        dk = sb(st, "dk", [P, 2, NT])
        dki = sb(st, "dki", [P, 2, NT], I32)
        pay = sb(st, "pay", [P, NT, 2, 4], I32)
        ce = sb(st, "ce", [P, 5, NE])
        eo = sb(st, "eo", [1, OVER, NE])
        eov = sb(st, "eov", [1, 1 + OVER])
        far = sb(st, "far", [P, TABLE * 4 // P], I32)
        gp = [pb(st, f"gp{i}") for i in range(3)]
        yp = [pb(st, f"yp{i}") for i in range(3)]
        lp, cp = pb(st, "lp"), pb(st, "cp")
        kept_in, wo_in, h_in = [sem(f"kept_in{i}") for i in range(KT)], [sem(f"wo_in{i}") for i in range(2)], [sem(f"h_in{i}") for i in range(NT)]
        ln_in, far_out, h2_out, tab_in = sem("ln2_in"), sem("far_out"), sem("h2_out"), sem("tab_in")
        far_set, branch_done, part_done, merged_sum = (
            sem("mg_" + n) for n in ("far_set", "branch_done", "part_done", "merged_sum"))
        out_done, res_done = sem("mg_out_done"), sem("mg_res_done")
        stats_ready, std_ready, scale_ready, norm_ready, gmul_ready, h2_ready = (
            sem(f"ln2_{n}") for n in ("stats", "std", "scale", "norm", "gmul", "h"))
        turned, turn_copied, logit_done, score_done = sem("mg_turned"), sem("mg_turn_copied"), sem("mg_logits"), sem("mg_scores")
        earlier_done = sem("mg_earlier")
        mask_done, pos_done, pay_done, scattered = sem("mg_mask"), sem("mg_pos"), sem("mg_pay"), sem("mg_scattered")
        dve_chain = sem("mg_dve_chain")
        experts_in = [sem(f"experts_in{u}") for u in range(NRAW)]

        def first_experts(sp):
            for u in range(NRAW):
                w = (v["moe_w1"], v["moe_w2"], v["moe_w3"])[u // 2].rearrange("e (p k) n -> e p (k n)", p=P)
                sp.dma_start(v["wraw"][:, u, :], w[0][:, (u % 2) * HALF:(u % 2 + 1) * HALF]).then_inc(experts_in[u], 16)

        with nc.Block() as block:
            @block.sync
            def _(sp):
                for c in range(KT):
                    sp.dma_start(sig[:, c, :], v["kept_dram"][0, c]).then_inc(kept_in[c], 16)
                    sp.dma_start(merged[:, c, :], v["kept_dram"][1, c]).then_inc(kept_in[c], 16)
                for half in range(2):
                    sp.dma_start(wo[:, half, :, :], w_out.rearrange("(k p) n -> p k n", p=P)[:, :, half * 512:half * 512 + 512]).then_inc(wo_in[half], 16)
                sp.dma_start(lng[:, :], v["ln_mix_g"].to_broadcast([P, DM])).then_inc(ln_in, 16)
                sp.dma_start(lnb[:, :], v["ln_mix_b"].to_broadcast([P, DM])).then_inc(ln_in, 16)
                sp.wait_ge(far_set, 1)
                sp.dma_start(v["slots_dram"].rearrange("(p a) b -> p (a b)", p=P), far[:, :]).then_inc(far_out, 16)
                sp.wait_ge(branch_done, KT)
                for t in range(NT):
                    sp.dma_start(h2[:, t, :], v["h_dram"][t * P:(t + 1) * P, :]).then_inc(h_in[t], 16)
                for t in range(NT):
                    sp.wait_ge(h2_ready, t + 1)
                    sp.dma_start(v["h2_dram"][t * P:(t + 1) * P, :], h2[:, t, :]).then_inc(h2_out, 16)
                    if t == 1:
                        sp.wait_ge(out_done, 2 * NT)
                        first_experts(sp)
                sp.wait_ge(scattered, 16 * 2 * NT)
                sd = v["slots_dram"]
                for half in range(2):
                    rows = slice(half * SLOTS, (half + 1) * SLOTS)
                    sp.dma_start(rows_all[rows, 0:NE, :], sd[0:SLOTS * NE, :].rearrange("(s e) w -> s e w", e=NE)).then_inc(tab_in, 16)
                    sp.dma_start(rows_all[rows, NE:NE + OVER, :], sd[SLOTS * NE:, :].rearrange("(s e) w -> s e w", e=OVER)).then_inc(tab_in, 16)
                sp.wait_ge(tab_in, 64)
                sp.wait_ge(h2_out, 16 * NT)
                for u in range(NRAW):
                    sp.wait_ge(experts_in[u], 16)

            @block.tensor
            def _(pe):
                for c in range(KT):
                    if c >= 3:
                        pe.wait_ge(part_done, c - 2)
                    for k in range(NH):
                        last = pe.matmul(yp[c % 3][:, :], bw[:, k, c * P:(c + 1) * P], yT[:, 0, k, :],
                                         start=(k == 0), stop=(k == NH - 1))
                    last.then_inc(branch_done, 1)
                pe.wait_ge(merged_sum, KT)
                wr = sml[:, SM_RW:SM_RW + KT * NE].rearrange("p (k n) -> p k n", k=KT)

                def project(t):
                    for half in range(2):
                        n = 2 * t + half
                        if n < 2:
                            pe.wait_ge(wo_in[half], 16)
                        if n >= 3:
                            pe.wait_ge(res_done, n - 2)
                        for k in range(KT):
                            last = pe.matmul(yp[n % 3][:, :], merged[:, k, t * P:(t + 1) * P], wo[:, half, k, :],
                                             start=(k == 0), stop=(k == KT - 1))
                        last.then_inc(out_done, 1)

                def turn(t):
                    pe.wait_ge(h2_ready, t + 1)
                    for half in range(2):
                        if t >= 1:
                            pe.wait_ge(turn_copied, 2 * t + half - 1)
                        for k in range(4):
                            last = pe.transpose(gp[half][:, k * P:(k + 1) * P], h2[:, t, 4 * half + k::KT], ident)
                        last.then_inc(turned, 1)

                def logits(t):
                    pe.wait_ge(turn_copied, 2 * t + 2)
                    for k in range(KT):
                        last = pe.matmul(lp[:, t * NE:(t + 1) * NE], hT[:, k, t * P:(t + 1) * P], wr[:, k, :],
                                         start=(k == 0), stop=(k == KT - 1))
                    last.then_inc(logit_done, 1)

                for t in range(NT):
                    project(t)
                    if t >= 1:
                        turn(t - 1)
                    if t >= 2:
                        logits(t - 2)
                turn(NT - 1)
                logits(NT - 2)
                logits(NT - 1)
                pe.wait_ge(earlier_done, NT)
                pe.matmul(cp[:, 0:NT * NE], cn("before"), mask[:, :, :].rearrange("p t e -> p (t e)"), start=True, stop=False)
                pe.matmul(cp[:, 0:NT * NE], ones, earlier[:, 0:NT, :].rearrange("p t e -> p (t e)"), start=False, stop=True)
                pe.matmul(cp[:, NT * NE:(NT + 1) * NE], ones, earlier[:, NT, :], start=True, stop=True).then_inc(pos_done, 1)

            @block.scalar
            def _(act):
                def copy_turned(t):
                    for half in range(2):
                        act.wait_ge(turned, 2 * t + half + 1)
                        act.activation(hT[:, 4 * half:4 * half + 4, t * P:(t + 1) * P],
                                       gp[half][:, :].rearrange("p (k s) -> p k s", k=4), ACT.Copy).then_inc(turn_copied, 1)

                def before(t):
                    if t >= 1:
                        copy_turned(t - 1)

                layer_norm_act(act, h2, mv, rstd, nmr, epsc[:, 0:1], stats_ready, std_ready, scale_ready, norm_ready, before)
                copy_turned(NT - 1)
                act.wait_ge(logit_done, NT)
                act.activation(sco[:, :, :], lp[:, 0:NT * NE].rearrange("p (t e) -> p t e", t=NT), ACT.Sigmoid).then_inc(score_done, 1)

            @block.vector
            def _(dve):
                chain = Chain(dve, dve_chain)
                dve.memset(far[:, :], FAR).then_inc(far_set, 1)
                chain.add(dve.memset(earlier[:, 0, :], 0.0))
                for c in range(KT):
                    dve.wait_ge(kept_in[c], 32)
                    dve.wait_ge(branch_done, c + 1)
                    dve.tensor_tensor(sig[:, c, :], sig[:, c, :], yp[c % 3][:, :], ALU.mult).then_inc(part_done, 1)
                    dve.wait_ge(part_done, c + 1)
                    dve.tensor_tensor(merged[:, c, :], merged[:, c, :], sig[:, c, :], ALU.add).then_inc(merged_sum, 1)
                def x_ready(t):
                    dve.wait_ge(h_in[t], 16)
                    for half in range(2):
                        n = 2 * t + half
                        dve.wait_ge(out_done, n + 1)
                        r = h2[:, t, half * 512:half * 512 + 512]
                        dve.scalar_tensor_tensor(r, r, ALPHA, yp[n % 3][:, :], ALU.mult, ALU.add).then_inc(res_done, 1)
                    dve.wait_ge(res_done, 2 * t + 2)
                layer_norm_dve(dve, chain, h2, stats, mv, rstd, nmr, x_ready, stats_ready, std_ready, scale_ready,
                               norm_ready, gmul_ready, lng[:, :], ln_in, 0)
                rb = sml[:, SM_RB:SM_RB + NE]
                flat = lambda ap: ap.rearrange("p t (g e) -> p (t g) e", e=EPG)
                dve.wait_ge(score_done, 1)
                chain.link(dve.tensor_tensor(sel[:, :, :], sco[:, :, :], bc(rb, 1, NT), ALU.add))
                sv = flat(sel[:, :, :])
                chain.add(dve.tensor_tensor(hi[:, :, :], sv[:, :, 0::2], sv[:, :, 1::2], ALU.max))
                chain.link(dve.tensor_tensor(lo[:, :, :], sv[:, :, 0::2], sv[:, :, 1::2], ALU.min))
                chain.add(dve.tensor_tensor(g3[:, 0, :], hi[:, :, 0], hi[:, :, 1], ALU.max))
                chain.add(dve.tensor_tensor(g3[:, 1, :], hi[:, :, 0], hi[:, :, 1], ALU.min))
                chain.link(dve.tensor_tensor(g3[:, 2, :], lo[:, :, 0], lo[:, :, 1], ALU.max))
                chain.link(dve.tensor_tensor(g3[:, 1, :], g3[:, 1, :], g3[:, 2, :], ALU.max))
                chain.link(dve.tensor_tensor(g3[:, 0, :], g3[:, 0, :], g3[:, 1, :], ALU.add))
                gs = g3[:, 0, :].rearrange("p (t g) -> p t g", t=NT)
                eq = g3[:, 1, :].rearrange("p (t g) -> p t g", t=NT)
                chain.link(dve.tensor_reduce(gm[:, 0, :], gs, AX.X, ALU.max))
                chain.link(dve.tensor_tensor(eq, gs, bc(gm[:, 0, :], 2, NG), ALU.is_equal))
                chain.link(dve.tensor_tensor(eq, eq, bc(cn("down"), 1, NT), ALU.mult))
                chain.link(dve.tensor_reduce(gm[:, 1, :], eq, AX.X, ALU.max))
                chain.link(dve.tensor_tensor(eq, eq, bc(gm[:, 1, :], 2, NG), ALU.is_equal))
                rk = flat(rank[:, :, :])
                gv = flat(gt[:, :, :])
                chain.link(dve.tensor_copy(rk, bc(cn("place"), 1, NT * NG)))
                for s in range(1, EPG):
                    chain.link(dve.tensor_tensor(gv[:, :, 0:EPG - s], sv[:, :, s:], sv[:, :, 0:EPG - s], ALU.is_gt))
                    chain.link(dve.tensor_tensor(rk[:, :, 0:EPG - s], rk[:, :, 0:EPG - s], gv[:, :, 0:EPG - s], ALU.add))
                    chain.link(dve.tensor_tensor(rk[:, :, s:], rk[:, :, s:], gv[:, :, 0:EPG - s], ALU.subtract))
                for k in range(2):
                    chain.add(dve.scalar_tensor_tensor(flat(onek[:, k, :, :]), rk, float(k), bc(g3[:, 1, :], 2, EPG),
                                                       ALU.is_equal, ALU.mult))
                chain.wait()
                dve.tensor_tensor(mask[:, :, :], onek[:, 0, :, :], onek[:, 1, :, :], ALU.add).then_inc(mask_done, 1)
                dve.wait_ge(mask_done, 1)
                for t in range(NT):
                    dve.tensor_tensor(earlier[:, t + 1, :], earlier[:, t, :], mask[:, t, :], ALU.add).then_inc(earlier_done, 1)
                    if t < NT - 1:
                        dve.wait_ge(earlier_done, t + 1)
                for k in range(2):
                    chain.link(dve.tensor_tensor(prod[:, :, :], onek[:, k, :, :], sco[:, :, :], ALU.mult))
                    chain.link(dve.tensor_reduce(sk[:, k, :], prod[:, :, :], AX.X, ALU.add))
                chain.link(dve.tensor_tensor(sk[:, 2, :], sk[:, 0, :], sk[:, 1, :], ALU.add))
                chain.link(dve.reciprocal(sk[:, 3, :], sk[:, 2, :]))
                for k in range(2):
                    chain.add(dve.tensor_copy(pay[:, :, k, 0], cn("token")))
                    chain.add(dve.tensor_scalar(pay[:, :, k, 1], cn("token"), float(k * SEQ), None, ALU.add))
                    chain.add(dve.memset(pay[:, :, k, 3], 0))
                    chain.add(dve.tensor_tensor(pay[:, :, k, 2].bitcast(F32), sk[:, k, :], sk[:, 3, :], ALU.mult))
                dve.wait_ge(pos_done, 1)
                chain.add(dve.tensor_copy(pos[:, :, :], cp[:, 0:NT * NE].rearrange("p (t e) -> p t e", t=NT)))
                chain.add(dve.tensor_copy(ce[:, 0, :], cp[:, NT * NE:(NT + 1) * NE]))
                chain.add(dve.memset(ce[:, 1, :], 0.0))
                chain.add(dve.memset(ce[:, 4, :], 1.0))
                chain.link(dve.memset(gt[:, :, :], 0.0))
                for b in range(1, SEQ // SLOTS):
                    chain.add(dve.scalar_tensor_tensor(ce[:, 1, :], ce[:, 0, :], float(b * SLOTS), ce[:, 1, :], ALU.is_gt, ALU.add))
                    chain.link(dve.scalar_tensor_tensor(gt[:, :, :], pos[:, :, :], float(b * SLOTS), gt[:, :, :], ALU.is_ge, ALU.add))
                chain.link(dve.tensor_tensor_scan(ce[:, 2, :], ce[:, 4, :], ce[:, 1, :], 0.0, ALU.mult, ALU.add))
                chain.link(dve.tensor_tensor(ce[:, 3, :], ce[:, 2, :], ce[:, 1, :], ALU.subtract))
                chain.add(dve.tensor_tensor(eo[:, :, :], bc(ce[0:1, 2, :], 1, OVER), bc(cn("expert", 1)[:, 0:OVER], 2, NE), ALU.is_le))
                chain.link(dve.scalar_tensor_tensor(pos[:, :, :], gt[:, :, :], -float(SLOTS), pos[:, :, :], ALU.mult, ALU.add))
                chain.link(dve.tensor_reduce(eov[:, 1:1 + OVER], eo[:, :, :], AX.X, ALU.add))
                chain.link(dve.tensor_scalar(eov[:, 1:1 + OVER], eov[:, 1:1 + OVER], float(NE - 1), None, ALU.min))
                chain.link(dve.tensor_copy(eov[:, 0:1], ce[0:1, 2, NE - 1:NE]))
                chain.add(dve.tensor_copy(flag[:, :], eov[:, :]))
                chain.link(dve.scalar_tensor_tensor(dest[:, :, :], pos[:, :, :], float(NE), bc(cn("expert"), 1, NT), ALU.mult, ALU.add))
                chain.link(dve.scalar_tensor_tensor(alt[:, :, :], pos[:, :, :], float(OVER), gt[:, :, :], ALU.mult, ALU.add))
                chain.link(dve.tensor_tensor(alt[:, :, :], alt[:, :, :], bc(ce[:, 3, :], 1, NT), ALU.add))
                chain.link(dve.scalar_tensor_tensor(alt[:, :, :], alt[:, :, :], float(SLOTS * NE - 1), dest[:, :, :], ALU.add, ALU.subtract))
                chain.link(dve.scalar_tensor_tensor(alt[:, :, :], gt[:, :, :], 1.0, alt[:, :, :], ALU.min, ALU.mult))
                chain.link(dve.tensor_tensor(dest[:, :, :], dest[:, :, :], alt[:, :, :], ALU.add))
                for k in range(2):
                    chain.link(dve.tensor_tensor(prod[:, :, :], onek[:, k, :, :], dest[:, :, :], ALU.mult))
                    chain.link(dve.tensor_reduce(dk[:, k, :], prod[:, :, :], AX.X, ALU.add))
                dve.tensor_copy(dki[:, :, :], dk[:, :, :]).then_inc(pay_done, 1)
                dve.memset(rows_all[:, NE + OVER, :], FAR)

            @block.gpsimd
            def _(pool):
                v["zero_last"](pool)
                for t in range(NT):
                    pool.wait_ge(gmul_ready, t + 1)
                    pool.wait_ge(ln_in, 32)
                    pool.tensor_tensor(h2[:, t, :], h2[:, t, :], lnb[:, :], ALU.add).then_inc(h2_ready, 1)
                pool.wait_ge(pay_done, 1)
                pool.wait_ge(far_out, 16)
                for t in range(NT):
                    for k in range(2):
                        pool.indirect_dma_start(v["slots_dram"], bass.IndirectOffsetOnAxis(ap=dki[:, k, t:t + 1], axis=0),
                                                pay[:, t, k, :], None, bounds_check=TABLE - 1, oob_is_err=False).then_inc(scattered, 16)
                pool.wait_ge(scattered, 16 * 2 * NT)


def experts(nc, sem, sb, pb, cn, v):
    rows_all, flag = v["rows_all"], v["flag"]
    w1, w3, w2 = (v[k] for k in ("moe_w1", "moe_w3", "moe_w2"))
    ident = v["ident"]
    w_dram = [w1.rearrange("e (p k) n -> e p (k n)", p=P), w3.rearrange("e (p k) n -> e p (k n)", p=P),
              w2.rearrange("e (p k) n -> e p (k n)", p=P)]
    FT = FE // P
    UNITS = 6
    st = ExitStack()
    with st:
        raw = v["wraw"]
        whi, wlo = sb(st, "whi", [P, NSPLIT, HALF], F32R), sb(st, "wlo", [P, NSPLIT, HALF], F32R)
        xg = sb(st, "xg", [SLOTS, 2, DM])
        tok = sb(st, "tok", [SLOTS, 2, 1], I32)
        idx = sb(st, "idx", [SLOTS, 2, 1], I32)
        gate = sb(st, "gate", [P, 2, 1])
        xs = sb(st, "xs", [P, 2, KT, 2, SLOTS], F32R)
        hc = sb(st, "hc", [P, 2, FE])
        sl = sb(st, "sl", [P, FT * SLOTS])
        prd = sb(st, "prd", [P, FT * SLOTS])
        ac = sb(st, "ac", [P, FT, 2, SLOTS], F32R)
        ylow = sb(st, "ylow", [SLOTS, DM])
        ys = sb(st, "ys", [SLOTS, 2, DM])
        tx, gb = pb(st, "tx"), pb(st, "gb")
        hb = [pb(st, f"hb{i}") for i in range(4)]
        yb = [pb(st, f"yb{i}") for i in range(2)]

        class Signals:

            def __init__(self, tag):
                self.w_in = [sem(f"{tag}_w_in{i}") for i in range(6)]
                self.gathered = [sem(f"{tag}_gathered{i}") for i in range(2)]
                self.hi_done = sem(f"{tag}_hi_done")
                self.lo_done = sem(f"{tag}_lo_done")
                self.part_used = sem(f"{tag}_part_used")
                self.gate_ready = sem(f"{tag}_gate_ready")
                self.row_ready = sem(f"{tag}_row_ready")
                self.index_ready = sem(f"{tag}_index_ready")
                self.x_turned = sem(f"{tag}_x_turned")
                self.xhi_done = sem(f"{tag}_xhi_done")
                self.xlo_done = sem(f"{tag}_xlo_done")
                self.h_copied = sem(f"{tag}_h_copied")
                self.paired = sem(f"{tag}_paired")
                self.silu_done = sem(f"{tag}_silu_done")
                self.act_done = sem(f"{tag}_act_done")
                self.ahi_done = sem(f"{tag}_ahi_done")
                self.alo_done = sem(f"{tag}_alo_done")
                self.ylow_ready = sem(f"{tag}_ylow_ready")
                self.y_ready = sem(f"{tag}_y_ready")
                self.scattered = sem(f"{tag}_scattered")
                self.stored = sem(f"{tag}_stored")
                self.steps_begun = sem(f"{tag}_steps_begun")
                self.turns_begun = sem(f"{tag}_turns_begun")

        def wait(eng, s, value):
            if not (isinstance(value, int) and value <= 0):
                eng.wait_ge(s, value)

        def blocks(eng, count, step):
            for e in range(2):
                step(e, e, 0)
            with eng.Fori(1, count // 2) as it:
                for j in range(2):
                    step(it * 2 + j, j, it)

        W1, W2, W3 = (0, 1), (2, 3), (4, 5)

        def sync_program(sp, S, count, expert, begun):
            def load(e, u, which, ex, half):
                if begun and isinstance(e, int) and e == 0:
                    sp.sem_inc(S.w_in[u], 16)
                    return
                wait(sp, S.lo_done, e * UNITS + (u + 1 - NRAW))
                sp.dma_start(raw[:, u, :], w_dram[which][bass.ds(ex, 1), :, half * HALF:(half + 1) * HALF].rearrange("o p n -> (o p) n"))\
                    .then_inc(S.w_in[u], 16)

            def step(e, j, it):
                ex = expert(sp, e)
                before = ex if isinstance(e, int) and e == 0 else expert(sp, e - 1)
                for half in range(2):
                    load(e, W1[half], 0, ex, half)
                for half in range(2):
                    load(e, W2[half], 2, before, half)
                for half in range(2):
                    load(e, W3[half], 1, ex, half)
            blocks(sp, count, step)
            last = expert(sp, count - 1)
            for half in range(2):
                load(count, half, 2, last, half)

        def pool_program(pool, S, count, first):
            def fetch(e, j):
                wait(pool, S.x_turned, e - 1)
                pool.tensor_copy(tok[:, j, :], rows_all[0:SLOTS, bass.ds(e + first, 1), 0:1].rearrange("p o w -> p (o w)")).then_inc(S.index_ready, 1)
                wait(pool, S.index_ready, e + 1)
                pool.sem_inc(S.steps_begun, 1)
                pool.indirect_dma_start(xg[:, j, :], None, v["h2_dram"], bass.IndirectOffsetOnAxis(ap=tok[:, j, :], axis=0),
                                        bounds_check=SEQ - 1, oob_is_err=False).then_inc(S.gathered[j], 16)

            def store(e, j):
                pool.tensor_copy(gate[:, j, :], rows_all[:, bass.ds(e + first, 1), 2:3].bitcast(F32).rearrange("p o w -> p (o w)"))\
                    .then_inc(S.gate_ready, 1)
                pool.tensor_copy(idx[:, j, :], rows_all[0:SLOTS, bass.ds(e + first, 1), 1:2].rearrange("p o w -> p (o w)")).then_inc(S.row_ready, 1)
                wait(pool, S.row_ready, e + 1)
                pool.wait_ge(S.y_ready, e * 2 + 2)
                pool.sem_inc(S.steps_begun, 1)
                pool.indirect_dma_start(v["y_dram"], bass.IndirectOffsetOnAxis(ap=idx[:, j, :], axis=0),
                                        ys[:, j, :], None, bounds_check=2 * SEQ - 1, oob_is_err=False).then_inc(S.scattered, 16)
                pool.wait_ge(S.scattered, e * 16 + 16)
                pool.sem_inc(S.stored, 1)

            def step(e, j, it):
                fetch(e + 1, 1 - j)
                if not (isinstance(e, int) and e == 0):
                    store(e - 1, 1 - j)
            fetch(0, 0)
            blocks(pool, count, step)
            store(count - 1, 1)
            pool.wait_ge(S.gathered[0], 16 * (count // 2 + 1))

        def tensor_program(pe, S, count):
            def turn(e, j, round_):
                wait(pe, S.xlo_done, e)
                pe.wait_ge(S.gathered[j], round_ * 16 + 16)
                pe.sem_inc(S.turns_begun, 1)
                for k in range(KT):
                    last = pe.transpose(tx[:, k * SLOTS:(k + 1) * SLOTS], xg[:, j, k::KT], ident[0:SLOTS, 0:SLOTS])
                last.then_inc(S.x_turned, 1)

            def first_products(e, j, u, w, half):
                part = (UNITS * j + u) % NSPLIT
                bank = hb[2 * j + w]
                pe.wait_ge(S.lo_done, e * UNITS + (u + 1))
                for kk in range(4):
                    lhs = xs[:, j, 4 * half + kk, :, :].rearrange("p a s -> p (a s)")
                    cols = slice(kk * FE, (kk + 1) * FE)
                    pe.matmul(bank[:, :], lhs, whi[:, part, cols], start=(half == 0 and kk == 0), stop=False)
                    last = pe.matmul(bank[:, :], lhs, wlo[:, part, cols], start=False, stop=(half == 1 and kk == 3))
                last.then_inc(S.part_used, 1)

            def add_pairs(e):
                for w in range(2):
                    pe.wait_ge(S.h_copied, e * 2 + (w + 1))
                    for f in range(FT):
                        last = pe.matmul(gb[:, (w * FT + f) * SLOTS:(w * FT + f + 1) * SLOTS], hc[:, w, f::FT], cn("pair"),
                                         start=True, stop=True)
                last.then_inc(S.paired, 1)

            def second_products(e, body, bj, u, half):
                part = (UNITS * bj + u) % NSPLIT
                pe.wait_ge(S.alo_done, e + 1)
                wait(pe, S.y_ready, e * 2)
                pe.wait_ge(S.lo_done, body * UNITS + (u + 1))
                for kk in range(2):
                    k = 2 * half + kk
                    lhs = ac[:, k, :, :].rearrange("p a s -> p (a s)")
                    for c in range(2):
                        cols = slice(kk * DM + c * 512, kk * DM + c * 512 + 512)
                        pe.matmul(yb[c][:, :], lhs, whi[:, part, cols], start=(k == 0), stop=False)
                        last = pe.matmul(yb[c][:, :], lhs, wlo[:, part, cols], start=False, stop=(k == FT - 1))
                last.then_inc(S.part_used, 1)

            def step(e, j, it):
                head = isinstance(e, int) and e == 0
                pe.wait_ge(S.xlo_done, e + 1)
                first_products(e, j, W1[0], 0, 0)
                if not head:
                    add_pairs(e - 1)
                first_products(e, j, W1[1], 0, 1)
                for half in range(2):
                    if head:
                        pe.wait_ge(S.lo_done, W2[half] + 1)
                        pe.wait_ge(S.part_used, W2[half])
                        pe.sem_inc(S.part_used, 1)
                    else:
                        second_products(e - 1, e, j, W2[half], half)
                first_products(e, j, W3[0], 1, 0)
                turn(e + 1, 1 - j, it + j)
                first_products(e, j, W3[1], 1, 1)
            turn(0, 0, 0)
            blocks(pe, count, step)
            add_pairs(count - 1)
            for half in range(2):
                second_products(count - 1, count, 0, half, half)

        def scalar_program(act, S, count):
            def high(e, j, u):
                act.wait_ge(S.w_in[u], e * 16 + 16)
                wait(act, S.part_used, e * UNITS + (u + 1 - NSPLIT))
                act.activation(whi[:, (UNITS * j + u) % NSPLIT, :], raw[:, u, :], ACT.Copy).then_inc(S.hi_done, 1)

            def x_high(e, j):
                act.wait_ge(S.x_turned, e + 1)
                wait(act, S.part_used, e * UNITS - UNITS)
                act.activation(xs[:, j, :, 0, :], tx[:, :].rearrange("p (k s) -> p k s", k=KT), ACT.Copy).then_inc(S.xhi_done, 1)

            def copy_h(e, j, w):
                act.wait_ge(S.part_used, e * UNITS + ((W1, W3)[w][1] + 1))
                act.activation(hc[:, w, :], hb[2 * j + w][:, :], ACT.Copy).then_inc(S.h_copied, 1)

            def gated(e):
                act.wait_ge(S.paired, e + 1)
                act.activation(sl[:, :], gb[:, 0:FT * SLOTS], ACT.Silu).then_inc(S.silu_done, 1)

            def act_high(e):
                act.wait_ge(S.act_done, e + 1)
                wait(act, S.part_used, e * UNITS + (W2[1] + 1))
                act.activation(ac[:, :, 0, :], prd[:, :].rearrange("p (f s) -> p f s", f=FT), ACT.Copy).then_inc(S.ahi_done, 1)

            def weigh_y(e, j, used):
                act.wait_ge(S.part_used, used)
                wait(act, S.y_ready, e * 2)
                act.wait_ge(S.gate_ready, e + 1)
                for half in range(2):
                    act.activation(ylow[:, half * 512:half * 512 + 512], yb[half][SLOTS:, :], ACT.Copy, scale=gate[SLOTS:, j, 0:1])\
                        .then_inc(S.ylow_ready, 1)

            def step(e, j, it):
                head = isinstance(e, int) and e == 0
                high(e, j, 0)
                high(e, j, 1)
                if not head:
                    copy_h(e - 1, 1 - j, 1)
                high(e, j, 2)
                high(e, j, 3)
                if not head:
                    gated(e - 1)
                    act_high(e - 1)
                high(e, j, 4)
                copy_h(e, j, 0)
                high(e, j, 5)
                if not head:
                    weigh_y(e - 1, 1 - j, e * UNITS + (W2[1] + 1))
                x_high(e + 1, 1 - j)
            x_high(0, 0)
            blocks(act, count, step)
            high(count, 0, 0)
            high(count, 0, 1)
            copy_h(count - 1, 1, 1)
            gated(count - 1)
            act_high(count - 1)
            weigh_y(count - 1, 1, count * UNITS + 2)

        def vector_program(dve, S, count):
            def low(e, j, u):
                part = (UNITS * j + u) % NSPLIT
                dve.wait_ge(S.hi_done, e * UNITS + (u + 1))
                dve.tensor_tensor(wlo[:, part, :], raw[:, u, :], whi[:, part, :].bitcast(F32), ALU.subtract).then_inc(S.lo_done, 1)

            def x_low(e, j):
                dve.wait_ge(S.xhi_done, e + 1)
                dve.tensor_tensor(xs[:, j, :, 1, :], tx[:, :].rearrange("p (k s) -> p k s", k=KT),
                                  xs[:, j, :, 0, :].bitcast(F32), ALU.subtract).then_inc(S.xlo_done, 1)

            def product(e):
                dve.wait_ge(S.silu_done, e + 1)
                dve.tensor_tensor(prd[:, :], sl[:, :], gb[:, FT * SLOTS:2 * FT * SLOTS], ALU.mult).then_inc(S.act_done, 1)
                dve.wait_ge(S.ahi_done, e + 1)
                dve.tensor_tensor(ac[:, :, 1, :], prd[:, :].rearrange("p (f s) -> p f s", f=FT),
                                  ac[:, :, 0, :].bitcast(F32), ALU.subtract).then_inc(S.alo_done, 1)

            def sum_y(e, j):
                wait(dve, S.stored, e - 1)
                for half in range(2):
                    cols = slice(half * 512, half * 512 + 512)
                    dve.wait_ge(S.ylow_ready, e * 2 + (half + 1))
                    dve.scalar_tensor_tensor(ys[:, j, cols], yb[half][0:SLOTS, :], gate[0:SLOTS, j, 0:1], ylow[:, cols],
                                             ALU.mult, ALU.add).then_inc(S.y_ready, 1)

            def step(e, j, it):
                head = isinstance(e, int) and e == 0
                low(e, j, 0)
                low(e, j, 1)
                low(e, j, 2)
                if not head:
                    product(e - 1)
                low(e, j, 3)
                low(e, j, 4)
                if not head:
                    sum_y(e - 1, 1 - j)
                low(e, j, 5)
                x_low(e + 1, 1 - j)
            x_low(0, 0)
            blocks(dve, count, step)
            low(count, 0, 0)
            low(count, 0, 1)
            product(count - 1)
            sum_y(count - 1, 1)

        zeroed = sem("moe_zeroed")
        first_blocks, more_blocks = Signals("moe"), Signals("over")
        with nc.Block() as block:
            S = first_blocks

            @block.sync
            def _(sp):
                sync_program(sp, S, NE, lambda eng, e: e, True)

            @block.gpsimd
            def _(pool):
                v["zero_last"](pool)
                pool.memset(xg[:, :, :], 0.0).then_inc(zeroed, 1)
                pool.wait_ge(zeroed, 1)
                pool_program(pool, S, NE, 0)

            @block.tensor
            def _(pe):
                tensor_program(pe, S, NE)

            @block.scalar
            def _(act):
                scalar_program(act, S, NE)

            @block.vector
            def _(dve):
                vector_program(dve, S, NE)

        def any_more(eng):
            return eng.value_load(flag[0:1, 0:1], min_val=0, max_val=OVER) > 0

        with nc.Block() as block:
            S2 = more_blocks

            @block.sync
            def _(sp):
                with sp.If(any_more(sp)):
                    sync_program(sp, S2, OVER, lambda eng, e: eng.value_load(flag[0:1, bass.ds(e + 1, 1)], min_val=0, max_val=NE - 1), False)

            @block.gpsimd
            def _(pool):
                with pool.If(any_more(pool)):
                    pool_program(pool, S2, OVER, NE)

            @block.tensor
            def _(pe):
                with pe.If(any_more(pe)):
                    tensor_program(pe, S2, OVER)

            @block.scalar
            def _(act):
                with act.If(any_more(act)):
                    scalar_program(act, S2, OVER)

            @block.vector
            def _(dve):
                with dve.If(any_more(dve)):
                    vector_program(dve, S2, OVER)


def final(nc, sem, sb, pb, cn, v):
    h2, epsc = v["h2"], v["epsc"]
    st = ExitStack()
    with st:
        yr = sb(st, "yr", [P, NT, 2, DM])
        lng, lnb = sb(st, "lng3", [P, DM]), sb(st, "lnb3", [P, DM])
        stats, mv, rstd, nmr = sb(st, "stats3", [P, NT, 2, 6]), sb(st, "mv3", [P, NT, 2]), sb(st, "rstd3", [P, NT]), sb(st, "nmr3", [P, NT])
        y_in = [sem(f"y_in{t}") for t in range(NT)]
        ln_in, summed, out_done = sem("ln3_in"), sem("fin_summed"), sem("out_done")
        stats_ready, std_ready, scale_ready, norm_ready, gmul_ready, o_ready = (
            sem(f"ln3_{n}") for n in ("stats", "std", "scale", "norm", "gmul", "o"))
        dve_chain = sem("fin_dve_chain")
        with nc.Block() as block:
            @block.sync
            def _(sp):
                for t in range(NT):
                    sp.dma_start(yr[:, t, :, :], v["y_dram"].rearrange("(q s) d -> s q d", q=2)[t * P:(t + 1) * P, :, :]).then_inc(y_in[t], 16)
                    if t == 0:
                        sp.dma_start(lng[:, :], v["ln_ffn_g"].to_broadcast([P, DM])).then_inc(ln_in, 16)
                        sp.dma_start(lnb[:, :], v["ln_ffn_b"].to_broadcast([P, DM])).then_inc(ln_in, 16)
                for t in range(NT):
                    sp.wait_ge(o_ready, t + 1)
                    sp.dma_start(v["out"][t * P:(t + 1) * P, :], h2[:, t, :]).then_inc(out_done, 16)
                sp.wait_ge(out_done, 16 * NT)

            @block.scalar
            def _(act):
                layer_norm_act(act, h2, mv, rstd, nmr, epsc[:, 0:1], stats_ready, std_ready, scale_ready, norm_ready)

            @block.vector
            def _(dve):
                chain = Chain(dve, dve_chain)

                def x_ready(t):
                    dve.wait_ge(y_in[t], 16)
                    r = h2[:, t, :]
                    chain.link(dve.scalar_tensor_tensor(r, r, ALPHA, yr[:, t, 0, :], ALU.mult, ALU.add))
                    chain.link(dve.tensor_tensor(r, r, yr[:, t, 1, :], ALU.add))
                layer_norm_dve(dve, chain, h2, stats, mv, rstd, nmr, x_ready, stats_ready, std_ready, scale_ready,
                               norm_ready, gmul_ready, lng[:, :], ln_in, 1)

            @block.gpsimd
            def _(pool):
                v["zero_last"](pool)
                for t in range(NT):
                    pool.wait_ge(gmul_ready, t + 1)
                    pool.tensor_tensor(h2[:, t, :], h2[:, t, :], lnb[:, :], ALU.add).then_inc(o_ready, 1)


def kernel(**inputs):
    import numpy as _np
    import concourse.bacc as _bacc
    from concourse import mybir as _mybir
    from concourse.bass_utils import run_bass_kernel_spmd as _run

    a = {k: _np.asarray(v) for k, v in inputs.items()}
    rows = lambda t: _np.broadcast_to(_np.reshape(t, (1, -1)), (P, t.size))
    by_part = lambda t: _np.reshape(t, (P, -1))
    column = lambda t: _np.reshape(t, (-1, P)).T
    w_in = a["w_in"][0]
    gate_cols = _np.concatenate([w_in[:, C_A:C_A + 16], w_in[:, C_I:C_I + 16]], axis=1)
    small = _np.concatenate([
        _np.reshape(_np.transpose(_np.reshape(a["dn_conv_w"][0], (TAPS, 12, P)), (2, 1, 0)), (P, 60)),
        column(a["dn_norm_w"][0]), column(a["pool_scale"][0]), column(a["ml_norm_w"][0]),
        by_part(gate_cols), rows(a["dn_a_log"][0]), rows(a["dn_dt_bias"][0]), rows(a["ml_gate_b"][0]),
        rows(a["router_b"]), by_part(a["router_w"])], axis=1)
    arrays = {
        "x": a["x"][0], "ln_in_g": a["ln_in_g"][None], "ln_in_b": a["ln_in_b"][None], "w_in": w_in,
        "pool_w": a["pool_w"][0], "w_branch": a["w_branch"][0], "w_out": a["w_out"][0],
        "ln_mix_g": a["ln_mix_g"], "ln_mix_b": a["ln_mix_b"], "moe_w1": a["moe_w1"][0], "moe_w3": a["moe_w3"][0],
        "moe_w2": a["moe_w2"][0], "ln_ffn_g": a["ln_ffn_g"], "ln_ffn_b": a["ln_ffn_b"],
        "const": _np.concatenate(list(CONST.values()), axis=1), "small": small,
    }
    nc = _bacc.Bacc("TRN2", target_bir_lowering=False, num_devices=1)
    feed, args = {}, []
    for name, t in arrays.items():
        if name.startswith("ln_") and t.ndim == 1:
            t = t[None]
        t = _np.ascontiguousarray(t)
        feed[f"in_{name}"] = t
        args.append(nc.dram_tensor(f"in_{name}", t.shape, _mybir.dt.from_np(t.dtype), kind="ExternalInput").ap())
    args.append(nc.dram_tensor("result", (SEQ, DM), _mybir.dt.float32, kind="ExternalOutput").ap())
    hybrid_encoder(nc, *args)
    r = _run(nc, [feed], core_ids=[0])
    return _np.reshape(r.results[0]["result"], (1, SEQ, DM))
```

```python
import concourse.bass as bass
from concourse import mybir
from concourse.alu_op_type import AluOpType as ALU
from contextlib import ExitStack
import numpy as np

F32 = mybir.dt.float32
F32R = mybir.dt.float32r
I32 = mybir.dt.int32
ACT = mybir.ActivationFunctionType
AX = mybir.AxisListType

P = 128
SEQ, DM = 512, 1024
NT = SEQ // P
KT = DM // P
MW = DM // 2
NH = 4
DV = MW // NH
QK = DV // 2
TAPS = 5
LN_EPS, NORM_EPS = 1e-5, 1e-6
ALPHA = 2.0 ** 0.25
NE, NG = 32, 8
EPG = NE // NG
FE = DM // 2
SLOTS = 64
WC = KT * FE
HALF = WC // 2
NRAW, NSPLIT = 6, 4
OVER = (2 * SEQ) // SLOTS
TABLE = SLOTS * (NE + OVER)
FAR = 1 << 20
NEG = -1.0e30

OFF = np.cumsum([0, 3 * MW, MW, 2 * NH, 2 * NH, MW, NH * QK, NH * QK, MW, MW, 2 * NH, 2 * NH, 3 * DM])
C_Q, C_K, C_V, C_Z, C_A, C_U, C_MQ, C_MV, C_MO, C_I, C_G = (
    0, MW, 2 * MW, int(OFF[1]), int(OFF[2]), int(OFF[4]), int(OFF[5]), int(OFF[7]), int(OFF[8]), int(OFF[9]), int(OFF[11]))
LEVELS = [1, 2, 4, 8, 16, 32, 64]
NL = len(LEVELS)


def constants():
    i = np.arange(P)[None, :]
    j = np.arange(P)[:, None]
    upto, after = (j <= i), (j >= i)
    cols = {"ident": np.eye(P), "ones": np.ones((P, P)), "upto": upto, "after": after,
            "neg_fwd": np.where(upto, 0.0, NEG), "neg_bwd": np.where(after, 0.0, NEG),
            "before": j < i}
    for d in range(2):
        for b in LEVELS:
            same = (i // (2 * b)) == (j // (2 * b))
            first_j, first_i = (j // b) % 2 == 0, (i // b) % 2 == 0
            cols[f"level{d}_{b}"] = same & (first_j & ~first_i if d == 0 else first_i & ~first_j)
    edge = np.zeros((P, 4, 16))
    for g, win in enumerate((2, 4, 8, 16)):
        half = win // 2
        for n in range(8):
            edge[:, g, n] = 1.0 / (min(n + half, SEQ) - max(n - half, 0))
            m = SEQ - 8 + n
            edge[:, g, 8 + n] = 1.0 / (min(m + half, SEQ) - max(m - half, 0))
    cols["edge"] = edge.reshape(P, 64)
    cols["pair"] = (i[:, 0:SLOTS] == j % SLOTS)
    cols["down"] = np.tile(np.arange(NG, 0, -1.0), (P, 1))
    cols["place"] = np.tile(np.arange(4.0), (P, 1))
    cols["expert"] = np.tile(np.arange(32.0), (P, 1))
    cols["token"] = np.arange(NT)[None, :] * P + j
    return {k: np.asarray(v, np.float32) for k, v in cols.items()}


CONST = constants()
COFF, NCONST = {}, 0
for _key, _table in CONST.items():
    COFF[_key] = (NCONST, _table.shape[1])
    NCONST += _table.shape[1]


PRODUCTS = ((0, 0), (0, 1), (1, 0))


class Chain:

    def __init__(self, eng, sem):
        self.eng, self.sem, self.n, self.base = eng, sem, 0, 0

    def add(self, ins):
        self.n += 1
        ins.then_inc(self.sem, 1)
        return ins

    def wait(self):
        self.eng.wait_ge(self.sem, self.base + self.n)

    def link(self, ins):
        self.add(ins)
        self.wait()


def bc(ap, dim, n):
    v = ap.unsqueeze(dim)
    shape = list(v.shape)
    shape[dim] = n
    return v.to_broadcast(shape)


SM_CONV, SM_NORM, SM_W, SM_BIAS, SM_RB, SM_RW = 0, 60, 72, 328, 360, 392
SM_COLS = 392 + KT * NE


def hybrid_encoder(nc, x, ln_in_g, ln_in_b, w_in, pool_w, w_branch, w_out, ln_mix_g, ln_mix_b,
                   moe_w1, moe_w3, moe_w2, ln_ffn_g, ln_ffn_b, const, small, out):
    root = ExitStack()
    stages = [[]]

    def sem(name):
        stages[-1].append(nc.alloc_semaphore(name))
        return stages[-1][-1]

    def zero_last(pool):
        if len(stages) > 1:
            numbers = sorted(s.num for s in stages[-2])
            while numbers:
                n = 1
                while n < len(numbers) and numbers[n] == numbers[0] + n:
                    n += 1
                pool.sem_clear(range(numbers[0], numbers[0] + n))
                numbers = numbers[n:]

    def next_stage():
        if len(stages) > 1:
            for s in stages[-2]:
                nc.release_semaphore(s)
        stages.append([])

    h2_dram = nc.dram_tensor("h2_dram", (SEQ, DM), F32, kind="Internal").ap()
    h_dram = nc.dram_tensor("h_dram", (SEQ, DM), F32, kind="Internal").ap()
    kept_dram = nc.dram_tensor("kept_dram", (2, KT, P, SEQ), F32, kind="Internal").ap()
    slots_dram = nc.dram_tensor("slots_dram", (TABLE, 4), I32, kind="Internal").ap()
    y_dram = nc.dram_tensor("y_dram", (2 * SEQ, DM), F32, kind="Internal").ap()
    with root:
        def sb(stack, name, shape, dt=F32, side=None):
            return stack.enter_context(nc.sbuf_tensor(name, shape, dt, side=side))

        def pb(stack, name, shape=(P, 512), dt=F32):
            return stack.enter_context(nc.psum_tensor(name, list(shape), dt))

        cst = sb(root, "cst", [P, NCONST])
        sml = sb(root, "sml", [P, SM_COLS])
        epsc = sb(root, "epsc", [P, 4])

        def cn(name, rows=P):
            a, n = COFF[name]
            return cst[0:rows, a:a + n]

        ident, ones = cn("ident"), cn("ones")
        h2 = sb(root, "h2", [P, NT, DM])
        rows_all = sb(root, "rows_all", [P, NE + OVER + 1, 4], I32)
        flag = sb(root, "flag", [1, 1 + OVER], I32)
        mixer = ExitStack()
        h_part = [sb(mixer, f"h_part{i}", [P, KT, SEQ], F32R) for i in range(2)]
        yT = sb(mixer, "yT", [P, 3, NH, SEQ])
        attention = ExitStack()
        qkT = sb(attention, "qkT", [P, 2, NH, SEQ])
        kTok = sb(attention, "kTok", [P, NT, NH, DV])
        vTok = sb(attention, "vTok", [P, NT, NH, DV])
        beta = sb(attention, "beta", [P, NT, 8])
        cum = sb(attention, "cum", [P, NT, 24])
        gg = sb(attention, "gg", [P, NT, 24])
        mstack = ExitStack()
        mk = sb(mstack, "mk", [P, 2, SEQ])
        mq = sb(mstack, "mq", [P, NH, SEQ])
        mvx = sb(mstack, "mvx", [P, NT, NH, DV + 1])
        mrow = sb(mstack, "mrow", [P, 2, SEQ])
        acol = sb(mstack, "acol", [P, NT, 8])
        emx = sb(mstack, "emx", [P, NT, 8])

        rooms = h2[:, :, :].rearrange("p a b -> p (a b)")
        gw = [rooms[:, KT * P * i:KT * P * (i + 1)].rearrange("p (k n) -> p k n", k=KT) for i in range(2)]
        bw = [rooms[:, 2 * KT * P + NH * P * i:2 * KT * P + NH * P * (i + 1)].rearrange("p (k n) -> p k n", k=NH) for i in range(2)]
        w_rows = w_in.rearrange("(p k) n -> p k n", k=KT)

        front(nc, sem, sb, pb, cn, locals())
        next_stage()
        mlstm(nc, sem, sb, pb, cn, locals())
        next_stage()
        mstack.close()
        deltanet(nc, sem, sb, pb, cn, locals())
        next_stage()
        attention.close()
        wraw = sb(root, "wraw", [P, NRAW, HALF], side="right")
        merge(nc, sem, sb, pb, cn, locals())
        next_stage()
        mixer.close()
        experts(nc, sem, sb, pb, cn, locals())
        next_stage()
        final(nc, sem, sb, pb, cn, locals())


def layer_norm_dve(dve, chain, src, stats, mv, rstd, nmr, x_ready, stats_ready, std_ready, scale_ready,
                   norm_ready, gmul_ready, g, ln_in, lag):
    for step in range(NT + lag):
        t = step
        if t < NT:
            x_ready(t)
            for half in range(2):
                chain.add(dve.bn_stats(stats[:, t, half, :], src[:, t, 512 * half:512 * half + 512]))
            chain.wait()
            dve.bn_aggr(mv[:, t, :], stats[:, t, :, :]).then_inc(stats_ready, 1)
            dve.wait_ge(std_ready, t + 1)
            chain.link(dve.reciprocal(rstd[:, t:t + 1], rstd[:, t:t + 1]))
            dve.wait_ge(stats_ready, t + 1)
            dve.tensor_scalar(nmr[:, t:t + 1], mv[:, t, 0:1], rstd[:, t:t + 1], -1.0, ALU.mult, ALU.mult).then_inc(scale_ready, 1)
        t = step - lag
        if t >= 0:
            if t == 0:
                dve.wait_ge(ln_in, 32)
            dve.wait_ge(norm_ready, t + 1)
            dve.tensor_tensor(src[:, t, :], src[:, t, :], g, ALU.mult).then_inc(gmul_ready, 1)


def layer_norm_act(act, src, mv, rstd, nmr, eps, stats_ready, std_ready, scale_ready, norm_ready, between=None):
    for t in range(NT):
        if between is not None:
            between(t)
        act.wait_ge(stats_ready, t + 1)
        act.activation(rstd[:, t:t + 1], mv[:, t, 1:2], ACT.Sqrt, bias=eps).then_inc(std_ready, 1)
        act.wait_ge(scale_ready, t + 1)
        act.activation(src[:, t, :], src[:, t, :], ACT.Identity, scale=rstd[:, t:t + 1],
                       bias=nmr[:, t:t + 1]).then_inc(norm_ready, 1)


def front(nc, sem, sb, pb, cn, v):
    x, w_in, small, const = v["x"], v["w_in"], v["small"], v["const"]
    cst, sml, epsc, yT, qkT = (v[k] for k in ("cst", "sml", "epsc", "yT", "qkT"))
    mk = v["mk"]
    kTok, vTok, beta, cum, gg, mq, mvx, mrow, acol, emx = (
        v[k] for k in ("kTok", "vTok", "beta", "cum", "gg", "mq", "mvx", "mrow", "acol", "emx"))
    ident, ones = v["ident"], v["ones"]
    st = ExitStack()
    with st:
        h = v["h2"]
        raw_rooms = [r[:, :, :, :].rearrange("p t h e -> p (t h e)").rearrange("p (k n) -> p k n", k=KT) for r in (kTok, vTok)]
        raw_rooms += [h[:, 2 * i:2 * i + 2, :].rearrange("p a b -> p (a b)").rearrange("p (k n) -> p k n", k=KT) for i in range(2)]
        wsplit = sb(st, "wsplit", [P, 2, 2, KT, 256], F32R)
        w_part = [[wsplit[:, r, i, :, :] for i in range(2)] for r in range(2)]
        h_part = v["h_part"]
        wssplit = sb(st, "wssplit", [P, 2, KT, 32], F32R)
        ws_part = [wssplit[:, i, :, :] for i in range(2)]
        lng = yT[:, 2, 0:2, :].rearrange("p a b -> p (a b)")
        lnb = yT[:, 2, 2:4, :].rearrange("p a b -> p (a b)")
        stats, mv, rstd, nmr = sb(st, "stats", [P, NT, 2, 6]), sb(st, "mv", [P, NT, 2]), sb(st, "rstd", [P, NT]), sb(st, "nmr", [P, NT])
        raw = sb(st, "raw", [P, 3, SEQ + 4])
        cv = sb(st, "cv", [P, 3, SEQ])
        sp = sb(st, "sp", [P, 3, NT, 16])
        ab = sb(st, "ab", [P, NT, 32])
        others = sb(st, "others", [P, NT, 8])
        pw = sb(st, "pw", [P, NH, DV])
        up = sb(st, "up", [P, 528])
        win = sb(st, "win", [P, 2, 528])
        vT = yT[:, 0, :, :]
        sq, nrm = sb(st, "sq", [P, 2, SEQ]), sb(st, "nrm", [P, 2, SEQ])
        tp = [pb(st, f"tp{i}") for i in range(2)]
        pj = [pb(st, f"pj{i}") for i in range(3)]
        gps = pb(st, "gps")
        rps = [pb(st, f"rps{i}") for i in range(2)]

        ident_in, const_in, small_in, ln_in = sem("ident_in"), sem("const_in"), sem("small_in"), sem("ln_in")
        x_in = [sem(f"x_in{t}") for t in range(NT)]
        rows_proj, rows_copied = sem("gate_rows_proj"), sem("gate_rows_copied")
        pw_in, h_out = sem("pw_in"), sem("h_out")
        chunk_in = [sem(f"chunk_in{i}") for i in range(2)]
        eps_set, pads_set = sem("eps_set"), sem("pads_set")
        w_high, w_low_dve, w_low_pool = sem("w_high"), sem("w_low_dve"), sem("w_low_pool")
        turn_low, ws_high, ws_low = sem("h_turn_low"), sem("ws_high"), sem("ws_low")
        stats_ready, std_ready, scale_ready, norm_ready, gmul_ready, h_ready = (
            sem(f"ln1_{n}") for n in ("stats", "std", "scale", "norm", "gmul", "h"))
        turned, turn_copied = sem("h_turned"), sem("h_turn_copied")
        small_proj, small_copied = sem("small_proj"), sem("small_copied")
        proj_done, proj_copied = sem("proj_done"), sem("proj_copied")
        conv_done, silu_done = sem("conv_done"), sem("silu_done")
        gate_abs = sem("gate_abs")
        gate_exp, gate_in, gate_ln, gates_done = sem("gate_exp"), sem("gate_in"), sem("gate_ln"), sem("gates_done")
        cum_done, cum_copied, a_done, a_turned, scan_done, m_turned = (
            sem(n) for n in ("cum_done", "cum_copied", "a_done", "a_turned", "scan_done", "m_turned"))
        em_arg, beta_done = sem("em_arg"), sem("beta_done")
        square_done, sum_done, root_done, qk_normed = sem("square_done"), sem("sum_done"), sem("root_done"), sem("qk_normed")
        tok_turned, tok_copied = sem("tok_turned"), sem("tok_copied")
        up_zero, rows_zero = sem("up_zero"), sem("rows_zero")
        up_copied, pooled, pool_mixed, pool_done = sem("up_copied"), sem("pooled"), sem("pool_mixed"), sem("pool_done")
        dve_chain, pool_chain = sem("front_dve_chain"), sem("front_pool_chain")

        W = 256
        starts = [at + W * i for at in (C_Q, C_K, C_V, C_MQ, C_MV, C_U, C_MO, C_Z) for i in range(2)]
        NCH = len(starts)
        POOL_LOW = range(2, 8)
        gate_banks = tp + pj + rps + [gps]

        def wait_low(eng, c):
            if c in POOL_LOW:
                eng.wait_ge(w_low_pool, c - POOL_LOW[0] + 1)
            else:
                eng.wait_ge(w_low_dve, c + 1 if c < POOL_LOW[0] else c + 1 - len(POOL_LOW))

        def raw_room(c):
            return raw_rooms[c if c < 2 else 2 + c % 2]

        w_rows = w_in.rearrange("(p k) n -> p k n", k=KT)
        NQKV = 12
        with nc.Block() as block:
            @block.sync
            def _(sp_):
                for t in range(NT):
                    sp_.dma_start(h[:, t, :], x[t * P:(t + 1) * P, :]).then_inc(x_in[t], 16)
                    if t == 0:
                        sp_.dma_start(lng, v["ln_in_g"].to_broadcast([P, DM])).then_inc(ln_in, 16)
                        sp_.dma_start(lnb, v["ln_in_b"].to_broadcast([P, DM])).then_inc(ln_in, 16)
                        sp_.dma_start(cst[:, 0:P], const[:, 0:P]).then_inc(ident_in, 16)
                for c, at in enumerate(starts):
                    if c == 2:
                        sp_.dma_start(sml[:, :], small).then_inc(small_in, 16)
                        sp_.dma_start(cst[:, P:], const[:, P:]).then_inc(const_in, 16)
                        sp_.dma_start(pw[:, :, :], v["pool_w"].rearrange("g c d -> c g d")).then_inc(pw_in, 16)
                        for t in range(NT):
                            sp_.wait_ge(h_ready, t + 1)
                            sp_.dma_start(v["h_dram"][t * P:(t + 1) * P, :], h[:, t, :]).then_inc(h_out, 16)
                        sp_.wait_ge(h_out, 16 * NT)
                        sp_.wait_ge(turned, 2 * NT)
                    if c >= 4:
                        wait_low(sp_, c - 2)
                    sp_.dma_start(raw_room(c), w_rows[:, :, at:at + W]).then_inc(chunk_in[c % 2], 16)

            @block.tensor
            def _(pe):
                pe.wait_ge(ident_in, 16)
                for n in range(2 * NT):
                    t, half = n // 2, n % 2
                    pe.wait_ge(h_ready, t + 1)
                    for k in range(4):
                        last = pe.transpose(gate_banks[n][:, k * P:(k + 1) * P], h[:, t, 4 * half + k::KT], ident)
                    last.then_inc(turned, 1)
                pe.wait_ge(turn_copied, 2 * NT)
                pe.wait_ge(turn_low, 2 * NT)
                n = 0

                def chunk(c, between=None):
                    nonlocal n
                    pe.wait_ge(w_high, c + 1)
                    wait_low(pe, c)
                    for m in range(2):
                        if n >= 3:
                            pe.wait_ge(proj_copied, n - 2)
                        if C_MV <= starts[c] < C_MV + MW:
                            for half in range(2):
                                t = 2 * m + half
                                for k in range(KT):
                                    for a, b in PRODUCTS:
                                        last = pe.matmul(pj[n % 3][:, W * half:W * half + W], h_part[a][:, k, t * P:(t + 1) * P],
                                                         w_part[c % 2][b][:, k, :], start=(k == 0 and a + b == 0),
                                                         stop=(k == KT - 1 and a == 1))
                        else:
                            for k in range(KT):
                                for a, b in PRODUCTS:
                                    last = pe.matmul(pj[n % 3][:, :], w_part[c % 2][a][:, k, m * P:(m + 1) * P], h_part[b][:, k, :],
                                                     start=(k == 0 and a + b == 0), stop=(k == KT - 1 and a == 1))
                        last.then_inc(proj_done, 1)
                        n += 1
                        if between is not None:
                            between(2 * (c % 2) + m)

                def chunk_pair(c, between=None):
                    chunk(2 * c, between)
                    chunk(2 * c + 1, between)

                chunk_pair(0)
                pe.wait_ge(ws_low, 1)
                for k in range(KT):
                    for a, b in PRODUCTS:
                        last = pe.matmul(rps[0][0:32, :], ws_part[a][:, k, :], h_part[b][:, k, :],
                                         start=(k == 0 and a + b == 0), stop=(k == KT - 1 and a == 1))
                last.then_inc(rows_proj, 1)

                def gate_rows(m):
                    if m == 1:
                        pe.wait_ge(rows_copied, 1)
                        for t in range(NT):
                            last = pe.transpose(gps[:, t * 32:(t + 1) * 32], nrm[0:32, 0, t * P:(t + 1) * P], ident[0:32, 0:32])
                        last.then_inc(small_proj, 1)

                chunk_pair(1, gate_rows)
                chunk_pair(2)
                pe.wait_ge(const_in, 16)
                pe.wait_ge(gates_done, 4)
                sums = gps[:, 128:224].rearrange("p (t n) -> p t n", t=NT)
                for d, tri in enumerate((cn("upto"), cn("after"))):
                    a, b = slice(4 * d, 4 * d + 4), slice(8 + 4 * d, 12 + 4 * d)
                    pe.matmul(sums[:, :, a], tri, gg[:, :, a], start=True, stop=True)
                    pe.matmul(sums[:, :, 16 + 4 * d:20 + 4 * d], tri, gg[:, :, b], start=True, stop=False)
                    pe.matmul(sums[:, :, 16 + 4 * d:20 + 4 * d], ones, others[:, :, a], start=False, stop=True)
                last = pe.matmul(sums[:, :, 8:16], ones, gg[:, :, 0:8], start=True, stop=True)
                last.then_inc(cum_done, 1)
                chunk_pair(3)
                pe.wait_ge(a_done, 1)
                for d in range(2):
                    for t in range(NT):
                        last = pe.transpose(rps[d][0:4, t * P:(t + 1) * P], acol[:, t, 4 * d:4 * d + 4], ident)
                last.then_inc(a_turned, 1)
                def head_sum(m):
                    pe.wait_ge(square_done, m + 1)
                    if m >= 2:
                        pe.wait_ge(root_done, m - 1)
                    pe.matmul(tp[m % 2][:, :], ones, sq[:, m % 2, :], start=True, stop=True).then_inc(sum_done, 1)

                def token_rows(m):
                    t = m % 4
                    if m < 4:
                        pe.wait_ge(qk_normed, 8)
                    else:
                        pe.wait_ge(silu_done, NQKV)
                    if m >= 2:
                        pe.wait_ge(tok_copied, m - 1)
                    for hd in range(NH):
                        src = qkT[:, 1, hd, :] if m < 4 else vT[:, hd, :]
                        last = pe.transpose(tp[m % 2][:, hd * P:(hd + 1) * P], src[:, t * P:(t + 1) * P], ident)
                    last.then_inc(tok_turned, 1)

                def pool_mix(g):
                    pe.wait_ge(pooled, g + 1)
                    if g >= 2:
                        pe.wait_ge(pool_done, g - 1)
                    pe.matmul(rps[g % 2][:, :], pw[:, g, :], yT[:, 1, g, :], start=True, stop=True).then_inc(pool_mixed, 1)

                chunk_pair(4, head_sum)
                pe.wait_ge(scan_done, 2)
                for d in range(2):
                    for t in range(NT):
                        last = pe.transpose(gps[:, 256 + 8 * t + 4 * d:260 + 8 * t + 4 * d], mrow[0:4, d, t * P:(t + 1) * P],
                                            ident[0:4, 0:4])
                last.then_inc(m_turned, 1)
                chunk_pair(5, lambda m: head_sum(4 + m))
                def both_rows(m):
                    token_rows(2 * m)
                    token_rows(2 * m + 1)

                chunk_pair(6, both_rows)
                pe.wait_ge(pw_in, 16)
                chunk_pair(7, pool_mix)

            @block.scalar
            def _(act):
                act.wait_ge(eps_set, 1)
                def copy_turned(t):
                    for half in range(2):
                        act.wait_ge(turned, 2 * t + half + 1)
                        act.activation(h_part[0][:, 4 * half:4 * half + 4, t * P:(t + 1) * P],
                                       gate_banks[2 * t + half][:, :].rearrange("p (k s) -> p k s", k=4), ACT.Copy).then_inc(turn_copied, 1)

                def high(c):
                    if c >= NCH:
                        return
                    act.wait_ge(chunk_in[c % 2], 16 * (c // 2 + 1))
                    if c >= 2:
                        act.wait_ge(proj_done, 2 * (c - 1))
                    act.activation(w_part[c % 2][0], raw_room(c), ACT.Copy).then_inc(w_high, 1)

                def before(t):
                    if t >= 2:
                        copy_turned(t - 2)

                layer_norm_act(act, h, mv, rstd, nmr, epsc[:, 0:1], stats_ready, std_ready, scale_ready, norm_ready, before)
                high(0)
                for t in range(NT - 2, NT):
                    copy_turned(t)
                high(1)
                act.wait_ge(small_in, 16)
                act.activation(ws_part[0], sml[:, SM_W:SM_W + KT * 32].rearrange("p (k n) -> p k n", k=KT), ACT.Copy).then_inc(ws_high, 1)
                def token_gates():
                    act.wait_ge(small_proj, 1)
                    act.activation(ab[:, :, :], gps[:, 0:128].rearrange("p (t n) -> p t n", t=NT), ACT.Copy).then_inc(small_copied, 1)
                    act.wait_ge(small_copied, 1)
                    act.activation(beta[:, :, :], ab[:, :, 8:16], ACT.Sigmoid).then_inc(beta_done, 1)
                    act.wait_ge(gate_in, 1)
                    act.activation(sp[:, 1, :, :], sp[:, 1, :, :], ACT.Abs).then_inc(gate_abs, 1)
                    act.wait_ge(gate_abs, 1)
                    act.activation(sp[:, 1, :, :], sp[:, 1, :, :], ACT.Exp, scale=-1.0).then_inc(gate_exp, 1)
                    act.activation(sml[:, SM_BIAS:SM_BIAS + 8], sml[:, SM_BIAS:SM_BIAS + 8], ACT.Exp).then_inc(gate_exp, 1)
                    act.wait_ge(gate_exp, 1)
                    act.activation(sp[:, 1, :, :], sp[:, 1, :, :], ACT.Ln, bias=1.0).then_inc(gate_ln, 1)

                def gates(n):
                    if n == 4:
                        act.wait_ge(rows_proj, 1)
                        act.activation(nrm[0:32, 0, :], rps[0][0:32, :], ACT.Copy).then_inc(rows_copied, 1)
                    if n != 6:
                        return
                    token_gates()

                def copy_qkv(n):
                    act.wait_ge(proj_done, n + 1)
                    if n >= 3:
                        act.wait_ge(conv_done, n - 2)
                    act.activation(raw[:, n % 3, 2:2 + SEQ], pj[n % 3][:, :], ACT.Copy).then_inc(proj_copied, 1)

                def silu_qkv(n):
                    act.wait_ge(conv_done, n + 1)
                    dst = qkT[:, n // 4, n % 4, :] if n < 8 else vT[:, n % 4, :]
                    act.activation(dst, cv[:, n % 3, :], ACT.Silu).then_inc(silu_done, 1)

                act.wait_ge(pads_set, 1)
                def ahead(n):
                    if n % 2 == 0 and n >= 2:
                        high(n // 2 + 1)

                for n in range(NQKV):
                    ahead(n)
                    copy_qkv(n)
                    if n >= 1:
                        silu_qkv(n - 1)
                    gates(n)
                silu_qkv(NQKV - 1)
                for n in range(12, 16):
                    ahead(n)
                    act.wait_ge(proj_done, n + 1)
                    if n < 14:
                        act.wait_ge(rows_zero, 2)
                        for half in range(2):
                            rows = slice(QK * half, QK * half + QK)
                            last = act.activation(mq[rows, 2 * (n - 12) + half, :], pj[n % 3][rows, :], ACT.Copy)
                    else:
                        last = act.activation(mk[:, n - 14, :], pj[n % 3][:, :], ACT.Copy, scale=QK ** -0.5)
                    last.then_inc(proj_copied, 1)
                def square(m):
                    act.wait_ge(silu_done, m + 1)
                    if m >= 2:
                        act.wait_ge(sum_done, m - 1)
                    act.activation(sq[:, m % 2, :], qkT[:, m // 4, m % 4, :], ACT.Square).then_inc(square_done, 1)

                def root(m):
                    act.wait_ge(sum_done, m + 1)
                    if m >= 2:
                        act.wait_ge(qk_normed, m - 1)
                    act.activation(nrm[:, m % 2, :], tp[m % 2][:, :], ACT.Sqrt, scale=(float(DV) if m < 4 else 1.0),
                                   bias=epsc[:, 1 if m < 4 else 2:(1 if m < 4 else 2) + 1]).then_inc(root_done, 1)

                def token_copy(m):
                    act.wait_ge(tok_turned, m + 1)
                    dst = (kTok if m < 4 else vTok)[:, m % 4, :, :]
                    act.activation(dst, tp[m % 2][:, :].rearrange("p (h e) -> p h e", h=NH), ACT.Copy).then_inc(tok_copied, 1)

                square(0)
                for n in range(16, 20):
                    ahead(n)
                    act.wait_ge(proj_done, n + 1)
                    heads, tiles = 2 * ((n - 16) // 2), 2 * (n % 2)
                    src = pj[n % 3][:, :].rearrange("p (t h e) -> p t h e", t=2, h=2)
                    for half in range(2):
                        last = act.activation(mvx[:, tiles + half, heads:heads + 2, 0:DV], src[:, half], ACT.Copy)
                    last.then_inc(proj_copied, 1)
                    square(n - 15)
                    root(n - 16)
                for n in range(20, 24):
                    ahead(n)
                    act.wait_ge(proj_done, n + 1)
                    if n >= 21:
                        act.wait_ge(pooled, n - 20)
                    act.activation(up[:, 8:8 + SEQ], pj[n % 3][:, :], ACT.Copy).then_inc(proj_copied, 1)
                    if n < 23:
                        square(n - 15)
                    root(n - 16)
                for n in range(24, 28):
                    ahead(n)
                    act.wait_ge(proj_done, n + 1)
                    act.activation(yT[:, 2, n - 24, :], pj[n % 3][:, :], ACT.Sigmoid).then_inc(proj_copied, 1)
                    token_copy(2 * (n - 24))
                    token_copy(2 * (n - 24) + 1)
                act.wait_ge(em_arg, 1)
                act.activation(emx[:, :, :], emx[:, :, :], ACT.Exp, scale=-1.0).then_inc(gate_exp, 1)
                for n in range(28, 32):
                    ahead(n)
                    act.wait_ge(proj_done, n + 1)
                    act.activation(yT[:, 0, n - 28, :], pj[n % 3][:, :], ACT.Silu).then_inc(proj_copied, 1)
                    g = n - 28
                    act.wait_ge(pool_mixed, g + 1)
                    act.activation(yT[:, 1, g, :], rps[g % 2][:, :], ACT.Copy,
                                   scale=sml[:, SM_NORM + 4 + g:SM_NORM + 5 + g]).then_inc(pool_done, 1)

            @block.vector
            def _(dve):
                chain = Chain(dve, dve_chain)
                dve.memset(epsc[:, 0:1], LN_EPS)
                dve.memset(epsc[:, 1:2], DV * NORM_EPS)
                dve.memset(epsc[:, 2:3], NORM_EPS).then_inc(eps_set, 1)
                dve.memset(raw[:, :, 0:2], 0.0)
                dve.memset(raw[:, :, SEQ + 2:SEQ + 4], 0.0).then_inc(pads_set, 1)
                dve.memset(mvx[:, :, :, DV:DV + 1], 1.0)

                def x_ready(t):
                    dve.wait_ge(x_in[t], 16)
                layer_norm_dve(dve, chain, h, stats, mv, rstd, nmr, x_ready, stats_ready, std_ready, scale_ready,
                               norm_ready, gmul_ready, lng, ln_in, 1)

                def low(c):
                    if c >= 2:
                        dve.wait_ge(proj_done, 2 * (c - 1))
                    dve.wait_ge(w_high, c + 1)
                    dve.tensor_tensor(w_part[c % 2][1], raw_room(c), w_part[c % 2][0].bitcast(F32), ALU.subtract).then_inc(w_low_dve, 1)

                for n in range(2 * NT):
                    t, half = n // 2, n % 2
                    if n == 4:
                        low(0)
                    at = (slice(None), slice(4 * half, 4 * half + 4), slice(t * P, (t + 1) * P))
                    dve.wait_ge(turn_copied, n + 1)
                    dve.tensor_tensor(h_part[1][at], gate_banks[n][:, :].rearrange("p (k s) -> p k s", k=4),
                                      h_part[0][at].bitcast(F32), ALU.subtract).then_inc(turn_low, 1)
                low(1)
                dve.wait_ge(ws_high, 1)
                dve.tensor_tensor(ws_part[1], sml[:, SM_W:SM_W + KT * 32].rearrange("p (k n) -> p k n", k=KT),
                                  ws_part[0].bitcast(F32), ALU.subtract).then_inc(ws_low, 1)

                def gates():
                    dve.wait_ge(small_copied, 1)
                    dve.wait_ge(small_in, 16)
                    bias = sml[:, SM_BIAS:SM_BIAS + 32]
                    chain.add(dve.tensor_tensor(sp[:, 0, :, 0:8], ab[:, :, 0:8], bc(bias[:, 8:16], 1, NT), ALU.add))
                    chain.add(dve.tensor_tensor(sp[:, 0, :, 8:16], ab[:, :, 24:32], bc(bias[:, 24:32], 1, NT), ALU.add))
                    chain.add(dve.tensor_tensor(gg[:, :, 16:24], ab[:, :, 16:24], bc(bias[:, 16:24], 1, NT), ALU.add))
                    chain.wait()
                    dve.tensor_scalar(sp[:, 1, :, :], sp[:, 0, :, :], 1.0, None, ALU.mult).then_inc(gate_in, 1)
                    chain.add(dve.tensor_scalar(sp[:, 2, :, 0:8], sp[:, 0, :, 0:8], 0.0, None, ALU.max))
                    chain.wait()
                    dve.tensor_scalar(sp[:, 2, :, 8:16], sp[:, 0, :, 8:16], 0.0, None, ALU.min).then_inc(gate_in, 1)
                    dve.wait_ge(gate_ln, 1)
                    dve.wait_ge(gate_in, 2)
                    chain.link(dve.tensor_tensor(sp[:, 2, :, 0:8], sp[:, 2, :, 0:8], sp[:, 1, :, 0:8], ALU.add))
                    dve.wait_ge(gate_exp, 2)
                    chain.link(dve.tensor_tensor(sp[:, 2, :, 0:8], sp[:, 2, :, 0:8], bc(bias[:, 0:8], 1, NT), ALU.mult))
                    dve.tensor_scalar(gg[:, :, 0:8], sp[:, 2, :, 0:8], -1.0, None, ALU.mult).then_inc(gates_done, 1)
                    dve.tensor_tensor(gg[:, :, 8:16], sp[:, 2, :, 8:16], sp[:, 1, :, 8:16], ALU.subtract).then_inc(gates_done, 1)
                    dve.wait_ge(gates_done, 2)
                    dve.memset(others[:, 0, 0:4], 0.0)
                    chain.link(dve.memset(others[:, NT - 1, 4:8], 0.0))
                    for t in range(1, NT):
                        u = NT - 1 - t
                        first = dve.tensor_tensor(others[:, t, 0:4], others[:, t - 1, 0:4], gg[:, t - 1, 8:12], ALU.add)
                        second = dve.tensor_tensor(others[:, u, 4:8], others[:, u + 1, 4:8], gg[:, u + 1, 12:16], ALU.add)
                        if t < NT - 1:
                            chain.add(first)
                            chain.link(second)
                        else:
                            first.then_inc(gates_done, 1)
                            second.then_inc(gates_done, 1)

                dve.wait_ge(small_in, 16)
                for n in range(NQKV):
                    dve.wait_ge(proj_copied, n + 1)
                    if n >= 3:
                        dve.wait_ge(silu_done, n - 2)
                    taps = sml[:, SM_CONV + TAPS * n:SM_CONV + TAPS * (n + 1)]
                    chain.link(dve.tensor_scalar(cv[:, n % 3, :], raw[:, n % 3, 0:SEQ], taps[:, 0:1], None, ALU.mult))
                    for j in range(1, TAPS):
                        ins = dve.scalar_tensor_tensor(cv[:, n % 3, :], raw[:, n % 3, j:j + SEQ], taps[:, j:j + 1],
                                                       cv[:, n % 3, :], ALU.mult, ALU.add)
                        if j < TAPS - 1:
                            chain.link(ins)
                        else:
                            ins.then_inc(conv_done, 1)
                    if n == 6:
                        gates()
                dve.wait_ge(cum_done, 1)
                dve.tensor_copy(cum[:, :, :], gps[:, 128:224].rearrange("p (t n) -> p t n", t=NT)).then_inc(cum_copied, 1)
                dve.wait_ge(cum_copied, 1)
                dve.tensor_tensor(acol[:, :, :], gg[:, :, 16:24], cum[:, :, 16:24], ALU.subtract).then_inc(a_done, 1)
                zrow = up[0:4, 0:SEQ]
                dve.wait_ge(up_zero, 1)
                dve.wait_ge(rows_zero, 2)
                dve.wait_ge(a_turned, 1)
                dve.tensor_tensor_scan(mrow[0:4, 0, :], rps[0][0:4, :], zrow,
                                       0.0, ALU.max, ALU.max).then_inc(scan_done, 1)
                dve.tensor_tensor_scan(mrow[0:4, 1, ::-1], rps[1][0:4, ::-1], zrow,
                                       0.0, ALU.max, ALU.max).then_inc(scan_done, 1)
                low(8)
                low(9)
                for m in range(8):
                    if m == 4:
                        dve.wait_ge(m_turned, 1)
                        dve.tensor_tensor(emx[:, :, :], gps[:, 256:288].rearrange("p (t n) -> p t n", t=NT), cum[:, :, 16:24],
                                          ALU.add).then_inc(em_arg, 1)
                    dve.wait_ge(root_done, m + 1)
                    chain.link(dve.reciprocal(nrm[:, m % 2, :], nrm[:, m % 2, :]))
                    dve.tensor_tensor(qkT[:, m // 4, m % 4, :], qkT[:, m // 4, m % 4, :], nrm[:, m % 2, :],
                                      ALU.mult).then_inc(qk_normed, 1)
                    if m % 2 == 1:
                        low(10 + m // 2)
                low(14)
                low(15)

            @block.gpsimd
            def _(pool):
                v["zero_last"](pool)
                chain = Chain(pool, pool_chain)
                pool.memset(mrow[:, :, :], 0.0).then_inc(rows_zero, 1)
                pool.memset(mq[:, :, :], 0.0).then_inc(rows_zero, 1)
                pool.memset(up[:, :], 0.0).then_inc(up_zero, 1)
                chain.add(pool.memset(win[:, :, :], 0.0))
                for t in range(NT):
                    pool.wait_ge(gmul_ready, t + 1)
                    pool.wait_ge(ln_in, 32)
                    pool.tensor_tensor(h[:, t, :], h[:, t, :], lnb, ALU.add).then_inc(h_ready, 1)
                for c in POOL_LOW:
                    pool.wait_ge(proj_done, 2 * (c - 1))
                    pool.wait_ge(w_high, c + 1)
                    pool.tensor_tensor(w_part[c % 2][1], raw_room(c), w_part[c % 2][0].bitcast(F32), ALU.subtract).then_inc(w_low_pool, 1)
                chain.wait()
                edge = cn("edge").rearrange("p (g n) -> p g n", g=4)
                pool.wait_ge(const_in, 16)
                for g in range(4):
                    pool.wait_ge(proj_copied, 21 + g)
                    chain.link(pool.tensor_tensor(win[:, 0, 1:528], up[:, 0:527], up[:, 1:528], ALU.add))
                    cur = 0
                    for lvl in range(g):
                        r = 1 << lvl
                        lo, hi = 2 * r, 528 - 2 * r
                        chain.link(pool.tensor_tensor(win[:, 1 - cur, lo:hi], win[:, cur, lo - r:hi - r],
                                                      win[:, cur, lo + r:hi + r], ALU.add))
                        cur = 1 - cur
                    w = win[:, cur, 8:8 + SEQ]
                    chain.add(pool.tensor_tensor(w[:, 0:8], w[:, 0:8], edge[:, g, 0:8], ALU.mult))
                    chain.add(pool.tensor_tensor(w[:, SEQ - 8:SEQ], w[:, SEQ - 8:SEQ], edge[:, g, 8:16], ALU.mult))
                    chain.add(pool.tensor_scalar(w[:, 8:SEQ - 8], w[:, 8:SEQ - 8], 1.0 / (2 << g), None, ALU.mult))
                    chain.wait()
                    pool.tensor_tensor(yT[:, 1, g, :], w, up[:, 8:8 + SEQ], ALU.subtract).then_inc(pooled, 1)
                    pool.wait_ge(pooled, g + 1)


def mlstm(nc, sem, sb, pb, cn, v):
    sml, epsc, yT, mq, mvx, mrow, acol, emx = (v[k] for k in ("sml", "epsc", "yT", "mq", "mvx", "mrow", "acol", "emx"))
    ident = v["ident"]
    st = ExitStack()
    with st:
        scores = sb(st, "scores", [P, 2, NT, SEQ])
        wts = sb(st, "wts", [P, 2, NT, SEQ])
        mdiag = sb(st, "mdiag", [P, 2, NT, P])
        hs = sb(st, "hs", [P, NT, NH, DV])
        tmp = sb(st, "htmp", [P, NT, DV])
        den = sb(st, "den", [P, 2, NT])
        stats, mv, rstd = sb(st, "mstats", [P, NT * NH, 6]), sb(st, "mmv", [P, NT * NH, 2]), sb(st, "mrstd", [P, NT * NH])
        qb = [pb(st, f"qb{i}") for i in range(2)]
        mb = [pb(st, f"mb{i}") for i in range(2)]
        nu = [pb(st, f"nu{i}") for i in range(4)]
        score_done, score_copied, max_spread, diag_ready, exp_done, weighted = (
            sem(n) for n in ("score_done", "score_copied", "max_spread", "diag_ready", "exp_done", "weighted"))
        num_done, den_abs, num_used = sem("num_done"), sem("den_abs"), sem("num_used")
        mvar_ready, mroot_done, mnormed, mturned, yml_done = (
            sem(n) for n in ("mvar_ready", "mroot_done", "mnormed", "mturned", "yml_done"))
        dve_chain, rooms_filled = sem("mlstm_dve_chain"), sem("rooms_filled")

        def span(d, j):
            return (j * P, SEQ) if d == 0 else (0, (j + 1) * P)

        with nc.Block() as block:
            @block.sync
            def _(sp):
                for i, r in enumerate((1, 2)):
                    at = C_G + r * DM
                    sp.dma_start(v["gw"][i], v["w_rows"][:, :, at:at + P]).then_inc(rooms_filled, 16)
                    sp.dma_start(v["bw"][i], v["w_branch"][r].rearrange("(k p) n -> p k n", p=P)[:, :, 0:P])\
                        .then_inc(rooms_filled, 16)
                sp.wait_ge(rooms_filled, 16 * 4)

            @block.tensor
            def _(pe):
                def score(h):
                    for j in range(NT):
                        n = 4 * h + j
                        if n >= 2:
                            pe.wait_ge(score_copied, n - 1)
                        pe.matmul(qb[n % 2][:, :], v["mk"][:, h // 2, j * P:(j + 1) * P], mq[:, h, :],
                                  start=True, stop=True).then_inc(score_done, 1)

                def spread(n):
                    h, d = n // 2, n % 2
                    if n >= 2:
                        pe.wait_ge(exp_done, n - 1)
                        pe.wait_ge(diag_ready, n - 1)
                    pe.matmul(mb[n % 2][:, :], ident[:, h:h + 1].to_broadcast([P, P]), mrow[:, d, :],
                              start=True, stop=True).then_inc(max_spread, 1)

                def numerator(n):
                    h, d = n // 2, n % 2
                    pe.wait_ge(weighted, n + 1)
                    if n >= 2:
                        pe.wait_ge(num_used, n - 1)
                    for i in range(NT):
                        js = range(i + 1) if d == 0 else range(i, NT)
                        for j in js:
                            last = pe.matmul(nu[2 * (n % 2) + i // 2][:, (i % 2) * (DV + 1):(i % 2 + 1) * (DV + 1)],
                                             wts[:, n % 2, j, i * P:(i + 1) * P], mvx[:, j, h, :],
                                             start=(j == js[0]), stop=(j == js[-1]))
                    last.then_inc(num_done, 1)

                score(0)
                spread(0)
                spread(1)
                for h in range(NH):
                    if h + 1 < NH:
                        score(h + 1)
                        spread(2 * h + 2)
                    numerator(2 * h)
                    if h + 1 < NH:
                        spread(2 * h + 3)
                    numerator(2 * h + 1)
                for h in range(NH):
                    pe.wait_ge(mnormed, NT * (h + 1))
                    if h >= 2:
                        pe.wait_ge(yml_done, h - 1)
                    for t in range(NT):
                        last = pe.transpose(qb[h % 2][:, t * P:(t + 1) * P], hs[:, t, h, :], ident)
                    last.then_inc(mturned, 1)

            @block.scalar
            def _(act):
                def copy_scores(h):
                    if h >= 2:
                        act.wait_ge(weighted, 2 * (h - 1))
                    for j in range(NT):
                        n = 4 * h + j
                        act.wait_ge(score_done, n + 1)
                        act.activation(scores[:, h % 2, j, :], qb[n % 2][:, :], ACT.Copy).then_inc(score_copied, 1)

                def exps(n):
                    h, d = n // 2, n % 2
                    act.wait_ge(diag_ready, n + 1)
                    if n >= 2:
                        act.wait_ge(num_done, n - 1)
                    for j in range(NT):
                        bias = acol[:, j, 4 * d + h:4 * d + h + 1]
                        last = act.activation(wts[:, n % 2, j, j * P:(j + 1) * P], mdiag[:, n % 2, j, :], ACT.Exp, bias=bias)
                        lo, hi = ((j + 1) * P, SEQ) if d == 0 else (0, j * P)
                        if lo < hi:
                            last = act.activation(wts[:, n % 2, j, lo:hi], mb[n % 2][:, lo:hi], ACT.Exp, bias=bias, scale=-1.0)
                    last.then_inc(exp_done, 1)

                def absolute(n):
                    act.wait_ge(num_done, n + 1)
                    if n >= 2:
                        act.wait_ge(num_used, n - 1)
                    for i2 in range(2):
                        src = nu[2 * (n % 2) + i2][:, 0:2 * (DV + 1)].rearrange("p (i e) -> p i e", i=2)[:, :, DV]
                        last = act.activation(den[:, n % 2, 2 * i2:2 * i2 + 2], src, ACT.Abs)
                    last.then_inc(den_abs, 1)

                copy_scores(0)
                exps(0)
                exps(1)
                for h in range(NH):
                    if h + 1 < NH:
                        copy_scores(h + 1)
                    absolute(2 * h)
                    if h + 1 < NH:
                        exps(2 * h + 2)
                    absolute(2 * h + 1)
                    if h + 1 < NH:
                        exps(2 * h + 3)
                act.wait_ge(mvar_ready, NH)
                act.activation(rstd[:, :], mv[:, :, 1], ACT.Sqrt, bias=epsc[:, 2:3]).then_inc(mroot_done, 1)

            @block.vector
            def _(dve):
                chain = Chain(dve, dve_chain)

                def diag(n):
                    dve.wait_ge(max_spread, n + 1)
                    if n >= 2:
                        dve.wait_ge(exp_done, n - 1)
                    neg = cn("neg_fwd" if n % 2 == 0 else "neg_bwd")
                    dve.scalar_tensor_tensor(mdiag[:, n % 2, :, :], mb[n % 2][:, :].rearrange("p (j i) -> p j i", j=NT), -1.0,
                                             bc(neg, 1, NT), ALU.mult, ALU.add).then_inc(diag_ready, 1)

                def weigh(n):
                    h, d = n // 2, n % 2
                    dve.wait_ge(exp_done, n + 1)
                    dve.wait_ge(score_copied, 4 * (h + 1))
                    for j in range(NT):
                        lo, hi = span(d, j)
                        w = wts[:, n % 2, j, lo:hi]
                        last = dve.tensor_tensor(w, w, scores[:, h % 2, j, lo:hi], ALU.mult)
                    last.then_inc(weighted, 1)

                def divide(n):
                    h, d = n // 2, n % 2
                    dn = den[:, n % 2, :]
                    dve.wait_ge(den_abs, n + 1)
                    chain.link(dve.tensor_tensor(dn, dn, emx[:, :, 4 * d + h], ALU.max))
                    chain.link(dve.reciprocal(dn, dn))
                    for i2 in range(2):
                        src = nu[2 * (n % 2) + i2][:, 0:2 * (DV + 1)].rearrange("p (i e) -> p i e", i=2)[:, :, 0:DV]
                        dst = hs[:, 2 * i2:2 * i2 + 2, h, :] if d == 0 else tmp[:, 2 * i2:2 * i2 + 2, :]
                        last = dve.tensor_tensor(dst, src, bc(dn[:, 2 * i2:2 * i2 + 2], 2, DV), ALU.mult)
                    last.then_inc(num_used, 1)
                    if d == 1:
                        dve.wait_ge(num_used, n + 1)
                        chain.link(dve.tensor_tensor(hs[:, :, h, :], hs[:, :, h, :], tmp[:, :, :], ALU.add))
                        for t in range(NT):
                            chain.add(dve.bn_stats(stats[:, h * NT + t, :], hs[:, t, h, :]))
                        chain.wait()
                        for t in range(NT):
                            last = dve.bn_aggr(mv[:, h * NT + t, :], stats[:, h * NT + t, :])
                        last.then_inc(mvar_ready, 1)

                diag(0)
                diag(1)
                weigh(0)
                for n in range(2 * NH):
                    if n + 2 < 2 * NH:
                        diag(n + 2)
                    if n + 1 < 2 * NH:
                        weigh(n + 1)
                    divide(n)
                dve.wait_ge(mroot_done, 1)
                chain.link(dve.reciprocal(rstd[:, :], rstd[:, :]))

                def norm(h):
                    for t in range(NT):
                        g = h * NT + t
                        o = hs[:, t, h, :]
                        dve.tensor_scalar(o, o, mv[:, g, 0:1], rstd[:, g:g + 1], ALU.subtract, ALU.mult).then_inc(mnormed, 1)

                def place(h):
                    dve.wait_ge(mturned, h + 1)
                    dve.scalar_tensor_tensor(yT[:, 2, h, :], qb[h % 2][:, :], sml[:, SM_NORM + 8 + h:SM_NORM + 9 + h],
                                             yT[:, 2, h, :], ALU.mult, ALU.mult).then_inc(yml_done, 1)

                norm(0)
                norm(1)
                for h in range(NH):
                    place(h)
                    if h + 2 < NH:
                        norm(h + 2)

            @block.gpsimd
            def _(pool):
                v["zero_last"](pool)


def deltanet(nc, sem, sb, pb, cn, v):
    sml, epsc, yT, qkT, kTok, vTok, beta, cum, gg = (
        v[k] for k in ("sml", "epsc", "yT", "qkT", "kTok", "vTok", "beta", "cum", "gg"))
    ident, ones = v["ident"], v["ones"]
    st = ExitStack()
    NB = 2 * NT
    BATCH = [(m % 2, m // 2 if m % 2 == 0 else NT - 1 - m // 2) for m in range(NB)]
    with st:
        def four(name, n):
            return sb(st, name, [P, n, NH, P])

        mt, tt, tn, at, qe = (four(name, 4) for name in ("mt", "tt", "tn", "at", "qe"))
        ot, rhs = four("ot", 2), four("rhs", 2)
        y1s = four("y1s", 2)
        stage = v["h2"][:, 3, :].rearrange("p (a s) -> p a s", a=2)
        sig = sb(st, "sigd", [P, SEQ])
        gw, bw = v["gw"], v["bw"]
        w_rows, w_branch = v["w_rows"], v["w_branch"]
        h_part = v["h_part"]
        gws = sb(st, "gws", [P, 2, 2, KT, P], F32R)
        gw_part = [[gws[:, r, i, :, :] for i in range(2)] for r in range(2)]

        vn, vnd = rhs, four("vnd", 2)
        state = four("state", 2)
        oT = sb(st, "oT", [P, NH, SEQ])
        eg = sb(st, "eg", [P, NT, 3, 8])
        pr = [pb(st, f"pr{i}") for i in range(2)]
        lv = [pb(st, f"lv{i}") for i in range(2)]
        gate_ps, branch_ps = pb(st, "gate_ps"), pb(st, "branch_ps")
        sc = [pb(st, f"sc{i}") for i in range(2)]
        (gr_done, kk_done, qk_done, turn_done, dif_ready, dec_ready, egr_ready, qe_ready, kk_used, mt_ready, tt_ready,
         at_ready, tn_copied) = (sem("dn_" + n) for n in (
             "gr_done", "kk_done", "qk_done", "turn_done", "dif_ready", "dec_ready", "egr_ready", "qe_ready", "kk_used",
             "mt_ready", "tt_ready", "at_ready", "tn_copied"))
        ot_ready, y1_done, y1_copied, p2_done, t_updated, again_done, again_copied = (
            sem("dn_" + n) for n in ("ot_ready", "y1_done", "y1_copied", "p2_done", "t_updated", "again_done", "again_copied"))
        ks_done, r_ready, tr_done, vn_ready, ds_done, o_done, s_updated, o_taken = (
            sem("dn_" + n) for n in ("ks_done", "r_ready", "tr_done", "vn_ready", "ds_done", "o_done", "s_updated", "o_taken"))
        eg_arg, eg_ready, s_zero = sem("dn_eg_arg"), sem("dn_eg_ready"), sem("dn_s_zero")
        osq_done, osum_done, oroot_done, y_done = (sem("dn_" + n) for n in ("osq", "osum", "oroot", "y"))
        dve_chain, y1_cleared = sem("dn_dve_chain"), sem("dn_y1_cleared")
        gw_in, bw_in = [sem(f"dn_gw_in{i}") for i in range(2)], [sem(f"dn_bw_in{i}") for i in range(2)]
        gate_done, branch_done, sig_done, gated, kept_done, next_bw = (
            sem("dn_" + n) for n in ("gate_done", "branch_done", "sig_done", "gated", "kept_done", "next_bw"))
        gw_high, gw_low = sem("dn_gw_high"), sem("dn_gw_low")
        kept_out = [sem(f"dn_kept_out{i}") for i in range(2)]

        order = []
        for m in range(2):
            order += [("gram", m), ("attn", m), ("turn", m)]
        for p in range(NT):
            a, b = 2 * p, 2 * p + 1
            for l in range(1, NL):
                order += [("y1", a, l), ("y1", b, l)]
                if p >= 1 and l <= 3:
                    order += [(("read", "solve", "write")[l - 1], m) for m in (a - 2, b - 2)]
                if l == 4:
                    order += [("norm", m) for m in (a - 2, b - 2) if m >= NB // 2]
                if p + 1 < NT:
                    order += {3: [("gram", a + 2)], 4: [("attn", a + 2), ("turn", a + 2)],
                              5: [("gram", b + 2)], 6: [("attn", b + 2), ("turn", b + 2)]}.get(l, [])
                order += [("p2", a, l), ("p2", b, l)]
                if l < NL - 1:
                    order += [("again", a, l), ("again", b, l)]
        for step in ("read", "solve", "write"):
            order += [(step, NB - 2), (step, NB - 1)]
        order += [("norm", NB - 2), ("norm", NB - 1)]
        fill = []
        for c in range(KT):
            for what, r, n in (("gate", 1, KT), ("branch", 1, NH), ("gate", 2, KT), ("branch", 2, NH), ("gate", 0, KT)):
                fill += [("fill", what, c, r, k) for k in range(n)]
        weight = {"gram": 2.2, "attn": 1.2, "turn": 1.0, "y1": 0.8, "p2": 1.0, "again": 0.7,
                  "read": 0.5, "solve": 0.5, "write": 0.2, "norm": 3.0}
        slot = lambda op: weight[op[0]] if op[1] % 2 == 1 or op[0] in ("gram", "attn", "turn", "norm") else 0.0
        whole = sum(slot(op) for op in order)
        mixed, given, seen = [], 0, 0.0
        for op in order:
            mixed.append(op)
            seen += slot(op)
            upto = min(len(fill), int(len(fill) * seen / whole + 0.5))
            mixed += fill[given:upto]
            given = upto
        order = mixed

        def at_level(m, l):
            return (m // 2) * 2 * (NL - 1) + 2 * (l - 1) + m % 2

        def at_again(m, l):
            return (m // 2) * 2 * (NL - 2) + 2 * (l - 1) + m % 2

        def tile(t):
            return slice(t * P, (t + 1) * P)

        def heads(ap):
            return ap[:, :].rearrange("p (h e) -> p h e", h=NH)

        def halves(ap, l, side):
            return ap.rearrange("p h (n s b) -> p h n s b", s=2, b=LEVELS[l])[:, :, :, side, :]

        def packed(bank, part, l):
            return bank[:, 256 * part:256 * part + 256].rearrange("p (h n b) -> p h n b", h=NH, b=LEVELS[l])

        def fill_gate(c, r):
            return 3 * c + (1, 2, 0).index(r)

        def fill_branch(c, r):
            return 2 * c + r - 1

        with nc.Block() as block:
            @block.sync
            def _(sp):
                def load_gate(g):
                    c, r = g // 3, (1, 2, 0)[g % 3]
                    at = C_G + r * DM + c * P
                    if g >= 2:
                        sp.wait_ge(gw_low, g - 1)
                        sp.dma_start(gw[g % 2], w_rows[:, :, at:at + P]).then_inc(gw_in[g % 2], 16)

                def load_branch(b):
                    c, r = b // 2, b % 2 + 1
                    if b >= 2:
                        sp.wait_ge(branch_done, b - 1)
                        sp.dma_start(bw[b % 2], w_branch[r].rearrange("(k p) n -> p k n", p=P)[:, :, c * P:c * P + P])\
                            .then_inc(bw_in[b % 2], 16)

                def keep(sp, c):
                    sp.wait_ge(kept_done, c + 1)
                    sp.dma_start(v["kept_dram"][1, c], stage[:, 1, :]).then_inc(kept_out[1], 16)
                    sp.wait_ge(sig_done, 3 * (c + 1))
                    sp.dma_start(v["kept_dram"][0, c], stage[:, 0, :]).then_inc(kept_out[0], 16)

                for c in range(KT):
                    for i in range(3):
                        load_gate(3 * c + i)
                        if i < 2:
                            load_branch(2 * c + i)
                        if i == 1 and c >= 1:
                            keep(sp, c - 1)
                for k in range(NH):
                    if k == 0:
                        sp.wait_ge(gw_low, 3 * KT)
                    if k == 2:
                        sp.wait_ge(branch_done, 2 * KT)
                    if k == 3:
                        keep(sp, KT - 1)
                        for i in range(2):
                            sp.wait_ge(kept_out[i], 16 * KT)
                    sp.dma_start(v["h2"][:, k, :], w_branch[0][k * P:(k + 1) * P, :]).then_inc(next_bw, 16)
                sp.wait_ge(next_bw, 16 * NH)

            @block.tensor
            def _(pe):
                pe.wait_ge(s_zero, 2)
                for op in order:
                    if op[0] == "fill":
                        what, c, r, k = op[1:]
                        if what == "gate":
                            g = fill_gate(c, r)
                            if k == 0:
                                pe.wait_ge(gw_low, g + 1)
                                if g >= 1:
                                    pe.wait_ge(sig_done, g)
                            for a, b in PRODUCTS:
                                last = pe.matmul(gate_ps[:, :], gw_part[g % 2][a][:, k, :], h_part[b][:, k, :],
                                                 start=(k == 0 and a + b == 0), stop=(k == KT - 1 and a == 1))
                            if k == KT - 1:
                                last.then_inc(gate_done, 1)
                        else:
                            b = fill_branch(c, r)
                            if k == 0:
                                if b >= 2:
                                    pe.wait_ge(bw_in[b % 2], 16 * (b // 2))
                                if b >= 1:
                                    pe.wait_ge(gated, b)
                            last = pe.matmul(branch_ps[:, :], bw[b % 2][:, k, :], yT[:, r, k, :], start=(k == 0), stop=(k == NH - 1))
                            if k == NH - 1:
                                last.then_inc(branch_done, 1)
                        continue
                    kind, m = op[0], op[1]
                    d, t = BATCH[m]
                    tri = cn("upto" if d == 0 else "after")
                    if kind == "gram":
                        if m >= 1:
                            pe.wait_ge(at_ready, m)
                            pe.wait_ge(tn_copied, m)
                        for h in range(NH):
                            last = pe.matmul(pr[0][:, tile(h)], gg[:, t, 4 * d + h:4 * d + h + 1].to_broadcast([P, P]), tri,
                                             start=True, stop=True)
                        last.then_inc(gr_done, 1)
                        for h in range(NH):
                            last = pe.matmul(pr[1][:, tile(h)], qkT[:, 1, h, tile(t)], qkT[:, 1, h, tile(t)],
                                             start=True, stop=True)
                        last.then_inc(kk_done, 1)
                    elif kind == "attn":
                        pe.wait_ge(dif_ready, m + 1)
                        pe.wait_ge(egr_ready, m + 1)
                        for h in range(NH):
                            last = pe.matmul(pr[0][:, tile(h)], qkT[:, 1, h, tile(t)], qkT[:, 0, h, tile(t)],
                                             start=True, stop=True)
                        last.then_inc(qk_done, 1)
                    elif kind == "turn":
                        pe.wait_ge(kk_used, m + 1)
                        pe.wait_ge(tt_ready, m + 1)
                        for h in range(NH):
                            last = pe.transpose(pr[1][:, tile(h)], tt[:, m % 4, h, :], ident)
                        last.then_inc(turn_done, 1)
                    elif kind == "y1":
                        l = op[2]
                        i = at_level(m, l)
                        pe.wait_ge(ot_ready, i + 1)
                        pe.wait_ge(tn_copied, m + 1)
                        if i >= 2:
                            pe.wait_ge(t_updated, i - 1)
                        if l > 1:
                            pe.wait_ge(again_copied, at_again(m, l - 1) + 1)
                        for h in range(NH):
                            last = pe.matmul(packed(lv[d], 0, l)[:, h], ot[:, i % 2, h, :],
                                             halves(tn[:, m % 4, :, :], l, d)[:, h], start=True, stop=True)
                        last.then_inc(y1_done, 1)
                    elif kind == "p2":
                        l = op[2]
                        pe.wait_ge(y1_copied, at_level(m, l) + 1)
                        pe.wait_ge(y1_cleared, at_level(m, l) + 1)
                        for h in range(NH):
                            last = pe.matmul(packed(lv[d], 1, l)[:, h], y1s[:, d, h, :],
                                             halves(tt[:, m % 4, :, :], l, 1 - d)[:, h], start=True, stop=True)
                        last.then_inc(p2_done, 1)
                    elif kind == "again":
                        l = op[2]
                        pe.wait_ge(t_updated, at_level(m, l) + 1)
                        for h in range(NH):
                            last = pe.transpose(lv[d][:, tile(h)], tt[:, m % 4, h, :], ident)
                        last.then_inc(again_done, 1)
                    elif kind == "norm":
                        n = m - NB // 2
                        pe.wait_ge(osq_done, n + 1)
                        pe.wait_ge(o_taken, m + 1)
                        if m < NB - 2:
                            pe.wait_ge(s_updated, m + 1)
                        pe.matmul(sc[m % 2][:, :], ones, mt[:, m % 4, :, :].rearrange("p h e -> p (h e)"),
                                  start=True, stop=True).then_inc(osum_done, 1)
                    elif kind == "read":
                        if m >= 2:
                            pe.wait_ge(s_updated, m - 1)
                        if m >= 1:
                            pe.wait_ge(r_ready, m)
                            if m % 2 == 0:
                                pe.wait_ge(s_updated, m)
                        if m >= NB // 2 + 2:
                            pe.wait_ge(oroot_done, m - NB // 2 - 1)
                        for h in range(NH):
                            last = pe.matmul(sc[m % 2][:, tile(h)], qkT[:, 1, h, tile(t)], state[:, d, h, :],
                                             start=True, stop=True)
                        last.then_inc(ks_done, 1)
                    elif kind == "solve":
                        pe.wait_ge(r_ready, m + 1)
                        pe.wait_ge(t_updated, at_level(m, NL - 1) + 1)
                        for h in range(NH):
                            last = pe.matmul(sc[m % 2][:, tile(h)], tt[:, m % 4, h, :], rhs[:, d, h, :], start=True, stop=True)
                        last.then_inc(tr_done, 1)
                    elif kind == "write":
                        pe.wait_ge(vn_ready, m + 1)
                        pe.wait_ge(at_ready, m + 1)
                        pe.wait_ge(qe_ready, m + 1)
                        for h in range(NH):
                            pe.matmul(sc[m % 2][:, tile(h)], vn[:, d, h, :], at[:, m % 4, h, :], start=True, stop=False)
                            last = pe.matmul(sc[m % 2][:, tile(h)], state[:, d, h, :], qe[:, m % 4, h, :], start=False, stop=True)
                        last.then_inc(o_done, 1)
                        if m < NB - 2:
                            pe.wait_ge(o_taken, m + 1)
                            for h in range(NH):
                                last = pe.matmul(sc[m % 2][:, tile(h)], kTok[:, t, h, :], vnd[:, d, h, :], start=True, stop=True)
                            last.then_inc(ds_done, 1)

            @block.scalar
            def _(act):
                act.wait_ge(eg_arg, 1)
                act.activation(eg[:, :, :, :], eg[:, :, :, :], ACT.Exp).then_inc(eg_ready, 1)

                def high(g):
                    if g >= 3 * KT:
                        return
                    if g >= 2:
                        act.wait_ge(gw_in[g % 2], 16 * (g // 2))
                        act.wait_ge(gate_done, g - 1)
                    act.activation(gw_part[g % 2][0], gw[g % 2], ACT.Copy).then_inc(gw_high, 1)

                high(0)
                high(1)
                for op in order:
                    if op[0] == "fill":
                        what, c, r, k = op[1:]
                        if what == "gate" and k == KT - 1:
                            g = fill_gate(c, r)
                            act.wait_ge(gate_done, g + 1)
                            if r == 0:
                                dst = stage[:, 0, :]
                                if c >= 1:
                                    act.wait_ge(kept_out[0], 16 * c)
                            else:
                                dst = sig[:, :]
                                if r == 2:
                                    act.wait_ge(gated, fill_branch(c, r))
                                elif c >= 1:
                                    act.wait_ge(kept_done, c)
                            act.activation(dst, gate_ps[:, :], ACT.Sigmoid).then_inc(sig_done, 1)
                            high(g + 2)
                        continue
                    kind, m = op[0], op[1]
                    d, t = BATCH[m]
                    if kind == "gram":
                        act.wait_ge(gr_done, m + 1)
                        if m >= 4:
                            act.wait_ge(o_done, m - 3)
                        act.activation(qe[:, m % 4, :, :], heads(pr[0]), ACT.Exp).then_inc(egr_ready, 1)
                        act.wait_ge(dif_ready, m + 1)
                        act.activation(at[:, m % 4, :, :], at[:, m % 4, :, :], ACT.Exp).then_inc(dec_ready, 1)
                    elif kind == "turn":
                        act.wait_ge(turn_done, m + 1)
                        act.activation(tn[:, m % 4, :, :], heads(pr[1]), ACT.Copy).then_inc(tn_copied, 1)
                    elif kind == "again":
                        l = op[2]
                        act.wait_ge(again_done, at_again(m, l) + 1)
                        act.activation(halves(tn[:, m % 4, :, :], l, d), halves(heads(lv[d]), l, d), ACT.Copy).then_inc(again_copied, 1)
                    elif kind == "y1":
                        act.wait_ge(y1_done, at_level(m, op[2]) + 1)
                        act.wait_ge(y1_cleared, at_level(m, op[2]) + 1)
                        act.activation(halves(y1s[:, d, :, :], op[2], d), packed(lv[d], 0, op[2]),
                                       ACT.Copy).then_inc(y1_copied, 1)
                    elif kind == "write" and m < NB // 2:
                        act.wait_ge(o_done, m + 1)
                        act.activation(oT[:, :, tile(t)], heads(sc[m % 2]), ACT.Copy).then_inc(o_taken, 1)
                    elif kind == "norm":
                        n = m - NB // 2
                        act.wait_ge(o_taken, m + 1)
                        if n >= 1:
                            act.wait_ge(osum_done, n)
                        act.activation(mt[:, m % 4, :, :], oT[:, :, tile(t)], ACT.Square).then_inc(osq_done, 1)
                        act.wait_ge(osum_done, n + 1)
                        if n >= 1:
                            act.wait_ge(y_done, n)
                        act.activation(tn[:, m % 4, :, :], heads(sc[m % 2]), ACT.Sqrt,
                                       scale=1.0 / DV, bias=epsc[:, 2:3]).then_inc(oroot_done, 1)

            @block.vector
            def _(dve):
                chain = Chain(dve, dve_chain)
                for d in range(2):
                    dve.memset(state[:, d, :, :], 0.0).then_inc(s_zero, 1)
                chain.add(dve.tensor_copy(eg[:, :, 0, :], cum[:, :, 0:8]))
                chain.add(dve.tensor_tensor(eg[:, :, 1, :], cum[:, :, 8:16], cum[:, :, 0:8], ALU.subtract))
                chain.wait()
                dve.tensor_copy(eg[:, :, 2, :], cum[:, :, 8:16]).then_inc(eg_arg, 1)

                def low(g):
                    if g >= 3 * KT:
                        return
                    dve.wait_ge(gw_high, g + 1)
                    if g >= 2:
                        dve.wait_ge(gate_done, g - 1)
                    dve.tensor_tensor(gw_part[g % 2][1], gw[g % 2], gw_part[g % 2][0].bitcast(F32), ALU.subtract).then_inc(gw_low, 1)

                low(0)
                low(1)
                for op in order:
                    if op[0] == "fill":
                        what, c, r, k = op[1:]
                        if what == "gate" and k == KT - 1:
                            low(fill_gate(c, r) + 2)
                        if what == "branch" and k == NH - 1:
                            b = fill_branch(c, r)
                            dve.wait_ge(branch_done, b + 1)
                            dve.wait_ge(sig_done, fill_gate(c, r) + 1)
                            dst = stage[:, 1, :]
                            if r == 1:
                                if c >= 1:
                                    dve.wait_ge(kept_out[1], 16 * c)
                                dve.tensor_tensor(dst, sig[:, :], branch_ps[:, :], ALU.mult).then_inc(gated, 1)
                            else:
                                dve.tensor_tensor(sig[:, :], sig[:, :], branch_ps[:, :], ALU.mult).then_inc(gated, 1)
                                dve.wait_ge(gated, b + 1)
                                dve.tensor_tensor(dst, dst, sig[:, :], ALU.add).then_inc(kept_done, 1)
                                dve.wait_ge(kept_done, c + 1)
                        continue
                    kind, m = op[0], op[1]
                    d, t = BATCH[m]
                    col = slice(4 * d, 4 * d + 4)
                    if kind == "gram":
                        dve.wait_ge(egr_ready, m + 1)
                        if m >= 4:
                            dve.wait_ge(o_done, m - 3)
                        dd = at[:, m % 4, :, :]
                        chain.link(dve.tensor_tensor(dd, heads(pr[0]), bc(cum[:, t, col], 2, P), ALU.subtract))
                        dve.tensor_tensor(dd, dd, bc(cn("neg_fwd" if d == 0 else "neg_bwd"), 1, NH), ALU.add).then_inc(dif_ready, 1)
                        dve.wait_ge(kk_done, m + 1)
                        dve.wait_ge(dec_ready, m + 1)
                        if m >= 4:
                            dve.wait_ge(ot_ready, at_level(m - 4, NL - 1) + 1)
                            dve.wait_ge(tr_done, m - 3)
                        dve.tensor_tensor(mt[:, m % 4, :, :], heads(pr[1]), dd, ALU.mult).then_inc(kk_used, 1)
                        dve.wait_ge(kk_used, m + 1)
                        dve.tensor_tensor(mt[:, m % 4, :, :], mt[:, m % 4, :, :], bc(beta[:, t, col], 2, P), ALU.mult).then_inc(mt_ready, 1)
                        dve.wait_ge(mt_ready, m + 1)
                        chain.link(dve.scalar_tensor_tensor(tt[:, m % 4, :, :], mt[:, m % 4, :, :], -1.0,
                                                            bc(cn(f"level{d}_1"), 1, NH), ALU.mult, ALU.mult))
                        dve.tensor_tensor(tt[:, m % 4, :, :], tt[:, m % 4, :, :], bc(ident, 1, NH), ALU.add).then_inc(tt_ready, 1)
                    elif kind == "attn":
                        dve.wait_ge(qk_done, m + 1)
                        if m >= 4:
                            dve.wait_ge(o_done, m - 3)
                        dve.tensor_tensor(at[:, m % 4, :, :], heads(pr[0]), at[:, m % 4, :, :], ALU.mult).then_inc(at_ready, 1)
                    elif kind == "p2":
                        l = op[2]
                        dve.wait_ge(p2_done, at_level(m, l) + 1)
                        old = halves(tt[:, m % 4, :, :], l, 1 - d)
                        dve.tensor_tensor(old, old, packed(lv[d], 1, l), ALU.subtract).then_inc(t_updated, 1)
                    elif kind == "read":
                        dve.wait_ge(ks_done, m + 1)
                        dve.wait_ge(eg_ready, 1)
                        r = rhs[:, d, :, :]
                        chain.link(dve.tensor_tensor(r, heads(sc[m % 2]), bc(eg[:, t, 0, col], 2, DV), ALU.mult))
                        dve.tensor_tensor(r, vTok[:, t, :, :], r, ALU.subtract).then_inc(r_ready, 1)
                    elif kind == "solve":
                        dve.wait_ge(tr_done, m + 1)
                        chain.link(dve.tensor_tensor(vn[:, d, :, :], heads(sc[m % 2]), bc(beta[:, t, col], 2, DV), ALU.mult))
                        if m >= 2:
                            dve.wait_ge(ds_done, m - 1)
                        dve.tensor_tensor(vnd[:, d, :, :], vn[:, d, :, :], bc(eg[:, t, 1, col], 2, DV), ALU.mult).then_inc(vn_ready, 1)
                    elif kind == "write":
                        dve.wait_ge(o_done, m + 1)
                        if m >= NB // 2:
                            dve.tensor_tensor(oT[:, :, tile(t)], oT[:, :, tile(t)], heads(sc[m % 2]), ALU.add).then_inc(o_taken, 1)
                        if m < NB - 2:
                            s = state[:, d, :, :]
                            chain.link(dve.tensor_tensor(s, s, bc(eg[:, t, 2, col], 2, DV), ALU.mult))
                            dve.wait_ge(ds_done, m + 1)
                            dve.tensor_tensor(s, s, heads(sc[m % 2]), ALU.add).then_inc(s_updated, 1)
                    elif kind == "norm":
                        r, o = tn[:, m % 4, :, :], oT[:, :, tile(t)]
                        dve.wait_ge(o_taken, m + 1)
                        dve.wait_ge(oroot_done, m - NB // 2 + 1)
                        chain.link(dve.reciprocal(r, r))
                        chain.link(dve.tensor_tensor(r, r, o, ALU.mult))
                        chain.link(dve.tensor_tensor(r, r, bc(sml[:, SM_NORM:SM_NORM + NH], 2, P), ALU.mult))
                        dve.tensor_tensor(yT[:, 0, :, tile(t)], yT[:, 0, :, tile(t)], r, ALU.mult).then_inc(y_done, 1)

            @block.gpsimd
            def _(pool):
                v["zero_last"](pool)
                for op in order:
                    if op[0] == "fill":
                        continue
                    kind, m = op[0], op[1]
                    d, t = BATCH[m]
                    if kind == "gram":
                        pool.wait_ge(egr_ready, m + 1)
                        pool.tensor_tensor(qe[:, m % 4, :, :], qe[:, m % 4, :, :], qkT[:, 0, :, tile(t)], ALU.mult).then_inc(qe_ready, 1)
                    elif kind == "y1":
                        l = op[2]
                        i = at_level(m, l)
                        if i >= 2:
                            pool.wait_ge(p2_done, i - 1)
                        pool.memset(y1s[:, d, :, :], 0.0).then_inc(y1_cleared, 1)
                        pool.wait_ge(mt_ready, m + 1)
                        if i >= 2:
                            pool.wait_ge(y1_done, i - 1)
                        pool.tensor_tensor(ot[:, i % 2, :, :], mt[:, m % 4, :, :], bc(cn(f"level{d}_{LEVELS[l]}"), 1, NH),
                                           ALU.mult).then_inc(ot_ready, 1)


def merge(nc, sem, sb, pb, cn, v):
    w_in, w_branch, w_out = v["w_in"], v["w_branch"], v["w_out"]
    sml, epsc, yT, h2, rows_all, flag = (v[k] for k in ("sml", "epsc", "yT", "h2", "rows_all", "flag"))
    ident, ones = v["ident"], v["ones"]
    st = ExitStack()
    with st:
        wo = v["wraw"][:, 0:4, :].rearrange("p (r a) (b n) -> p r (a b) n", r=2, n=512)
        bw = h2[:, :, :]
        hT = sb(st, "h2T", [P, KT, SEQ])
        merged = v["wraw"][:, 4:6, :].rearrange("p a (b n) -> p (a b) n", n=SEQ)
        sig = sb(st, "sig", [P, KT, SEQ])
        lng, lnb = sb(st, "lng2", [P, DM]), sb(st, "lnb2", [P, DM])
        stats, mv, rstd, nmr = sb(st, "stats2", [P, NT, 2, 6]), sb(st, "mv2", [P, NT, 2]), sb(st, "rstd2", [P, NT]), sb(st, "nmr2", [P, NT])
        r4 = lambda name: sb(st, name, [P, NT, NE])
        sco, sel, rank, gt, pos, dest, alt, prod = (r4(n) for n in ("sco", "sel", "rank", "gt", "pos", "dest", "alt", "prod"))
        onek = sb(st, "onek", [P, 2, NT, NE])
        mask = r4("mask")
        earlier = sb(st, "earlier", [P, NT + 1, NE])
        hi, lo = sb(st, "hi", [P, NT * NG, 2]), sb(st, "lo", [P, NT * NG, 2])
        g3 = sb(st, "g3", [P, 4, NT * NG])
        gm = sb(st, "gm", [P, 2, NT])
        sk = sb(st, "sk", [P, 4, NT])
        dk = sb(st, "dk", [P, 2, NT])
        dki = sb(st, "dki", [P, 2, NT], I32)
        pay = sb(st, "pay", [P, NT, 2, 4], I32)
        ce = sb(st, "ce", [P, 5, NE])
        eo = sb(st, "eo", [1, OVER, NE])
        eov = sb(st, "eov", [1, 1 + OVER])
        far = sb(st, "far", [P, TABLE * 4 // P], I32)
        gp = [pb(st, f"gp{i}") for i in range(3)]
        yp = [pb(st, f"yp{i}") for i in range(3)]
        lp, cp = pb(st, "lp"), pb(st, "cp")
        kept_in, wo_in, h_in = [sem(f"kept_in{i}") for i in range(KT)], [sem(f"wo_in{i}") for i in range(2)], [sem(f"h_in{i}") for i in range(NT)]
        ln_in, far_out, h2_out, tab_in = sem("ln2_in"), sem("far_out"), sem("h2_out"), sem("tab_in")
        far_set, branch_done, part_done, merged_sum = (
            sem("mg_" + n) for n in ("far_set", "branch_done", "part_done", "merged_sum"))
        out_done, res_done = sem("mg_out_done"), sem("mg_res_done")
        stats_ready, std_ready, scale_ready, norm_ready, gmul_ready, h2_ready = (
            sem(f"ln2_{n}") for n in ("stats", "std", "scale", "norm", "gmul", "h"))
        turned, turn_copied, logit_done, score_done = sem("mg_turned"), sem("mg_turn_copied"), sem("mg_logits"), sem("mg_scores")
        earlier_done = sem("mg_earlier")
        mask_done, pos_done, pay_done, scattered = sem("mg_mask"), sem("mg_pos"), sem("mg_pay"), sem("mg_scattered")
        dve_chain = sem("mg_dve_chain")
        experts_in = [sem(f"experts_in{u}") for u in range(NRAW)]

        def first_experts(sp):
            for u in range(NRAW):
                w = (v["moe_w1"], v["moe_w2"], v["moe_w3"])[u // 2].rearrange("e (p k) n -> e p (k n)", p=P)
                sp.dma_start(v["wraw"][:, u, :], w[0][:, (u % 2) * HALF:(u % 2 + 1) * HALF]).then_inc(experts_in[u], 16)

        with nc.Block() as block:
            @block.sync
            def _(sp):
                for c in range(KT):
                    sp.dma_start(sig[:, c, :], v["kept_dram"][0, c]).then_inc(kept_in[c], 16)
                    sp.dma_start(merged[:, c, :], v["kept_dram"][1, c]).then_inc(kept_in[c], 16)
                for half in range(2):
                    sp.dma_start(wo[:, half, :, :], w_out.rearrange("(k p) n -> p k n", p=P)[:, :, half * 512:half * 512 + 512]).then_inc(wo_in[half], 16)
                sp.dma_start(lng[:, :], v["ln_mix_g"].to_broadcast([P, DM])).then_inc(ln_in, 16)
                sp.dma_start(lnb[:, :], v["ln_mix_b"].to_broadcast([P, DM])).then_inc(ln_in, 16)
                sp.wait_ge(far_set, 1)
                sp.dma_start(v["slots_dram"].rearrange("(p a) b -> p (a b)", p=P), far[:, :]).then_inc(far_out, 16)
                sp.wait_ge(branch_done, KT)
                for t in range(NT):
                    sp.dma_start(h2[:, t, :], v["h_dram"][t * P:(t + 1) * P, :]).then_inc(h_in[t], 16)
                for t in range(NT):
                    sp.wait_ge(h2_ready, t + 1)
                    sp.dma_start(v["h2_dram"][t * P:(t + 1) * P, :], h2[:, t, :]).then_inc(h2_out, 16)
                    if t == 1:
                        sp.wait_ge(out_done, 2 * NT)
                        first_experts(sp)
                sp.wait_ge(scattered, 16 * 2 * NT)
                sd = v["slots_dram"]
                for half in range(2):
                    rows = slice(half * SLOTS, (half + 1) * SLOTS)
                    sp.dma_start(rows_all[rows, 0:NE, :], sd[0:SLOTS * NE, :].rearrange("(s e) w -> s e w", e=NE)).then_inc(tab_in, 16)
                    sp.dma_start(rows_all[rows, NE:NE + OVER, :], sd[SLOTS * NE:, :].rearrange("(s e) w -> s e w", e=OVER)).then_inc(tab_in, 16)
                sp.wait_ge(tab_in, 64)
                sp.wait_ge(h2_out, 16 * NT)
                for u in range(NRAW):
                    sp.wait_ge(experts_in[u], 16)

            @block.tensor
            def _(pe):
                for c in range(KT):
                    if c >= 3:
                        pe.wait_ge(part_done, c - 2)
                    for k in range(NH):
                        last = pe.matmul(yp[c % 3][:, :], bw[:, k, c * P:(c + 1) * P], yT[:, 0, k, :],
                                         start=(k == 0), stop=(k == NH - 1))
                    last.then_inc(branch_done, 1)
                pe.wait_ge(merged_sum, KT)
                wr = sml[:, SM_RW:SM_RW + KT * NE].rearrange("p (k n) -> p k n", k=KT)

                def project(t):
                    for half in range(2):
                        n = 2 * t + half
                        if n < 2:
                            pe.wait_ge(wo_in[half], 16)
                        if n >= 3:
                            pe.wait_ge(res_done, n - 2)
                        for k in range(KT):
                            last = pe.matmul(yp[n % 3][:, :], merged[:, k, t * P:(t + 1) * P], wo[:, half, k, :],
                                             start=(k == 0), stop=(k == KT - 1))
                        last.then_inc(out_done, 1)

                def turn(t):
                    pe.wait_ge(h2_ready, t + 1)
                    for half in range(2):
                        if t >= 1:
                            pe.wait_ge(turn_copied, 2 * t + half - 1)
                        for k in range(4):
                            last = pe.transpose(gp[half][:, k * P:(k + 1) * P], h2[:, t, 4 * half + k::KT], ident)
                        last.then_inc(turned, 1)

                def logits(t):
                    pe.wait_ge(turn_copied, 2 * t + 2)
                    for k in range(KT):
                        last = pe.matmul(lp[:, t * NE:(t + 1) * NE], hT[:, k, t * P:(t + 1) * P], wr[:, k, :],
                                         start=(k == 0), stop=(k == KT - 1))
                    last.then_inc(logit_done, 1)

                for t in range(NT):
                    project(t)
                    if t >= 1:
                        turn(t - 1)
                    if t >= 2:
                        logits(t - 2)
                turn(NT - 1)
                logits(NT - 2)
                logits(NT - 1)
                pe.wait_ge(earlier_done, NT)
                pe.matmul(cp[:, 0:NT * NE], cn("before"), mask[:, :, :].rearrange("p t e -> p (t e)"), start=True, stop=False)
                pe.matmul(cp[:, 0:NT * NE], ones, earlier[:, 0:NT, :].rearrange("p t e -> p (t e)"), start=False, stop=True)
                pe.matmul(cp[:, NT * NE:(NT + 1) * NE], ones, earlier[:, NT, :], start=True, stop=True).then_inc(pos_done, 1)

            @block.scalar
            def _(act):
                def copy_turned(t):
                    for half in range(2):
                        act.wait_ge(turned, 2 * t + half + 1)
                        act.activation(hT[:, 4 * half:4 * half + 4, t * P:(t + 1) * P],
                                       gp[half][:, :].rearrange("p (k s) -> p k s", k=4), ACT.Copy).then_inc(turn_copied, 1)

                def before(t):
                    if t >= 1:
                        copy_turned(t - 1)

                layer_norm_act(act, h2, mv, rstd, nmr, epsc[:, 0:1], stats_ready, std_ready, scale_ready, norm_ready, before)
                copy_turned(NT - 1)
                act.wait_ge(logit_done, NT)
                act.activation(sco[:, :, :], lp[:, 0:NT * NE].rearrange("p (t e) -> p t e", t=NT), ACT.Sigmoid).then_inc(score_done, 1)

            @block.vector
            def _(dve):
                chain = Chain(dve, dve_chain)
                dve.memset(far[:, :], FAR).then_inc(far_set, 1)
                chain.add(dve.memset(earlier[:, 0, :], 0.0))
                for c in range(KT):
                    dve.wait_ge(kept_in[c], 32)
                    dve.wait_ge(branch_done, c + 1)
                    dve.tensor_tensor(sig[:, c, :], sig[:, c, :], yp[c % 3][:, :], ALU.mult).then_inc(part_done, 1)
                    dve.wait_ge(part_done, c + 1)
                    dve.tensor_tensor(merged[:, c, :], merged[:, c, :], sig[:, c, :], ALU.add).then_inc(merged_sum, 1)
                def x_ready(t):
                    dve.wait_ge(h_in[t], 16)
                    for half in range(2):
                        n = 2 * t + half
                        dve.wait_ge(out_done, n + 1)
                        r = h2[:, t, half * 512:half * 512 + 512]
                        dve.scalar_tensor_tensor(r, r, ALPHA, yp[n % 3][:, :], ALU.mult, ALU.add).then_inc(res_done, 1)
                    dve.wait_ge(res_done, 2 * t + 2)
                layer_norm_dve(dve, chain, h2, stats, mv, rstd, nmr, x_ready, stats_ready, std_ready, scale_ready,
                               norm_ready, gmul_ready, lng[:, :], ln_in, 0)
                rb = sml[:, SM_RB:SM_RB + NE]
                flat = lambda ap: ap.rearrange("p t (g e) -> p (t g) e", e=EPG)
                dve.wait_ge(score_done, 1)
                chain.link(dve.tensor_tensor(sel[:, :, :], sco[:, :, :], bc(rb, 1, NT), ALU.add))
                sv = flat(sel[:, :, :])
                chain.add(dve.tensor_tensor(hi[:, :, :], sv[:, :, 0::2], sv[:, :, 1::2], ALU.max))
                chain.link(dve.tensor_tensor(lo[:, :, :], sv[:, :, 0::2], sv[:, :, 1::2], ALU.min))
                chain.add(dve.tensor_tensor(g3[:, 0, :], hi[:, :, 0], hi[:, :, 1], ALU.max))
                chain.add(dve.tensor_tensor(g3[:, 1, :], hi[:, :, 0], hi[:, :, 1], ALU.min))
                chain.link(dve.tensor_tensor(g3[:, 2, :], lo[:, :, 0], lo[:, :, 1], ALU.max))
                chain.link(dve.tensor_tensor(g3[:, 1, :], g3[:, 1, :], g3[:, 2, :], ALU.max))
                chain.link(dve.tensor_tensor(g3[:, 0, :], g3[:, 0, :], g3[:, 1, :], ALU.add))
                gs = g3[:, 0, :].rearrange("p (t g) -> p t g", t=NT)
                eq = g3[:, 1, :].rearrange("p (t g) -> p t g", t=NT)
                chain.link(dve.tensor_reduce(gm[:, 0, :], gs, AX.X, ALU.max))
                chain.link(dve.tensor_tensor(eq, gs, bc(gm[:, 0, :], 2, NG), ALU.is_equal))
                chain.link(dve.tensor_tensor(eq, eq, bc(cn("down"), 1, NT), ALU.mult))
                chain.link(dve.tensor_reduce(gm[:, 1, :], eq, AX.X, ALU.max))
                chain.link(dve.tensor_tensor(eq, eq, bc(gm[:, 1, :], 2, NG), ALU.is_equal))
                rk = flat(rank[:, :, :])
                gv = flat(gt[:, :, :])
                chain.link(dve.tensor_copy(rk, bc(cn("place"), 1, NT * NG)))
                for s in range(1, EPG):
                    chain.link(dve.tensor_tensor(gv[:, :, 0:EPG - s], sv[:, :, s:], sv[:, :, 0:EPG - s], ALU.is_gt))
                    chain.link(dve.tensor_tensor(rk[:, :, 0:EPG - s], rk[:, :, 0:EPG - s], gv[:, :, 0:EPG - s], ALU.add))
                    chain.link(dve.tensor_tensor(rk[:, :, s:], rk[:, :, s:], gv[:, :, 0:EPG - s], ALU.subtract))
                for k in range(2):
                    chain.add(dve.scalar_tensor_tensor(flat(onek[:, k, :, :]), rk, float(k), bc(g3[:, 1, :], 2, EPG),
                                                       ALU.is_equal, ALU.mult))
                chain.wait()
                dve.tensor_tensor(mask[:, :, :], onek[:, 0, :, :], onek[:, 1, :, :], ALU.add).then_inc(mask_done, 1)
                dve.wait_ge(mask_done, 1)
                for t in range(NT):
                    dve.tensor_tensor(earlier[:, t + 1, :], earlier[:, t, :], mask[:, t, :], ALU.add).then_inc(earlier_done, 1)
                    if t < NT - 1:
                        dve.wait_ge(earlier_done, t + 1)
                for k in range(2):
                    chain.link(dve.tensor_tensor(prod[:, :, :], onek[:, k, :, :], sco[:, :, :], ALU.mult))
                    chain.link(dve.tensor_reduce(sk[:, k, :], prod[:, :, :], AX.X, ALU.add))
                chain.link(dve.tensor_tensor(sk[:, 2, :], sk[:, 0, :], sk[:, 1, :], ALU.add))
                chain.link(dve.reciprocal(sk[:, 3, :], sk[:, 2, :]))
                for k in range(2):
                    chain.add(dve.tensor_copy(pay[:, :, k, 0], cn("token")))
                    chain.add(dve.tensor_scalar(pay[:, :, k, 1], cn("token"), float(k * SEQ), None, ALU.add))
                    chain.add(dve.memset(pay[:, :, k, 3], 0))
                    chain.add(dve.tensor_tensor(pay[:, :, k, 2].bitcast(F32), sk[:, k, :], sk[:, 3, :], ALU.mult))
                dve.wait_ge(pos_done, 1)
                chain.add(dve.tensor_copy(pos[:, :, :], cp[:, 0:NT * NE].rearrange("p (t e) -> p t e", t=NT)))
                chain.add(dve.tensor_copy(ce[:, 0, :], cp[:, NT * NE:(NT + 1) * NE]))
                chain.add(dve.memset(ce[:, 1, :], 0.0))
                chain.add(dve.memset(ce[:, 4, :], 1.0))
                chain.link(dve.memset(gt[:, :, :], 0.0))
                for b in range(1, SEQ // SLOTS):
                    chain.add(dve.scalar_tensor_tensor(ce[:, 1, :], ce[:, 0, :], float(b * SLOTS), ce[:, 1, :], ALU.is_gt, ALU.add))
                    chain.link(dve.scalar_tensor_tensor(gt[:, :, :], pos[:, :, :], float(b * SLOTS), gt[:, :, :], ALU.is_ge, ALU.add))
                chain.link(dve.tensor_tensor_scan(ce[:, 2, :], ce[:, 4, :], ce[:, 1, :], 0.0, ALU.mult, ALU.add))
                chain.link(dve.tensor_tensor(ce[:, 3, :], ce[:, 2, :], ce[:, 1, :], ALU.subtract))
                chain.add(dve.tensor_tensor(eo[:, :, :], bc(ce[0:1, 2, :], 1, OVER), bc(cn("expert", 1)[:, 0:OVER], 2, NE), ALU.is_le))
                chain.link(dve.scalar_tensor_tensor(pos[:, :, :], gt[:, :, :], -float(SLOTS), pos[:, :, :], ALU.mult, ALU.add))
                chain.link(dve.tensor_reduce(eov[:, 1:1 + OVER], eo[:, :, :], AX.X, ALU.add))
                chain.link(dve.tensor_scalar(eov[:, 1:1 + OVER], eov[:, 1:1 + OVER], float(NE - 1), None, ALU.min))
                chain.link(dve.tensor_copy(eov[:, 0:1], ce[0:1, 2, NE - 1:NE]))
                chain.add(dve.tensor_copy(flag[:, :], eov[:, :]))
                chain.link(dve.scalar_tensor_tensor(dest[:, :, :], pos[:, :, :], float(NE), bc(cn("expert"), 1, NT), ALU.mult, ALU.add))
                chain.link(dve.scalar_tensor_tensor(alt[:, :, :], pos[:, :, :], float(OVER), gt[:, :, :], ALU.mult, ALU.add))
                chain.link(dve.tensor_tensor(alt[:, :, :], alt[:, :, :], bc(ce[:, 3, :], 1, NT), ALU.add))
                chain.link(dve.scalar_tensor_tensor(alt[:, :, :], alt[:, :, :], float(SLOTS * NE - 1), dest[:, :, :], ALU.add, ALU.subtract))
                chain.link(dve.scalar_tensor_tensor(alt[:, :, :], gt[:, :, :], 1.0, alt[:, :, :], ALU.min, ALU.mult))
                chain.link(dve.tensor_tensor(dest[:, :, :], dest[:, :, :], alt[:, :, :], ALU.add))
                for k in range(2):
                    chain.link(dve.tensor_tensor(prod[:, :, :], onek[:, k, :, :], dest[:, :, :], ALU.mult))
                    chain.link(dve.tensor_reduce(dk[:, k, :], prod[:, :, :], AX.X, ALU.add))
                dve.tensor_copy(dki[:, :, :], dk[:, :, :]).then_inc(pay_done, 1)
                dve.memset(rows_all[:, NE + OVER, :], FAR)

            @block.gpsimd
            def _(pool):
                v["zero_last"](pool)
                for t in range(NT):
                    pool.wait_ge(gmul_ready, t + 1)
                    pool.wait_ge(ln_in, 32)
                    pool.tensor_tensor(h2[:, t, :], h2[:, t, :], lnb[:, :], ALU.add).then_inc(h2_ready, 1)
                pool.wait_ge(pay_done, 1)
                pool.wait_ge(far_out, 16)
                for t in range(NT):
                    for k in range(2):
                        pool.indirect_dma_start(v["slots_dram"], bass.IndirectOffsetOnAxis(ap=dki[:, k, t:t + 1], axis=0),
                                                pay[:, t, k, :], None, bounds_check=TABLE - 1, oob_is_err=False).then_inc(scattered, 16)
                pool.wait_ge(scattered, 16 * 2 * NT)


def experts(nc, sem, sb, pb, cn, v):
    rows_all, flag = v["rows_all"], v["flag"]
    w1, w3, w2 = (v[k] for k in ("moe_w1", "moe_w3", "moe_w2"))
    ident = v["ident"]
    w_dram = [w1.rearrange("e (p k) n -> e p (k n)", p=P), w3.rearrange("e (p k) n -> e p (k n)", p=P),
              w2.rearrange("e (p k) n -> e p (k n)", p=P)]
    FT = FE // P
    UNITS = 6
    st = ExitStack()
    with st:
        raw = v["wraw"]
        whi, wlo = sb(st, "whi", [P, NSPLIT, HALF], F32R), sb(st, "wlo", [P, NSPLIT, HALF], F32R)
        xg = sb(st, "xg", [SLOTS, 2, DM])
        tok = sb(st, "tok", [SLOTS, 2, 1], I32)
        idx = sb(st, "idx", [SLOTS, 2, 1], I32)
        gate = sb(st, "gate", [P, 2, 1])
        xs = sb(st, "xs", [P, 2, KT, 2, SLOTS], F32R)
        hc = sb(st, "hc", [P, 2, FE])
        sl = sb(st, "sl", [P, FT * SLOTS])
        prd = sb(st, "prd", [P, FT * SLOTS])
        ac = sb(st, "ac", [P, FT, 2, SLOTS], F32R)
        ylow = sb(st, "ylow", [SLOTS, DM])
        ys = sb(st, "ys", [SLOTS, 2, DM])
        tx, gb = pb(st, "tx"), pb(st, "gb")
        hb = [pb(st, f"hb{i}") for i in range(4)]
        yb = [pb(st, f"yb{i}") for i in range(2)]

        class Signals:

            def __init__(self, tag):
                self.w_in = [sem(f"{tag}_w_in{i}") for i in range(6)]
                self.gathered = [sem(f"{tag}_gathered{i}") for i in range(2)]
                self.hi_done = sem(f"{tag}_hi_done")
                self.lo_done = sem(f"{tag}_lo_done")
                self.part_used = sem(f"{tag}_part_used")
                self.gate_ready = sem(f"{tag}_gate_ready")
                self.row_ready = sem(f"{tag}_row_ready")
                self.index_ready = sem(f"{tag}_index_ready")
                self.x_turned = sem(f"{tag}_x_turned")
                self.xhi_done = sem(f"{tag}_xhi_done")
                self.xlo_done = sem(f"{tag}_xlo_done")
                self.h_copied = sem(f"{tag}_h_copied")
                self.paired = sem(f"{tag}_paired")
                self.silu_done = sem(f"{tag}_silu_done")
                self.act_done = sem(f"{tag}_act_done")
                self.ahi_done = sem(f"{tag}_ahi_done")
                self.alo_done = sem(f"{tag}_alo_done")
                self.ylow_ready = sem(f"{tag}_ylow_ready")
                self.y_ready = sem(f"{tag}_y_ready")
                self.scattered = sem(f"{tag}_scattered")
                self.stored = sem(f"{tag}_stored")
                self.steps_begun = sem(f"{tag}_steps_begun")
                self.turns_begun = sem(f"{tag}_turns_begun")

        def wait(eng, s, value):
            if not (isinstance(value, int) and value <= 0):
                eng.wait_ge(s, value)

        def blocks(eng, count, step):
            for e in range(2):
                step(e, e, 0)
            with eng.Fori(1, count // 2) as it:
                for j in range(2):
                    step(it * 2 + j, j, it)

        W1, W2, W3 = (0, 1), (2, 3), (4, 5)

        def sync_program(sp, S, count, expert, begun):
            def load(e, u, which, ex, half):
                if begun and isinstance(e, int) and e == 0:
                    sp.sem_inc(S.w_in[u], 16)
                    return
                wait(sp, S.lo_done, e * UNITS + (u + 1 - NRAW))
                sp.dma_start(raw[:, u, :], w_dram[which][bass.ds(ex, 1), :, half * HALF:(half + 1) * HALF].rearrange("o p n -> (o p) n"))\
                    .then_inc(S.w_in[u], 16)

            def step(e, j, it):
                ex = expert(sp, e)
                before = ex if isinstance(e, int) and e == 0 else expert(sp, e - 1)
                for half in range(2):
                    load(e, W1[half], 0, ex, half)
                for half in range(2):
                    load(e, W2[half], 2, before, half)
                for half in range(2):
                    load(e, W3[half], 1, ex, half)
            blocks(sp, count, step)
            last = expert(sp, count - 1)
            for half in range(2):
                load(count, half, 2, last, half)

        def pool_program(pool, S, count, first):
            def fetch(e, j):
                wait(pool, S.x_turned, e - 1)
                pool.tensor_copy(tok[:, j, :], rows_all[0:SLOTS, bass.ds(e + first, 1), 0:1].rearrange("p o w -> p (o w)")).then_inc(S.index_ready, 1)
                wait(pool, S.index_ready, e + 1)
                pool.sem_inc(S.steps_begun, 1)
                pool.indirect_dma_start(xg[:, j, :], None, v["h2_dram"], bass.IndirectOffsetOnAxis(ap=tok[:, j, :], axis=0),
                                        bounds_check=SEQ - 1, oob_is_err=False).then_inc(S.gathered[j], 16)

            def store(e, j):
                pool.tensor_copy(gate[:, j, :], rows_all[:, bass.ds(e + first, 1), 2:3].bitcast(F32).rearrange("p o w -> p (o w)"))\
                    .then_inc(S.gate_ready, 1)
                pool.tensor_copy(idx[:, j, :], rows_all[0:SLOTS, bass.ds(e + first, 1), 1:2].rearrange("p o w -> p (o w)")).then_inc(S.row_ready, 1)
                wait(pool, S.row_ready, e + 1)
                pool.wait_ge(S.y_ready, e * 2 + 2)
                pool.sem_inc(S.steps_begun, 1)
                pool.indirect_dma_start(v["y_dram"], bass.IndirectOffsetOnAxis(ap=idx[:, j, :], axis=0),
                                        ys[:, j, :], None, bounds_check=2 * SEQ - 1, oob_is_err=False).then_inc(S.scattered, 16)
                pool.wait_ge(S.scattered, e * 16 + 16)
                pool.sem_inc(S.stored, 1)

            def step(e, j, it):
                fetch(e + 1, 1 - j)
                if not (isinstance(e, int) and e == 0):
                    store(e - 1, 1 - j)
            fetch(0, 0)
            blocks(pool, count, step)
            store(count - 1, 1)
            pool.wait_ge(S.gathered[0], 16 * (count // 2 + 1))

        def tensor_program(pe, S, count):
            def turn(e, j, round_):
                wait(pe, S.xlo_done, e)
                pe.wait_ge(S.gathered[j], round_ * 16 + 16)
                pe.sem_inc(S.turns_begun, 1)
                for k in range(KT):
                    last = pe.transpose(tx[:, k * SLOTS:(k + 1) * SLOTS], xg[:, j, k::KT], ident[0:SLOTS, 0:SLOTS])
                last.then_inc(S.x_turned, 1)

            def first_products(e, j, u, w, half):
                part = (UNITS * j + u) % NSPLIT
                bank = hb[2 * j + w]
                pe.wait_ge(S.lo_done, e * UNITS + (u + 1))
                for kk in range(4):
                    lhs = xs[:, j, 4 * half + kk, :, :].rearrange("p a s -> p (a s)")
                    cols = slice(kk * FE, (kk + 1) * FE)
                    pe.matmul(bank[:, :], lhs, whi[:, part, cols], start=(half == 0 and kk == 0), stop=False)
                    last = pe.matmul(bank[:, :], lhs, wlo[:, part, cols], start=False, stop=(half == 1 and kk == 3))
                last.then_inc(S.part_used, 1)

            def add_pairs(e):
                for w in range(2):
                    pe.wait_ge(S.h_copied, e * 2 + (w + 1))
                    for f in range(FT):
                        last = pe.matmul(gb[:, (w * FT + f) * SLOTS:(w * FT + f + 1) * SLOTS], hc[:, w, f::FT], cn("pair"),
                                         start=True, stop=True)
                last.then_inc(S.paired, 1)

            def second_products(e, body, bj, u, half):
                part = (UNITS * bj + u) % NSPLIT
                pe.wait_ge(S.alo_done, e + 1)
                wait(pe, S.y_ready, e * 2)
                pe.wait_ge(S.lo_done, body * UNITS + (u + 1))
                for kk in range(2):
                    k = 2 * half + kk
                    lhs = ac[:, k, :, :].rearrange("p a s -> p (a s)")
                    for c in range(2):
                        cols = slice(kk * DM + c * 512, kk * DM + c * 512 + 512)
                        pe.matmul(yb[c][:, :], lhs, whi[:, part, cols], start=(k == 0), stop=False)
                        last = pe.matmul(yb[c][:, :], lhs, wlo[:, part, cols], start=False, stop=(k == FT - 1))
                last.then_inc(S.part_used, 1)

            def step(e, j, it):
                head = isinstance(e, int) and e == 0
                pe.wait_ge(S.xlo_done, e + 1)
                first_products(e, j, W1[0], 0, 0)
                if not head:
                    add_pairs(e - 1)
                first_products(e, j, W1[1], 0, 1)
                for half in range(2):
                    if head:
                        pe.wait_ge(S.lo_done, W2[half] + 1)
                        pe.wait_ge(S.part_used, W2[half])
                        pe.sem_inc(S.part_used, 1)
                    else:
                        second_products(e - 1, e, j, W2[half], half)
                first_products(e, j, W3[0], 1, 0)
                turn(e + 1, 1 - j, it + j)
                first_products(e, j, W3[1], 1, 1)
            turn(0, 0, 0)
            blocks(pe, count, step)
            add_pairs(count - 1)
            for half in range(2):
                second_products(count - 1, count, 0, half, half)

        def scalar_program(act, S, count):
            def high(e, j, u):
                act.wait_ge(S.w_in[u], e * 16 + 16)
                wait(act, S.part_used, e * UNITS + (u + 1 - NSPLIT))
                act.activation(whi[:, (UNITS * j + u) % NSPLIT, :], raw[:, u, :], ACT.Copy).then_inc(S.hi_done, 1)

            def x_high(e, j):
                act.wait_ge(S.x_turned, e + 1)
                wait(act, S.part_used, e * UNITS - UNITS)
                act.activation(xs[:, j, :, 0, :], tx[:, :].rearrange("p (k s) -> p k s", k=KT), ACT.Copy).then_inc(S.xhi_done, 1)

            def copy_h(e, j, w):
                act.wait_ge(S.part_used, e * UNITS + ((W1, W3)[w][1] + 1))
                act.activation(hc[:, w, :], hb[2 * j + w][:, :], ACT.Copy).then_inc(S.h_copied, 1)

            def gated(e):
                act.wait_ge(S.paired, e + 1)
                act.activation(sl[:, :], gb[:, 0:FT * SLOTS], ACT.Silu).then_inc(S.silu_done, 1)

            def act_high(e):
                act.wait_ge(S.act_done, e + 1)
                wait(act, S.part_used, e * UNITS + (W2[1] + 1))
                act.activation(ac[:, :, 0, :], prd[:, :].rearrange("p (f s) -> p f s", f=FT), ACT.Copy).then_inc(S.ahi_done, 1)

            def weigh_y(e, j, used):
                act.wait_ge(S.part_used, used)
                wait(act, S.y_ready, e * 2)
                act.wait_ge(S.gate_ready, e + 1)
                for half in range(2):
                    act.activation(ylow[:, half * 512:half * 512 + 512], yb[half][SLOTS:, :], ACT.Copy, scale=gate[SLOTS:, j, 0:1])\
                        .then_inc(S.ylow_ready, 1)

            def step(e, j, it):
                head = isinstance(e, int) and e == 0
                high(e, j, 0)
                high(e, j, 1)
                if not head:
                    copy_h(e - 1, 1 - j, 1)
                high(e, j, 2)
                high(e, j, 3)
                if head:
                    x_high(0, 0)
                if not head:
                    gated(e - 1)
                    act_high(e - 1)
                high(e, j, 4)
                copy_h(e, j, 0)
                high(e, j, 5)
                if not head:
                    weigh_y(e - 1, 1 - j, e * UNITS + (W2[1] + 1))
                x_high(e + 1, 1 - j)
            blocks(act, count, step)
            high(count, 0, 0)
            high(count, 0, 1)
            copy_h(count - 1, 1, 1)
            gated(count - 1)
            act_high(count - 1)
            weigh_y(count - 1, 1, count * UNITS + 2)

        def vector_program(dve, S, count):
            def low(e, j, u):
                part = (UNITS * j + u) % NSPLIT
                dve.wait_ge(S.hi_done, e * UNITS + (u + 1))
                dve.tensor_tensor(wlo[:, part, :], raw[:, u, :], whi[:, part, :].bitcast(F32), ALU.subtract).then_inc(S.lo_done, 1)

            def x_low(e, j):
                dve.wait_ge(S.xhi_done, e + 1)
                dve.tensor_tensor(xs[:, j, :, 1, :], tx[:, :].rearrange("p (k s) -> p k s", k=KT),
                                  xs[:, j, :, 0, :].bitcast(F32), ALU.subtract).then_inc(S.xlo_done, 1)

            def product(e):
                dve.wait_ge(S.silu_done, e + 1)
                dve.tensor_tensor(prd[:, :], sl[:, :], gb[:, FT * SLOTS:2 * FT * SLOTS], ALU.mult).then_inc(S.act_done, 1)
                dve.wait_ge(S.ahi_done, e + 1)
                dve.tensor_tensor(ac[:, :, 1, :], prd[:, :].rearrange("p (f s) -> p f s", f=FT),
                                  ac[:, :, 0, :].bitcast(F32), ALU.subtract).then_inc(S.alo_done, 1)

            def sum_y(e, j):
                wait(dve, S.stored, e - 1)
                for half in range(2):
                    cols = slice(half * 512, half * 512 + 512)
                    dve.wait_ge(S.ylow_ready, e * 2 + (half + 1))
                    dve.scalar_tensor_tensor(ys[:, j, cols], yb[half][0:SLOTS, :], gate[0:SLOTS, j, 0:1], ylow[:, cols],
                                             ALU.mult, ALU.add).then_inc(S.y_ready, 1)

            def step(e, j, it):
                head = isinstance(e, int) and e == 0
                low(e, j, 0)
                low(e, j, 1)
                low(e, j, 2)
                if not head:
                    product(e - 1)
                if head:
                    x_low(0, 0)
                low(e, j, 3)
                low(e, j, 4)
                if not head:
                    sum_y(e - 1, 1 - j)
                low(e, j, 5)
                x_low(e + 1, 1 - j)
            blocks(dve, count, step)
            low(count, 0, 0)
            low(count, 0, 1)
            product(count - 1)
            sum_y(count - 1, 1)

        zeroed = sem("moe_zeroed")
        first_blocks, more_blocks = Signals("moe"), Signals("over")
        with nc.Block() as block:
            S = first_blocks

            @block.sync
            def _(sp):
                sync_program(sp, S, NE, lambda eng, e: e, True)

            @block.gpsimd
            def _(pool):
                v["zero_last"](pool)
                for i in range(2):
                    pool.memset(xg[:, i, :], 0.0).then_inc(zeroed, 1)
                pool.wait_ge(zeroed, 2)
                pool_program(pool, S, NE, 0)

            @block.tensor
            def _(pe):
                tensor_program(pe, S, NE)

            @block.scalar
            def _(act):
                scalar_program(act, S, NE)

            @block.vector
            def _(dve):
                vector_program(dve, S, NE)

        def any_more(eng):
            return eng.value_load(flag[0:1, 0:1], min_val=0, max_val=OVER) > 0

        with nc.Block() as block:
            S2 = more_blocks

            @block.sync
            def _(sp):
                with sp.If(any_more(sp)):
                    sync_program(sp, S2, OVER, lambda eng, e: eng.value_load(flag[0:1, bass.ds(e + 1, 1)], min_val=0, max_val=NE - 1), False)

            @block.gpsimd
            def _(pool):
                with pool.If(any_more(pool)):
                    pool_program(pool, S2, OVER, NE)

            @block.tensor
            def _(pe):
                with pe.If(any_more(pe)):
                    tensor_program(pe, S2, OVER)

            @block.scalar
            def _(act):
                with act.If(any_more(act)):
                    scalar_program(act, S2, OVER)

            @block.vector
            def _(dve):
                with dve.If(any_more(dve)):
                    vector_program(dve, S2, OVER)


def final(nc, sem, sb, pb, cn, v):
    h2, epsc = v["h2"], v["epsc"]
    st = ExitStack()
    with st:
        yr = sb(st, "yr", [P, NT, 2, DM])
        lng, lnb = sb(st, "lng3", [P, DM]), sb(st, "lnb3", [P, DM])
        stats, mv, rstd, nmr = sb(st, "stats3", [P, NT, 2, 6]), sb(st, "mv3", [P, NT, 2]), sb(st, "rstd3", [P, NT]), sb(st, "nmr3", [P, NT])
        y_in = [sem(f"y_in{t}") for t in range(NT)]
        ln_in, summed, out_done = sem("ln3_in"), sem("fin_summed"), sem("out_done")
        stats_ready, std_ready, scale_ready, norm_ready, gmul_ready, o_ready = (
            sem(f"ln3_{n}") for n in ("stats", "std", "scale", "norm", "gmul", "o"))
        dve_chain = sem("fin_dve_chain")
        with nc.Block() as block:
            @block.sync
            def _(sp):
                for t in range(NT):
                    sp.dma_start(yr[:, t, :, :], v["y_dram"].rearrange("(q s) d -> s q d", q=2)[t * P:(t + 1) * P, :, :]).then_inc(y_in[t], 16)
                    if t == 0:
                        sp.dma_start(lng[:, :], v["ln_ffn_g"].to_broadcast([P, DM])).then_inc(ln_in, 16)
                        sp.dma_start(lnb[:, :], v["ln_ffn_b"].to_broadcast([P, DM])).then_inc(ln_in, 16)
                for t in range(NT):
                    sp.wait_ge(o_ready, t + 1)
                    sp.dma_start(v["out"][t * P:(t + 1) * P, :], h2[:, t, :]).then_inc(out_done, 16)
                sp.wait_ge(out_done, 16 * NT)

            @block.scalar
            def _(act):
                layer_norm_act(act, h2, mv, rstd, nmr, epsc[:, 0:1], stats_ready, std_ready, scale_ready, norm_ready)

            @block.vector
            def _(dve):
                chain = Chain(dve, dve_chain)

                def x_ready(t):
                    dve.wait_ge(y_in[t], 16)
                    r = h2[:, t, :]
                    chain.link(dve.scalar_tensor_tensor(r, r, ALPHA, yr[:, t, 0, :], ALU.mult, ALU.add))
                    chain.link(dve.tensor_tensor(r, r, yr[:, t, 1, :], ALU.add))
                layer_norm_dve(dve, chain, h2, stats, mv, rstd, nmr, x_ready, stats_ready, std_ready, scale_ready,
                               norm_ready, gmul_ready, lng[:, :], ln_in, 1)

            @block.gpsimd
            def _(pool):
                v["zero_last"](pool)
                for t in range(NT):
                    pool.wait_ge(gmul_ready, t + 1)
                    pool.tensor_tensor(h2[:, t, :], h2[:, t, :], lnb[:, :], ALU.add).then_inc(o_ready, 1)


def kernel(**inputs):
    import numpy as _np
    import concourse.bacc as _bacc
    from concourse import mybir as _mybir
    from concourse.bass_utils import run_bass_kernel_spmd as _run

    a = {k: _np.asarray(v) for k, v in inputs.items()}
    rows = lambda t: _np.broadcast_to(_np.reshape(t, (1, -1)), (P, t.size))
    by_part = lambda t: _np.reshape(t, (P, -1))
    column = lambda t: _np.reshape(t, (-1, P)).T
    w_in = a["w_in"][0]
    gate_cols = _np.concatenate([w_in[:, C_A:C_A + 16], w_in[:, C_I:C_I + 16]], axis=1)
    small = _np.concatenate([
        _np.reshape(_np.transpose(_np.reshape(a["dn_conv_w"][0], (TAPS, 12, P)), (2, 1, 0)), (P, 60)),
        column(a["dn_norm_w"][0]), column(a["pool_scale"][0]), column(a["ml_norm_w"][0]),
        by_part(gate_cols), rows(a["dn_a_log"][0]), rows(a["dn_dt_bias"][0]), rows(a["ml_gate_b"][0]),
        rows(a["router_b"]), by_part(a["router_w"])], axis=1)
    arrays = {
        "x": a["x"][0], "ln_in_g": a["ln_in_g"][None], "ln_in_b": a["ln_in_b"][None], "w_in": w_in,
        "pool_w": a["pool_w"][0], "w_branch": a["w_branch"][0], "w_out": a["w_out"][0],
        "ln_mix_g": a["ln_mix_g"], "ln_mix_b": a["ln_mix_b"], "moe_w1": a["moe_w1"][0], "moe_w3": a["moe_w3"][0],
        "moe_w2": a["moe_w2"][0], "ln_ffn_g": a["ln_ffn_g"], "ln_ffn_b": a["ln_ffn_b"],
        "const": _np.concatenate(list(CONST.values()), axis=1), "small": small,
    }
    nc = _bacc.Bacc("TRN2", target_bir_lowering=False, num_devices=1)
    feed, args = {}, []
    for name, t in arrays.items():
        if name.startswith("ln_") and t.ndim == 1:
            t = t[None]
        t = _np.ascontiguousarray(t)
        feed[f"in_{name}"] = t
        args.append(nc.dram_tensor(f"in_{name}", t.shape, _mybir.dt.from_np(t.dtype), kind="ExternalInput").ap())
    args.append(nc.dram_tensor("result", (SEQ, DM), _mybir.dt.float32, kind="ExternalOutput").ap())
    hybrid_encoder(nc, *args)
    r = _run(nc, [feed], core_ids=[0])
    return _np.reshape(r.results[0]["result"], (1, SEQ, DM))
```
